# Optimizing a Trainium2 kernel written in Bass

```python
import math
import jax
import jax.numpy as jnp
from jax import lax
import numpy as np

D_MODEL = 1024
BATCH = 1
SEQ = 256
DEPTH = 2

GRID_W = 64
CTX_LEN = 256

HY_CH = 256
RW_HEADS = 4
RW_HD = 64
RW_W = RW_HEADS * RW_HD
AT_HQ = 8
AT_HKV = 2
AT_G = AT_HQ // AT_HKV
AT_HD = 64
AT_W = AT_HQ * AT_HD
AT_KVW = AT_HKV * AT_HD
MIX_W = HY_CH + RW_W + AT_W

RW_DECAY_R = 64
RW_ICLR_R = 64
RW_GATE_R = 128
RW_LORA_W = 2 * RW_DECAY_R + 2 * RW_ICLR_R + RW_GATE_R
RW_GN_EPS = RW_HD * 1e-5

HY_EMB = 33
HY_BANDS = (HY_EMB - 1) // 2
HY_HID = 64
HY_SHIFT = 0.05
HY_MIN_DECAY = math.log(1e-2) / 1.5
HY_MAX_DECAY = math.log(1e-2) / 0.3

ATT_WINDOW = 128
ATT_BLOCK = 128
ROPE_BASE = 10000.0
NEG_INF = -1e30

PEER_HEADS = 8
PEER_NKEYS = 128
PEER_NEXP = PEER_NKEYS * PEER_NKEYS
PEER_DQ = 256
PEER_TOPK = 16
PEER_CHUNK = 128

OFF_HY = 0
OFF_RK = OFF_HY + 3 * HY_CH
OFF_LORA = OFF_RK + 3 * RW_W
OFF_AT = OFF_LORA + RW_LORA_W
IN_W = OFF_AT + AT_W + 2 * AT_KVW
CONV_COLS = OFF_LORA

kernel_name = 'hybrid_hyena_rwkv7_swa_peer_dit'

def rmsnorm(x, g, eps=1e-6):
    xf = x.astype(jnp.float32)
    y = xf * lax.rsqrt(jnp.mean(xf * xf, axis=-1, keepdims=True) + eps)
    return (y * g.astype(jnp.float32)).astype(x.dtype)

def short_conv3(u, w, b):
    up = jnp.pad(u, ((0, 0), (1, 1), (0, 0)))
    return up[:, :-2] * w[0] + up[:, 1:-1] * w[1] + up[:, 2:] * w[2] + b

def hyena_filter(L, w1, b1, w2, b2, w3, b3, freq):
    f32 = jnp.float32
    j = jnp.arange(L, dtype=f32)
    t = j / max(L - 1, 1)
    bands = jnp.linspace(1e-4, HY_BANDS - 1, HY_BANDS, dtype=f32)
    ang = 2.0 * math.pi * j[:, None] * bands[None, :] / L
    z = jnp.concatenate([t[:, None], jnp.cos(ang), -jnp.sin(ang)], axis=-1)
    h = jnp.sin(freq[0] * (z @ w1 + b1))
    h = jnp.sin(freq[1] * (h @ w2 + b2))
    h = (h @ w3 + b3).astype(f32).reshape(L, 2, HY_CH)
    deltas = jnp.abs(jnp.linspace(HY_MIN_DECAY, HY_MAX_DECAY, HY_CH, dtype=f32))
    window = jnp.exp(-t[:, None] * deltas[None, :]) + HY_SHIFT
    h = h * window[:, None, :]
    k = jnp.concatenate([h[:, 0], jnp.zeros((1, HY_CH), f32), h[:0:-1, 1]], axis=0)
    return k * lax.rsqrt(jnp.sum(k * k, axis=0, keepdims=True) + 1e-6)

def hyena_mix(z, filt, d_bias):
    f32 = jnp.float32
    L = z.shape[1]
    x0 = z[..., :HY_CH].astype(f32)
    x1 = z[..., HY_CH:2 * HY_CH].astype(f32)
    v = z[..., 2 * HY_CH:].astype(f32)
    u = x1 * v
    n = 2 * L
    y = jnp.fft.irfft(jnp.fft.rfft(u, n=n, axis=1) * jnp.fft.rfft(filt, n=n, axis=0)[None], n=n, axis=1)[:, :L]
    return (x0 * (y + u * d_bias)).astype(z.dtype)

def rwkv7_scan(r, w, k, v, a, b):
    B, L, H, N = r.shape

    def step(S, inp):
        r_t, w_t, k_t, v_t, a_t, b_t = inp
        sa = jnp.einsum('bhvk,bhk->bhv', S, a_t)
        S = S * w_t[:, :, None, :] + sa[..., None] * b_t[:, :, None, :] + v_t[..., None] * k_t[:, :, None, :]
        return S, jnp.einsum('bhvk,bhk->bhv', S, r_t)

    S0 = jnp.zeros((B, H, N, N), jnp.float32)
    xs = tuple(jnp.swapaxes(s, 0, 1) for s in (r, w, k, v, a, b))
    _, ys = lax.scan(step, S0, xs)
    return jnp.swapaxes(ys, 0, 1)

def rwkv7_mix(rkv_c, rkv_l, lora_c, lora_l, lp):
    f32 = jnp.float32
    B, Lc, _ = rkv_c.shape
    T = rkv_l.shape[1]
    Lt = Lc + T
    hs = (B, Lt, RW_HEADS, RW_HD)
    rkv = jnp.concatenate([rkv_c, rkv_l], axis=1).astype(f32)
    lora = jnp.concatenate([lora_c, lora_l], axis=1).astype(f32)
    r = rkv[..., :RW_W].reshape(hs)
    k = rkv[..., RW_W:2 * RW_W].reshape(hs)
    v = rkv[..., 2 * RW_W:].reshape(hs)
    kk = k * lp['rw_k_k'].astype(f32).reshape(RW_HEADS, RW_HD)
    kk = kk * lax.rsqrt(jnp.sum(kk * kk, axis=-1, keepdims=True) + 1e-12)
    k_a = lp['rw_k_a'].astype(f32).reshape(RW_HEADS, RW_HD)
    r_k = lp['rw_r_k'].astype(f32)
    perm = jnp.concatenate([jnp.arange(Lc - 1, -1, -1), Lc + jnp.arange(T - 1, -1, -1)])
    y_sum = jnp.zeros(hs, f32)
    bonus = jnp.zeros(hs, f32)
    for d in range(2):
        wd = lora[..., d * RW_DECAY_R:(d + 1) * RW_DECAY_R]
        ad = lora[..., 2 * RW_DECAY_R + d * RW_ICLR_R:2 * RW_DECAY_R + (d + 1) * RW_ICLR_R]
        w_log = -jax.nn.softplus(-(lp['rw_w0'][d] + jnp.tanh(wd) @ lp['rw_w_up'][d])) - 0.5
        decay = jnp.exp(-jnp.exp(w_log.astype(f32))).reshape(hs)
        a = jax.nn.sigmoid((lp['rw_a0'][d] + ad @ lp['rw_a_up'][d]).astype(f32)).reshape(hs)
        k_d = k * (1.0 + (a - 1.0) * k_a)
        seqs = (r, decay, k_d, v, -kk, kk * a)
        if d == 1:
            seqs = tuple(s[:, perm] for s in seqs)
        y = rwkv7_scan(*seqs)
        if d == 1:
            y = y[:, perm]
        y_sum = y_sum + y
        bonus = bonus + jnp.sum(r * k_d * r_k, axis=-1, keepdims=True) * v
    mu = jnp.mean(y_sum, axis=-1, keepdims=True)
    var = jnp.mean(jnp.square(y_sum - mu), axis=-1, keepdims=True)
    yn = (y_sum - mu) * lax.rsqrt(var + RW_GN_EPS)
    yn = yn * lp['rw_ln_w'].astype(f32).reshape(RW_HEADS, RW_HD) + lp['rw_ln_b'].astype(f32).reshape(RW_HEADS, RW_HD)
    g = jax.nn.sigmoid(lora[..., 2 * RW_DECAY_R + 2 * RW_ICLR_R:]) @ lp['rw_g_up']
    out = ((yn + bonus).reshape(B, Lt, RW_W) * g).astype(rkv_l.dtype)
    return out[:, :Lc], out[:, Lc:]

def axial_rope(x):
    f32 = jnp.float32
    T = x.shape[1]
    rows = T // GRID_W
    row = jnp.repeat(jnp.arange(rows), GRID_W).astype(f32)
    col = jnp.tile(jnp.arange(GRID_W), rows).astype(f32)
    half = AT_HD // 2
    quarter = half // 2
    inv = ROPE_BASE ** (-jnp.arange(quarter, dtype=f32) / quarter)

    def rot(xa, pos):
        ang = pos[:, None] * inv[None, :]
        cos = jnp.cos(ang)[None, :, None, :]
        sin = jnp.sin(ang)[None, :, None, :]
        x1, x2 = xa[..., :quarter], xa[..., quarter:]
        return jnp.concatenate([x1 * cos - x2 * sin, x2 * cos + x1 * sin], axis=-1)

    xf = x.astype(f32)
    return jnp.concatenate([rot(xf[..., :half], row), rot(xf[..., half:], col)], axis=-1).astype(x.dtype)

def split_attn(z):
    B, L, _ = z.shape
    a = z[..., OFF_AT:]
    q = a[..., :AT_W].reshape(B, L, AT_HQ, AT_HD)
    k = a[..., AT_W:AT_W + AT_KVW].reshape(B, L, AT_HKV, AT_HD)
    v = a[..., AT_W + AT_KVW:].reshape(B, L, AT_HKV, AT_HD)
    return q, k, v

def windowed_gqa(q, k, v, kc, vc, sink):
    B, T = q.shape[:2]
    Lc = kc.shape[1]
    nblk = T // ATT_BLOCK
    span = ATT_BLOCK + 2 * ATT_WINDOW
    scale = AT_HD ** -0.5
    kp = jnp.pad(k, ((0, 0), (ATT_WINDOW, ATT_WINDOW), (0, 0), (0, 0)))
    vp = jnp.pad(v, ((0, 0), (ATT_WINDOW, ATT_WINDOW), (0, 0), (0, 0)))
    sink_b = jnp.broadcast_to(sink.astype(jnp.float32)[None, :, :, None, None], (B, AT_HKV, AT_G, ATT_BLOCK, 1))

    def block(i):
        s0 = i * ATT_BLOCK
        qb = lax.dynamic_slice_in_dim(q, s0, ATT_BLOCK, axis=1)
        kb = lax.dynamic_slice_in_dim(kp, s0, span, axis=1)
        vb = lax.dynamic_slice_in_dim(vp, s0, span, axis=1)
        qpos = s0 + jnp.arange(ATT_BLOCK)
        kpos = s0 - ATT_WINDOW + jnp.arange(span)
        valid = (jnp.abs(qpos[:, None] - kpos[None, :]) <= ATT_WINDOW) & (kpos >= 0)[None, :] & (kpos < T)[None, :]
        s_lat = jnp.einsum('bqgjd,bkgd->bgjqk', qb, kb).astype(jnp.float32) * scale
        s_lat = jnp.where(valid, s_lat, NEG_INF)
        s_ctx = jnp.einsum('bqgjd,bkgd->bgjqk', qb, kc).astype(jnp.float32) * scale
        p = jax.nn.softmax(jnp.concatenate([s_lat, s_ctx, sink_b], axis=-1), axis=-1).astype(v.dtype)
        return (jnp.einsum('bgjqk,bkgd->bqgjd', p[..., :span], vb)
                + jnp.einsum('bgjqk,bkgd->bqgjd', p[..., span:span + Lc], vc))

    o = lax.map(block, jnp.arange(nblk))
    return jnp.swapaxes(o, 0, 1).reshape(B, T, AT_W)

def context_attention(qc, kc, vc, sink):
    B, Lc = qc.shape[:2]
    scale = AT_HD ** -0.5
    s = jnp.einsum('bqgjd,bkgd->bgjqk', qc, kc).astype(jnp.float32) * scale
    sink_b = jnp.broadcast_to(sink.astype(jnp.float32)[None, :, :, None, None], (B, AT_HKV, AT_G, Lc, 1))
    p = jax.nn.softmax(jnp.concatenate([s, sink_b], axis=-1), axis=-1)[..., :Lc].astype(vc.dtype)
    return jnp.einsum('bgjqk,bkgd->bqgjd', p, vc).reshape(B, Lc, AT_W)

def token_mixer(hl, hc, lp, need_ctx):
    B, T, _ = hl.shape
    Lc = hc.shape[1]
    zl = hl @ lp['w_in']
    zc = hc @ lp['w_in']
    sl = short_conv3(zl[..., :CONV_COLS], lp['conv_w'], lp['conv_b'])
    sc = short_conv3(zc[..., :CONV_COLS], lp['conv_w'], lp['conv_b'])
    filt_p = (lp['hy_w1'], lp['hy_b1'], lp['hy_w2'], lp['hy_b2'], lp['hy_w3'], lp['hy_b3'], lp['hy_freq'])
    hy_l = hyena_mix(sl[..., OFF_HY:OFF_RK], hyena_filter(T, *filt_p), lp['hy_bias'])
    rw_c, rw_l = rwkv7_mix(sc[..., OFF_RK:], sl[..., OFF_RK:], zc[..., OFF_LORA:OFF_AT], zl[..., OFF_LORA:OFF_AT], lp)
    ql, kl, vl = split_attn(zl)
    qc, kc, vc = split_attn(zc)
    sink = lp['attn_sink'].reshape(AT_HKV, AT_G)
    ql = axial_rope(ql).reshape(B, T, AT_HKV, AT_G, AT_HD)
    kl = axial_rope(kl)
    at_l = windowed_gqa(ql, kl, vl, kc, vc, sink)
    out_l = jnp.concatenate([rmsnorm(hy_l, lp['hy_out_g']), rw_l, rmsnorm(at_l, lp['at_out_g'])], axis=-1) @ lp['w_out']
    if not need_ctx:
        return out_l, None
    hy_c = hyena_mix(sc[..., OFF_HY:OFF_RK], hyena_filter(Lc, *filt_p), lp['hy_bias'])
    at_c = context_attention(qc.reshape(B, Lc, AT_HKV, AT_G, AT_HD), kc, vc, sink)
    out_c = jnp.concatenate([rmsnorm(hy_c, lp['hy_out_g']), rw_c, rmsnorm(at_c, lp['at_out_g'])], axis=-1) @ lp['w_out']
    return out_l, out_c

def peer_ffn(h, wq, k1, k2, u, v):
    n, d = h.shape
    hb = h.reshape(n // PEER_CHUNK, PEER_CHUNK, d)

    def chunk(xc):
        q = (xc @ wq).reshape(PEER_CHUNK, PEER_HEADS, 2, PEER_DQ // 2)
        s1 = jnp.einsum('chd,hnd->chn', q[:, :, 0], k1).astype(jnp.float32)
        s2 = jnp.einsum('chd,hnd->chn', q[:, :, 1], k2).astype(jnp.float32)
        v1, i1 = lax.top_k(s1, PEER_TOPK)
        v2, i2 = lax.top_k(s2, PEER_TOPK)
        cand = (v1[..., :, None] + v2[..., None, :]).reshape(PEER_CHUNK, PEER_HEADS, PEER_TOPK * PEER_TOPK)
        cidx = (i1[..., :, None] * PEER_NKEYS + i2[..., None, :]).reshape(PEER_CHUNK, PEER_HEADS, PEER_TOPK * PEER_TOPK)
        sc, pos = lax.top_k(cand, PEER_TOPK)
        eidx = jnp.take_along_axis(cidx, pos, axis=-1)
        gate = jax.nn.softmax(sc, axis=-1)
        act = jax.nn.gelu(jnp.einsum('cd,chkd->chk', xc, u[eidx]).astype(jnp.float32), approximate=False)
        return jnp.einsum('chk,chkd->cd', (gate * act).astype(xc.dtype), v[eidx])

    return lax.map(chunk, hb).reshape(n, d)

def setup_inputs(seed: int = 0) -> dict:
    key = jax.random.key(seed)
    ks = iter(jax.random.split(key, 48))
    f32 = jnp.float32

    def nrm(shape, scale):
        return jax.random.normal(next(ks), shape, f32) * scale

    def gain(shape):
        return 1.0 + nrm(shape, 0.05)

    D = D_MODEL
    return {
        'x': nrm((BATCH, SEQ, D), 1.0),
        'c': nrm((BATCH, D), 1.0),
        'ctx': nrm((BATCH, CTX_LEN, D), 1.0),
        'c_ctx': nrm((D,), 1.0),
        'mod_w': nrm((DEPTH, D, 6 * D), 0.01),
        'mod_b': nrm((DEPTH, 6 * D), 0.01),
        'norm1_g': gain((DEPTH, D)),
        'norm2_g': gain((DEPTH, D)),
        'w_in': nrm((DEPTH, D, IN_W), D ** -0.5),
        'conv_w': nrm((DEPTH, 3, CONV_COLS), 0.6),
        'conv_b': nrm((DEPTH, CONV_COLS), 0.01),
        'hy_w1': nrm((DEPTH, HY_EMB, HY_HID), HY_EMB ** -0.5),
        'hy_b1': nrm((DEPTH, HY_HID), 0.1),
        'hy_w2': nrm((DEPTH, HY_HID, HY_HID), HY_HID ** -0.5),
        'hy_b2': nrm((DEPTH, HY_HID), 0.1),
        'hy_w3': nrm((DEPTH, HY_HID, 2 * HY_CH), HY_HID ** -0.5),
        'hy_b3': nrm((DEPTH, 2 * HY_CH), 0.01),
        'hy_freq': 1.0 + nrm((DEPTH, 2, HY_HID), 0.1),
        'hy_bias': nrm((DEPTH, HY_CH), 0.5),
        'rw_w0': jax.random.uniform(next(ks), (DEPTH, 2, RW_W), f32, -6.0, 0.5),
        'rw_w_up': nrm((DEPTH, 2, RW_DECAY_R, RW_W), 0.1 * RW_DECAY_R ** -0.5),
        'rw_a0': nrm((DEPTH, 2, RW_W), 0.1),
        'rw_a_up': nrm((DEPTH, 2, RW_ICLR_R, RW_W), RW_ICLR_R ** -0.5),
        'rw_g_up': nrm((DEPTH, RW_GATE_R, RW_W), RW_GATE_R ** -0.5),
        'rw_k_k': 0.85 + nrm((DEPTH, RW_W), 0.05),
        'rw_k_a': gain((DEPTH, RW_W)),
        'rw_r_k': nrm((DEPTH, RW_HEADS, RW_HD), 0.1),
        'rw_ln_w': gain((DEPTH, RW_W)),
        'rw_ln_b': nrm((DEPTH, RW_W), 0.01),
        'attn_sink': nrm((DEPTH, AT_HQ), 0.5),
        'hy_out_g': gain((DEPTH, HY_CH)),
        'at_out_g': gain((DEPTH, AT_W)),
        'w_out': nrm((DEPTH, MIX_W, D), MIX_W ** -0.5),
        'peer_wq': nrm((DEPTH, D, PEER_HEADS * PEER_DQ), D ** -0.5),
        'peer_k1': nrm((DEPTH, PEER_HEADS, PEER_NKEYS, PEER_DQ // 2), (PEER_DQ // 2) ** -0.5),
        'peer_k2': nrm((DEPTH, PEER_HEADS, PEER_NKEYS, PEER_DQ // 2), (PEER_DQ // 2) ** -0.5),
        'peer_u': nrm((DEPTH, PEER_NEXP, D), D ** -0.5),
        'peer_v': nrm((DEPTH, PEER_NEXP, D), 1.0),
        'final_g': gain((D,)),
    }

def reference(x, c, ctx, c_ctx, mod_w, mod_b, norm1_g, norm2_g, w_in, conv_w, conv_b,
              hy_w1, hy_b1, hy_w2, hy_b2, hy_w3, hy_b3, hy_freq, hy_bias,
              rw_w0, rw_w_up, rw_a0, rw_a_up, rw_g_up, rw_k_k, rw_k_a, rw_r_k, rw_ln_w, rw_ln_b,
              attn_sink, hy_out_g, at_out_g, w_out,
              peer_wq, peer_k1, peer_k2, peer_u, peer_v, final_g):
    B, T, D = x.shape
    Lc = ctx.shape[1]
    c_s = jax.nn.silu(c)
    cc_s = jax.nn.silu(c_ctx)
    xl, xc = x, ctx
    for i in range(DEPTH):
        last = i == DEPTH - 1
        lp = dict(w_in=w_in[i], conv_w=conv_w[i], conv_b=conv_b[i],
                  hy_w1=hy_w1[i], hy_b1=hy_b1[i], hy_w2=hy_w2[i], hy_b2=hy_b2[i],
                  hy_w3=hy_w3[i], hy_b3=hy_b3[i], hy_freq=hy_freq[i], hy_bias=hy_bias[i],
                  rw_w0=rw_w0[i], rw_w_up=rw_w_up[i], rw_a0=rw_a0[i], rw_a_up=rw_a_up[i],
                  rw_g_up=rw_g_up[i], rw_k_k=rw_k_k[i], rw_k_a=rw_k_a[i], rw_r_k=rw_r_k[i],
                  rw_ln_w=rw_ln_w[i], rw_ln_b=rw_ln_b[i], attn_sink=attn_sink[i],
                  hy_out_g=hy_out_g[i], at_out_g=at_out_g[i], w_out=w_out[i])
        sh1, sc1, g1, sh2, sc2, g2 = jnp.split((c_s @ mod_w[i] + mod_b[i])[:, None, :], 6, axis=-1)
        csh1, csc1, cg1, csh2, csc2, cg2 = jnp.split(cc_s @ mod_w[i] + mod_b[i], 6, axis=-1)
        hl = rmsnorm(xl, norm1_g[i]) * (1.0 + sc1) + sh1
        hc = rmsnorm(xc, norm1_g[i]) * (1.0 + csc1) + csh1
        ml, mc = token_mixer(hl, hc, lp, not last)
        xl = xl + g1 * ml
        h2l = rmsnorm(xl, norm2_g[i]) * (1.0 + sc2) + sh2
        if last:
            fl = peer_ffn(h2l.reshape(B * T, D), peer_wq[i], peer_k1[i], peer_k2[i], peer_u[i], peer_v[i]).reshape(B, T, D)
        else:
            xc = xc + cg1 * mc
            h2c = rmsnorm(xc, norm2_g[i]) * (1.0 + csc2) + csh2
            tok = jnp.concatenate([h2l.reshape(B * T, D), h2c.reshape(B * Lc, D)], axis=0)
            f = peer_ffn(tok, peer_wq[i], peer_k1[i], peer_k2[i], peer_u[i], peer_v[i])
            fl = f[:B * T].reshape(B, T, D)
            xc = xc + cg2 * f[B * T:].reshape(B, Lc, D)
        xl = xl + g2 * fl
    return rmsnorm(xl, final_g)


_drawn_inputs = setup_inputs


def setup_inputs(seed=0):
    import zlib

    import numpy as np

    out = dict(_drawn_inputs(seed))
    spreads = {}
    factors = {'conv_b': 5.755,
     'hy_b3': 6.169,
     'rw_w_up': 8.0,
     'rw_a0': 5.332,
     'rw_k_k': 5.362,
     'rw_k_a': 4.393,
     'rw_ln_w': 6.032,
     'rw_ln_b': 41.05,
     'attn_sink': 8.0,
     'hy_out_g': 3.684,
     'at_out_g': 3.172}
    for name, (base, spread) in spreads.items():
        noise = np.random.default_rng([zlib.crc32(name.encode()), seed]).standard_normal(out[name].shape)
        drawn = base * np.exp(spread * noise) if base else spread * noise
        out[name] = jnp.asarray(drawn.astype(out[name].dtype))
    for name, factor in factors.items():
        out[name] = (out[name] * factor).astype(out[name].dtype)
    return out
```

```python
from contextlib import ExitStack

import numpy as np

import concourse.bass as bass
from concourse import mybir

F32 = mybir.dt.float32
U32 = mybir.dt.uint32
I32 = mybir.dt.int32
ALU = mybir.AluOpType
ACT = mybir.ActivationFunctionType
AX = mybir.AxisListType

P = 128
D = 1024
DEPTH = 2
SEQ = 256
TOK = 2 * SEQ
TILES = TOK // P
KD = D // P
BANK = 512

HY_CH, HY_EMB, HY_HID = 256, 33, 64
RW_W, RW_HD = 256, 64
AT_HQ, AT_HD, AT_W = 8, 64, 512
IN_W = 2688
IN_TILES = IN_W // P
CONV_TILES = 12
LORA0, Q0, K0, V0 = 12, 15, 19, 20
CHUNK = 64
NCHUNK = TOK // CHUNK
DECAY = float(np.exp(-0.5))
HEADS, NKEYS, TOPK, DQ = 8, 128, 16, 256
NEXP = NKEYS * NKEYS
SLOTS = HEADS * TOPK
RING = 8
GROUPS = SLOTS // RING
BIG = 1e30
TWO_PI = 2.0 * float(np.pi)
PI_BELOW = 3.1415925

ROWS = {}
_n = 0
for _name, _count in (("conv_w", 36), ("conv_b", 12), ("rw_w0", 4), ("rw_a0", 4), ("rw_k_k", 2), ("rw_k_a", 2),
                      ("rw_r_k", 2), ("rw_ln_w", 2), ("rw_ln_b", 2), ("hy_bias", 2), ("hy_out_g", 2),
                      ("at_out_g", 4), ("hy_b1", 1), ("hy_b2", 1), ("hy_freq", 2)):
    ROWS[_name] = _n
    _n += _count
NROWS = _n


def host_constants():
    f = np.float64
    j = np.arange(SEQ, dtype=f)
    t32 = np.arange(SEQ, dtype=np.float32) / np.float32(SEQ - 1)
    bands = np.linspace(1e-4, (HY_EMB - 1) // 2 - 1, (HY_EMB - 1) // 2, dtype=np.float32)
    ang = (np.float32(TWO_PI) * np.arange(SEQ, dtype=np.float32)[:, None] * bands[None, :] / np.float32(SEQ)).astype(f)
    emb = np.concatenate([t32[:, None].astype(f), np.cos(ang), -np.sin(ang)], axis=1).T
    deltas = np.abs(np.linspace(np.log(1e-2) / 1.5, np.log(1e-2) / 0.3, HY_CH, dtype=np.float32)).astype(f)
    window = np.exp(-t32.astype(f)[:, None] * deltas[None, :]) + 0.05
    w = (np.arange(SEQ, dtype=f) + 0.5) * TWO_PI / (2 * SEQ)
    cos, sin = np.cos(j[:, None] * w[None, :]), np.sin(j[:, None] * w[None, :])
    two_sided = np.stack([window, np.where(j[:, None] == 0, 0.0, window)], axis=1)
    tiles = lambda m: m.reshape(2, P, SEQ).transpose(1, 0, 2)
    dft = np.stack([tiles(cos), tiles(sin), tiles(cos.T / SEQ), tiles(sin.T / SEQ)], axis=1)
    t, s = np.meshgrid(np.arange(P), np.arange(P), indexing="ij")
    same = lambda n: (t // n) == (s // n)
    low = (s < t) & same(64)
    masks = [low & same(16), low & same(32) & ~same(16), low & ~same(32), low, (s <= t) & same(64)]
    masks = np.stack([m for m in masks] + [m.T for m in masks], axis=1).astype(f)
    head_pair = (t // 64 == s // 64).astype(f)
    d = np.arange(P) % 64
    inv = (10000.0 ** (-np.arange(16, dtype=np.float32) / np.float32(16))).astype(f)[d % 16]
    pos = np.where((d < 32)[:, None], (np.arange(SEQ) // 64)[None, :], (np.arange(SEQ) % 64)[None, :])
    rope = np.stack([np.cos(pos * inv[:, None]), np.sin(pos * inv[:, None])], axis=1)
    rot = np.zeros((P, P), f)
    for m in range(P):
        rot[m + 16 if m % 32 < 16 else m - 16, m] = -1.0 if m % 32 < 16 else 1.0
    swap = np.zeros((P, P), f)
    swap[(np.arange(P) + 64) % P, np.arange(P)] = 1.0
    q, k = np.arange(SEQ).reshape(2, P), np.arange(SEQ)
    band = np.where(np.abs(q[:, :, None] - k[None, None, :]) <= 128, 0.0, -BIG).transpose(1, 0, 2)
    band = np.concatenate([np.zeros_like(band), band], axis=2)
    iota16 = np.tile(np.arange(16, dtype=f), (P, 1))
    out = dict(k_emb=emb, k_window=two_sided.reshape(2, P, 2 * HY_CH).transpose(1, 0, 2), k_dft=dft, k_masks=masks,
               k_pair=head_pair, k_rope=rope, k_rot=rot, k_swap=swap, k_band=band, k_iota=iota16,
               k_ident=np.eye(P))
    return {n: np.ascontiguousarray(a.astype(np.float32)) for n, a in out.items()}


class Semaphores:

    def __init__(self, nc, per_bank=70):
        self.nc, self.turn = nc, 0
        first = min(nc.free_semaphores)
        self.banks = [range(first, first + per_bank), range(first + per_bank, first + 2 * per_bank)]

    def begin(self, stack):
        mine, self.other = self.banks[self.turn], self.banks[1 - self.turn]
        self.turn = 1 - self.turn
        nums = iter(mine)

        def sem(name):
            s = self.nc.alloc_semaphore(name, num=next(nums))
            stack.callback(self.nc.release_semaphore, s)
            return s
        return sem


def chained(eng, done):
    count = [0]

    def step(instruction):
        count[0] += 1
        instruction.then_inc(done, 1)
        eng.wait_ge(done, count[0])
    return step


class Shared:

    def __init__(self):
        self.uses = {}

    def name(self, base):
        self.uses[base] = self.uses.get(base, 0) + 1
        return f"{base}_{self.uses[base]}"


def stage_constants(nc, g):
    with ExitStack() as st:
        sem = g.sems.begin(st)
        rows = st.enter_context(nc.sbuf_tensor(g.name("param_rows"), [P, DEPTH, P], F32))
        crow = st.enter_context(nc.sbuf_tensor(g.name("cond_rows"), [2 * KD, P], F32))
        ps = st.enter_context(nc.psum_tensor(g.name("param_cols_ps"), [P, 4, BANK], F32))
        loaded, zeroed, rows_in, tp_done = sem("loaded"), sem("zeroed"), sem("rows_in"), sem("tp_done")
        v_done, silu_done = sem("v_done"), sem("silu_done")
        consts = [(g.ident, "k_ident"), (g.masks, "k_masks"),
                  (g.pair, "k_pair"), (g.rope, "k_rope"), (g.rot, "k_rot"), (g.swap, "k_swap"), (g.band, "k_band"),
                  (g.iota, "k_iota")]
        wide = []
        for l in range(DEPTH):
            for name, r in ROWS.items():
                src = g.dram[name][l]
                if name in ("hy_b1", "hy_b2"):
                    wide.append((rows[r:r + 1, l, 0:64], src.rearrange("(a n) -> a n", a=1)))
                elif name == "hy_freq":
                    wide.append((rows[r:r + 2, l, 0:64], src))
                else:
                    if name == "conv_w":
                        flat = src.rearrange("k (a n) -> (k a) n", n=P)
                    elif name in ("rw_w0", "rw_a0"):
                        flat = src.rearrange("k (a n) -> (k a) n", n=P)
                    elif name == "rw_r_k":
                        flat = src.rearrange("(a h) n -> a (h n)", h=2)
                    else:
                        flat = src.rearrange("(a n) -> a n", n=P)
                    wide.append((rows[r:r + flat.shape[0], l, :], flat))
        wide.append((crow[0:KD, :], g.dram["c"].rearrange("b (a n) -> (b a) n", n=P)))
        wide.append((crow[KD:2 * KD, :], g.dram["c_ctx"].rearrange("(a n) -> a n", n=P)))

        with nc.Block() as block:
            @block.sync
            def _(sp):
                sp.dma_start(g.ident[:], g.dram["k_ident"]).then_inc(rows_in, 16)
                sp.wait_ge(zeroed, 1)
                for dst, src in wide[0::2]:
                    sp.dma_start(dst, src).then_inc(rows_in, 16)
                sp.dma_start(g.X[:, 0:2, :], g.dram["ctx"][0].rearrange("(i p) d -> p i d", p=P)).then_inc(loaded, 16)
                sp.dma_start(g.X[:, 2:4, :], g.dram["x"][0].rearrange("(i p) d -> p i d", p=P)).then_inc(loaded, 16)
                for dst, name in consts[1:]:
                    sp.dma_start(dst[:], g.dram[name]).then_inc(loaded, 16)
                for l in range(DEPTH):
                    sp.dma_start(g.sink[:, l, :], g.dram["attn_sink"][l:l + 1, :].partition_broadcast(P)
                                 if False else g.dram["attn_sink"][l:l + 1, :].to_broadcast([P, AT_HQ])).then_inc(loaded, 16)
                sp.wait_ge(loaded, 16 * (2 + len(consts) - 1 + DEPTH))

            @block.gpsimd
            def _(po):
                po.sem_clear(g.sems.other)
                po.memset(rows[:], 0.0).then_inc(zeroed, 1)
                po.memset(g.ones[:], 1.0)

            @block.scalar
            def _(ac):
                ac.wait_ge(zeroed, 1)
                for dst, src in wide[1::2]:
                    ac.dma_start(dst, src).then_inc(rows_in, 16)
                ac.wait_ge(tp_done, 1)
                ac.activation(g.cond[:], ps[:, DEPTH, 0:2 * KD].rearrange("p (w k) -> p k w", w=2), ACT.Sigmoid).then_inc(silu_done, 1)

            @block.tensor
            def _(pe):
                pe.wait_ge(rows_in, 16 * (len(wide) + 1))
                pe.transpose(ps[:, DEPTH, 0:2 * KD], crow[:, :], g.ident[0:2 * KD, 0:2 * KD]).then_inc(tp_done, 1)
                for l in range(DEPTH):
                    pe.transpose(ps[:, l, 0:P], rows[:, l, :], g.ident[:]).then_inc(tp_done, 1)

            @block.vector
            def _(ve):
                step = chained(ve, v_done)
                for l in range(DEPTH):
                    ve.wait_ge(tp_done, 2 + l)
                    step(ve.tensor_copy(g.par[:, l, :], ps[:, l, 0:P]))
                for l in range(DEPTH):
                    a = ROWS["rw_k_a"]
                    step(ve.tensor_scalar(g.omka[:, l, :], g.par[:, l, a:a + 2], -1.0, 1.0, ALU.mult, ALU.add))
                ve.wait_ge(loaded, 16 * (2 + len(consts) - 1 + DEPTH))
                step(ve.tensor_scalar(g.sink8[:], g.sink[:], float(AT_HD) ** 0.5, None, ALU.mult))
                ve.wait_ge(silu_done, 1)
                step(ve.tensor_tensor(g.cond[:], g.cond[:], ps[:, DEPTH, 0:2 * KD].rearrange("p (w k) -> p k w", w=2), ALU.mult))


def stage_modulation(nc, g, l):
    NT = 6 * D // BANK
    WB = 3
    with ExitStack() as st:
        sem = g.sems.begin(st)
        w = st.enter_context(nc.sbuf_tensor(g.name("mod_w_ring"), [P, WB, KD, BANK], F32))
        mod = st.enter_context(nc.sbuf_tensor(g.name("mod_pair"), [2, 6 * D], F32))
        bias = st.enter_context(nc.sbuf_tensor(g.name("mod_bias"), [2, 6 * D], F32))
        gain = st.enter_context(nc.sbuf_tensor(g.name("norm_gain"), [2, 2, D], F32))
        ps = st.enter_context(nc.psum_tensor(g.name("mod_ps"), [P, 4, BANK], F32))
        landed = [sem(f"mod_w_landed{b}") for b in range(WB)]
        small, mm_done, evac = sem("mod_small"), sem("mod_mm_done"), sem("mod_evacuated")
        wv = g.dram["mod_w"][l].rearrange("(k p) n -> p k n", p=P)

        with nc.Block() as block:
            @block.sync
            def _(sp):
                sp.dma_start(bias[:], g.dram["mod_b"][l:l + 1, :].to_broadcast([2, 6 * D])).then_inc(small, 16)
                for n in range(2):
                    sp.dma_start(gain[:, n, :], g.dram[f"norm{n + 1}_g"][l:l + 1, :].to_broadcast([2, D])).then_inc(small, 16)
                for n in range(NT):
                    if n >= WB:
                        sp.wait_ge(mm_done, n - WB + 1)
                    sp.dma_start(w[:, n % WB, :, :], wv[:, :, n * BANK:(n + 1) * BANK]).then_inc(landed[n % WB], 16)
                sp.wait_ge(evac, NT + 2)
                for q in range(6):
                    sp.dma_start(g.mod[2 * q:2 * q + 2, :], mod[:, q * D:(q + 1) * D]).then_inc(small, 16)
                sp.wait_ge(small, 16 * 9)

            @block.gpsimd
            def _(po):
                po.sem_clear(g.sems.other)

            @block.tensor
            def _(pe):
                for n in range(NT):
                    pe.wait_ge(landed[n % WB], 16 * (n // WB + 1))
                    if n >= 4:
                        pe.wait_ge(evac, n - 3)
                    for k in range(KD):
                        mm = pe.matmul(ps[0:2, n % 4, :], g.cond[:, k, :], w[:, n % WB, k, :], start=k == 0, stop=k == KD - 1)
                    mm.then_inc(mm_done, 1)

            @block.vector
            def _(ve):
                step = chained(ve, evac)
                ve.wait_ge(small, 48)
                for n in range(NT):
                    ve.wait_ge(mm_done, n + 1)
                    step(ve.tensor_tensor(mod[:, n * BANK:(n + 1) * BANK], ps[0:2, n % 4, :], bias[:, n * BANK:(n + 1) * BANK], ALU.add))
                for n, part in ((0, 1), (1, 4)):
                    s = mod[:, part * D:(part + 1) * D]
                    step(ve.scalar_tensor_tensor(out=s, in0=s, scalar=1.0, in1=gain[:, n, :], op0=ALU.add, op1=ALU.mult))


def stage_norm(nc, g, tiles, part, H, HT):
    with ExitStack() as st:
        sem = g.sems.begin(st)
        h = H if H is not None else st.enter_context(nc.sbuf_tensor(g.name("h_rows"), [P, TILES, D], F32))
        sq = st.enter_context(nc.sbuf_tensor(g.name("squares"), [P, 2, D], F32))
        ms = st.enter_context(nc.sbuf_tensor(g.name("mean_square"), [P, TILES], F32))
        bc = st.enter_context(nc.psum_tensor(g.name("mod_bc"), [P, 4, BANK], F32))
        tp = st.enter_context(nc.psum_tensor(g.name("h_tp"), [P, 4, BANK], F32))
        ms_done, root_done, bc_done, v_done, h_done = sem("ms_done"), sem("root_done"), sem("bc_done"), sem("v_done"), sem("h_done")
        tp_done, tp_out = sem("tp_done"), sem("tp_out")
        streams = [w for w in (0, 1) if any((i < 2) == (w == 0) for i in tiles)]
        mine = lambda w: [i for i in tiles if (i < 2) == (w == 0)]

        with nc.Block() as block:
            @block.gpsimd
            def _(po):
                po.sem_clear(g.sems.other)

            @block.scalar
            def _(ac):
                for n, i in enumerate(tiles):
                    if n >= 2:
                        ac.wait_ge(ms_done, n - 1)
                    ac.activation(sq[:, n % 2, :], g.X[:, i, :], ACT.Square, scale=float(D) ** -0.5,
                                  accum_out=ms[:, i:i + 1]).then_inc(ms_done, 1)
                ac.wait_ge(v_done, 1)
                ac.activation(ms[:, tiles[0]:tiles[-1] + 1], ms[:, tiles[0]:tiles[-1] + 1], ACT.Sqrt).then_inc(root_done, 1)
                for n in range(2 * len(tiles)):
                    i, half = tiles[n // 2], n % 2
                    ac.wait_ge(tp_done, n + 1)
                    ac.activation(HT[:, half * 4:half * 4 + 4, i * P:(i + 1) * P],
                                  tp[:, n % 4, :].rearrange("p (k t) -> p k t", k=4), ACT.Copy).then_inc(tp_out, 1)

            @block.tensor
            def _(pe):
                n = 0
                for s, w in enumerate(streams):
                    if s:
                        pe.wait_ge(h_done, len(mine(streams[0])))
                    for q in range(2):
                        row = 2 * (part + 1 - q) + 1 - w
                        for j in range(2):
                            mm = pe.matmul(bc[:, 2 * q + j, :], g.ident[0:12, row:row + 1].to_broadcast([12, P]), g.mod[:, j * BANK:(j + 1) * BANK], start=True, stop=True)
                    mm.then_inc(bc_done, 1)
                    for i in mine(w):
                        pe.wait_ge(h_done, n // 2 + 1)
                        for half in range(2):
                            if n >= 4:
                                pe.wait_ge(tp_out, n - 3)
                            for k in range(4):
                                mm = pe.transpose(tp[:, n % 4, k * P:(k + 1) * P], h[:, i, (half * 4 + k) * P:(half * 4 + k + 1) * P], g.ident[:])
                            mm.then_inc(tp_done, 1)
                            n += 1

            @block.vector
            def _(ve):
                step = chained(ve, v_done)
                ve.wait_ge(ms_done, len(tiles))
                t0, t1 = tiles[0], tiles[-1] + 1
                step(ve.tensor_scalar(ms[:, t0:t1], ms[:, t0:t1], 1e-6, None, ALU.add))
                ve.wait_ge(root_done, 1)
                step(ve.reciprocal(ms[:, t0:t1], ms[:, t0:t1]))
                for s, w in enumerate(streams):
                    ve.wait_ge(bc_done, s + 1)
                    for i in mine(w):
                        step(ve.scalar_tensor_tensor(out=h[:, i, :], in0=g.X[:, i, :], scalar=ms[:, i:i + 1],
                                                     in1=bc[:, 0:2, :].rearrange("p a b -> p (a b)"), op0=ALU.mult, op1=ALU.mult))
                        ve.tensor_tensor(h[:, i, :], h[:, i, :], bc[:, 2:4, :].rearrange("p a b -> p (a b)"), ALU.add).then_inc(h_done, 1)


def stage_input_projection(nc, g, l, HT):
    CW, WB, ZB = 3, 3, 3
    with ExitStack() as st:
        sem = g.sems.begin(st)
        w = st.enter_context(nc.sbuf_tensor(g.name("w_in_ring"), [P, WB, KD, CW * P], F32))
        z = st.enter_context(nc.sbuf_tensor(g.name("z_padded"), [P, ZB, 2, SEQ + 2], F32))
        ps = st.enter_context(nc.psum_tensor(g.name("z_ps"), [P, 4, BANK], F32))
        landed = [sem(f"w_in_landed{b}") for b in range(WB)]
        padded, mm_done, evac, conv_done, v_done = sem("padded"), sem("mm_done"), sem("evacuated"), sem("conv_done"), sem("v_done")
        wv = g.dram["w_in"][l].rearrange("(k p) n -> p k n", p=P)
        cw, cb = ROWS["conv_w"], ROWS["conv_b"]

        with nc.Block() as block:
            @block.sync
            def _(sp):
                for n in range(IN_TILES // CW):
                    if n >= WB:
                        sp.wait_ge(mm_done, (n - WB + 1) * CW)
                    sp.dma_start(w[:, n % WB, :, :], wv[:, :, n * CW * P:(n + 1) * CW * P]).then_inc(landed[n % WB], 16)

            @block.gpsimd
            def _(po):
                po.sem_clear(g.sems.other)
                po.memset(z[:], 0.0).then_inc(padded, 1)

            @block.tensor
            def _(pe):
                for j in range(IN_TILES):
                    n = j // CW
                    pe.wait_ge(landed[n % WB], 16 * (n // WB + 1))
                    if j >= 4:
                        pe.wait_ge(evac, j - 3)
                    for k in range(KD):
                        mm = pe.matmul(ps[:, j % 4, :], w[:, n % WB, k, (j % CW) * P:(j % CW + 1) * P], HT[:, k, :], start=k == 0, stop=k == KD - 1)
                    mm.then_inc(mm_done, 1)

            @block.scalar
            def _(ac):
                ac.wait_ge(padded, 1)
                for j in range(IN_TILES):
                    ac.wait_ge(mm_done, j + 1)
                    if j < CONV_TILES:
                        if j >= ZB:
                            ac.wait_ge(conv_done, j - ZB + 1)
                        ac.activation(z[:, j % ZB, :, 1:SEQ + 1], ps[:, j % 4, :].rearrange("p (s t) -> p s t", s=2), ACT.Copy)
                        ac.activation(g.S[:, j, :], ps[:, j % 4, :], ACT.Identity, scale=g.par[:, l, cw + 12 + j:cw + 13 + j],
                                      bias=g.par[:, l, cb + j:cb + j + 1]).then_inc(evac, 1)
                    else:
                        f = {LORA0: ACT.Tanh, LORA0 + 2: ACT.Sigmoid}.get(j, ACT.Copy)
                        ac.activation(g.S[:, j, :], ps[:, j % 4, :], f).then_inc(evac, 1)

            @block.vector
            def _(ve):
                step = chained(ve, v_done)
                for j in range(CONV_TILES):
                    ve.wait_ge(evac, j + 1)
                    s = g.S[:, j, :].rearrange("p (s t) -> p s t", s=2)
                    step(ve.scalar_tensor_tensor(out=s, in0=z[:, j % ZB, :, 0:SEQ], scalar=g.par[:, l, cw + j:cw + j + 1], in1=s, op0=ALU.mult, op1=ALU.add))
                    ve.scalar_tensor_tensor(out=s, in0=z[:, j % ZB, :, 2:SEQ + 2], scalar=g.par[:, l, cw + 24 + j:cw + 25 + j], in1=s,
                                            op0=ALU.mult, op1=ALU.add).then_inc(conv_done, 1)


def stage_hyena(nc, g, l):
    FR = 2
    with ExitStack() as st:
        sem = g.sems.begin(st)
        sb = lambda name, shape: st.enter_context(nc.sbuf_tensor(g.name(name), shape, F32))
        w1, w2, w3, b3 = sb("hy_w1", [HY_EMB, HY_HID]), sb("hy_w2", [HY_HID, HY_HID]), sb("hy_w3", [HY_HID, 512]), sb("hy_b3", [1, 512])
        emb, window, dft = sb("emb", [HY_EMB, SEQ]), sb("window", [P, 2, 512]), sb("dft", [P, 4, 2, SEQ])
        arg, turns, hid = sb("hy_arg", [HY_HID, 2, SEQ]), sb("hy_turns", [HY_HID, 2, SEQ]), sb("hy_hid", [HY_HID, 2, SEQ])
        F, sq = sb("filter", [P, 2, 512]), sb("filter_sq", [P, 2, 512])
        even, odd, rk = sb("filter_even", [P, 2, HY_CH]), sb("filter_odd", [P, 2, HY_CH]), sb("filter_rnorm", [P, HY_CH])
        K = sb("filter_spectrum", [P, FR, 2, HY_CH])
        u, U = sb("u_cols", [P, 2, TOK]), sb("u_rows", [P, 2, 512])
        Yc, Yn, tmp = sb("y_cos", [P, FR, 512]), sb("y_sin", [P, FR, 512]), sb("y_tmp", [P, 512])
        hy, hsq, rs = sb("hy", [P, 2, TOK]), sb("hy_sq", [P, 2, TOK]), sb("hy_rnorm", [P, TOK])
        ps = st.enter_context(nc.psum_tensor(g.name("hy_ps"), [P, 8, BANK], F32))
        w_in, v_done, t_done, a_done = sem("w_in"), sem("v_done"), sem("t_done"), sem("a_done")
        layer_in, sin_done, filt_in, F_done, norm_sum, rk_ready, K_in, K_done = (
            sem(n) for n in ("layer_arg_in", "sin_done", "filter_in", "filter_done", "norm_sum", "norm_ready", "spectrum_in", "spectrum_done"))
        arg_ready, root_done, eps_done, u_done, ut_in, U_done, Uf_in, Y_done, y_in, hy_done, ms_in = (
            sem(n) for n in ("arg_ready", "root_done", "eps_done", "u_done", "u_transposed", "u_rows_done", "u_spectrum_in", "y_spectrum_done", "y_in", "hy_done", "hy_ms_in"))
        R = ROWS
        par = lambda name, k=0, p=P: g.par[0:p, l, R[name] + k:R[name] + k + 1]
        C = lambda t, f: dft[:, 0, t, f * P:(f + 1) * P]
        Sn = lambda t, f: dft[:, 1, t, f * P:(f + 1) * P]

        with nc.Block() as block:
            @block.sync
            def _(sp):
                for dst, name in ((w1, "hy_w1"), (w2, "hy_w2"), (w3, "hy_w3")):
                    sp.dma_start(dst[:], g.dram[name][l]).then_inc(w_in, 16)
                sp.dma_start(b3[:], g.dram["hy_b3"][l:l + 1, :]).then_inc(w_in, 16)
                for dst, name in ((emb, "k_emb"), (window, "k_window"), (dft, "k_dft")):
                    sp.dma_start(dst[:], g.dram[name]).then_inc(w_in, 16)

            @block.gpsimd
            def _(po):
                po.sem_clear(g.sems.other)

            @block.tensor
            def _(pe):
                pe.wait_ge(w_in, 16 * 7)
                pe.matmul(ps[0:HY_HID, 0, 0:SEQ], w1[:], emb[:], start=True, stop=True).then_inc(layer_in, 1)
                pe.wait_ge(u_done, 1)
                for t in range(2):
                    for s in range(2):
                        for c in range(2):
                            mm = pe.transpose(ps[:, 5 + t, s * 256 + c * P:s * 256 + (c + 1) * P], u[:, c, (2 * s + t) * P:(2 * s + t + 1) * P], g.ident[:])
                mm.then_inc(ut_in, 1)
                pe.wait_ge(sin_done, 1)
                pe.matmul(ps[0:HY_HID, 1, 0:SEQ], w2[:], hid[:, 0, :], start=True, stop=True).then_inc(layer_in, 1)
                pe.wait_ge(sin_done, 2)
                for t in range(2):
                    pe.matmul(ps[:, 2 + t, :], hid[:, 1, t * P:(t + 1) * P], w3[:], start=True, stop=False)
                    mm = pe.matmul(ps[:, 2 + t, :], g.ones[0:1, :], b3[:], start=False, stop=True)
                mm.then_inc(filt_in, 1)
                pe.wait_ge(U_done, 1)
                for f in range(FR):
                    for q, basis in ((0, C), (1, Sn)):
                        for t in range(2):
                            mm = pe.matmul(ps[:, 4 + 2 * f + q, :], basis(t, f), U[:, t, :], start=t == 0, stop=t == 1)
                mm.then_inc(Uf_in, 1)
                pe.wait_ge(F_done, 1)
                for n in range(4):
                    mm = pe.matmul(ps[:, 0, 0:HY_CH], g.ones[:], sq[:, n // 2, (n % 2) * HY_CH:(n % 2 + 1) * HY_CH], start=n == 0, stop=n == 3)
                mm.then_inc(norm_sum, 1)
                pe.wait_ge(F_done, 2)
                for f in range(FR):
                    for q, (basis, part) in enumerate(((C, even), (Sn, odd))):
                        for t in range(2):
                            mm = pe.matmul(ps[:, 2 + f, q * HY_CH:(q + 1) * HY_CH], basis(t, f), part[:, t, :], start=t == 0, stop=t == 1)
                mm.then_inc(K_in, 1)
                pe.wait_ge(Y_done, 1)
                for c in range(2):
                    for s in range(2):
                        cols = slice(s * 256 + c * P, s * 256 + (c + 1) * P)
                        for f in range(FR):
                            pe.matmul(ps[:, c, s * 256:(s + 1) * 256], Yc[:, f, cols], dft[:, 2, f, :], start=f == 0, stop=False)
                            mm = pe.matmul(ps[:, c, s * 256:(s + 1) * 256], Yn[:, f, cols], dft[:, 3, f, :], start=False, stop=f == FR - 1)
                mm.then_inc(y_in, 1)
                pe.wait_ge(hy_done, 1)
                for c in range(2):
                    mm = pe.matmul(ps[:, 2, :], g.ones[:], hsq[:, c, :], start=c == 0, stop=c == 1)
                mm.then_inc(ms_in, 1)

            @block.scalar
            def _(ac):
                for k in range(2):
                    ac.wait_ge(arg_ready, k + 1)
                    ac.activation(hid[:, k, :], arg[:, k, :], ACT.Sin).then_inc(sin_done, 1)
                for k, t in enumerate((rk, rs)):
                    ac.wait_ge(eps_done, k + 1)
                    ac.activation(t[:], t[:], ACT.Sqrt).then_inc(root_done, 1)

            @block.vector
            def _(ve):
                step = chained(ve, v_done)
                step(ve.tensor_tensor(u[:], g.S[:, 2:4, :], g.S[:, 4:6, :], ALU.mult))
                ve.sem_inc(u_done, 1)
                for k in range(2):
                    ve.wait_ge(layer_in, k + 1)
                    a, n = arg[:, k, :], turns[:, k, :]
                    step(ve.tensor_scalar(a, ps[0:HY_HID, k, 0:SEQ], par(f"hy_b{k + 1}", 0, HY_HID), par("hy_freq", k, HY_HID), ALU.add, ALU.mult))
                    step(ve.tensor_scalar(n, a, 1.0 / TWO_PI, 12582912.0, ALU.mult, ALU.add))
                    step(ve.tensor_scalar(n, n, 12582912.0, None, ALU.subtract))
                    step(ve.scalar_tensor_tensor(out=a, in0=n, scalar=-TWO_PI, in1=a, op0=ALU.mult, op1=ALU.add))
                    ve.tensor_scalar(a, a, PI_BELOW, -PI_BELOW, ALU.min, ALU.max).then_inc(arg_ready, 1)
                    if k == 0:
                        ve.wait_ge(ut_in, 1)
                        ve.tensor_copy(U[:], ps[:, 5:7, :]).then_inc(U_done, 1)
                ve.wait_ge(filt_in, 1)
                step(ve.tensor_tensor(F[:], ps[:, 2:4, :], window[:], ALU.mult))
                ve.tensor_tensor(sq[:], F[:], F[:], ALU.mult).then_inc(F_done, 1)
                step(ve.tensor_tensor(even[:], F[:, :, 0:HY_CH], F[:, :, HY_CH:512], ALU.add))
                ve.tensor_tensor(odd[:], F[:, :, HY_CH:512], F[:, :, 0:HY_CH], ALU.subtract).then_inc(F_done, 1)
                ve.wait_ge(norm_sum, 1)
                ve.tensor_scalar(rk[:], ps[:, 0, 0:HY_CH], 1e-6, None, ALU.add).then_inc(eps_done, 1)
                ve.wait_ge(root_done, 1)
                step(ve.reciprocal(rk[:], rk[:]))
                ve.wait_ge(K_in, 1)
                for f in range(FR):
                    step(ve.tensor_tensor(K[:, f, :, :], ps[:, 2 + f, :].rearrange("p (q c) -> p q c", q=2), rk[:].unsqueeze(1).to_broadcast([P, 2, HY_CH]), ALU.mult))
                ve.wait_ge(Uf_in, 1)
                for f in range(FR):
                    view = lambda x: x.rearrange("p (s c) -> p s c", s=2)
                    uc, us = view(ps[:, 4 + 2 * f, :]), view(ps[:, 5 + 2 * f, :])
                    kr, ki = (K[:, f, q, :].unsqueeze(1).to_broadcast([P, 2, HY_CH]) for q in range(2))
                    for dst, a, b, op in ((Yc, (uc, kr), (us, ki), ALU.add), (Yn, (us, kr), (uc, ki), ALU.subtract)):
                        step(ve.tensor_tensor(view(dst[:, f, :]), *a, ALU.mult))
                        step(ve.tensor_tensor(view(tmp[:]), *b, ALU.mult))
                        step(ve.tensor_tensor(dst[:, f, :], dst[:, f, :], tmp[:], op))
                ve.sem_inc(Y_done, 1)
                ve.wait_ge(y_in, 1)
                for c in range(2):
                    step(ve.scalar_tensor_tensor(out=hy[:, c, :], in0=u[:, c, :], scalar=par("hy_bias", c), in1=ps[:, c, :], op0=ALU.mult, op1=ALU.add))
                step(ve.tensor_tensor(hy[:], hy[:], g.S[:, 0:2, :], ALU.mult))
                ve.tensor_tensor(hsq[:], hy[:], hy[:], ALU.mult).then_inc(hy_done, 1)
                ve.wait_ge(ms_in, 1)
                ve.tensor_scalar(rs[:], ps[:, 2, :], 1.0 / HY_CH, 1e-6, ALU.mult, ALU.add).then_inc(eps_done, 1)
                ve.wait_ge(root_done, 2)
                step(ve.reciprocal(rs[:], rs[:]))
                for c in range(2):
                    step(ve.scalar_tensor_tensor(out=g.mix[:, c, :], in0=hy[:, c, :], scalar=par("hy_out_g", c), in1=rs[:], op0=ALU.mult, op1=ALU.mult))


def stage_attention(nc, g, l, tiles):
    SCALE = float(AT_HD) ** -0.5
    units = [(i, j) for i in tiles for j in range(4)]
    keys = lambda i: TOK if i >= 2 else SEQ
    with ExitStack() as st:
        sem = g.sems.begin(st)
        sb = lambda name, shape: st.enter_context(nc.sbuf_tensor(g.name(name), shape, F32))
        rot, KS, VT = sb("rotated", [P, 5, SEQ]), sb("k_swapped", [P, TOK]), sb("v_rows", [P, TILES, P])
        E, PT = sb("scores", [P, 2, 2, TOK]), sb("probs_cols", [P, 2, 2, TOK])
        mx, nm, total, es, rden = (sb(n, [P, 2, 2]) for n in ("row_max", "neg_max", "row_sum", "sink_exp", "rden"))
        O, osq, ms = sb("attn_rows", [P, TILES, AT_W]), sb("attn_sq", [P, AT_W]), sb("attn_ms", [P, TILES])
        sps = st.enter_context(nc.psum_tensor(g.name("scores_ps"), [P, 2, 2, BANK], F32))
        tps = st.enter_context(nc.psum_tensor(g.name("probs_ps"), [P, 2, BANK], F32))
        ops = st.enter_context(nc.psum_tensor(g.name("out_ps"), [P, 2, BANK], F32))
        rot_in, rope_done, ks_in, kv_done, v_done = (sem(n) for n in ("rot_in", "rope_done", "kv_in", "kv_done", "v_done"))
        s_in, s_out, max_done, exp_done, pt_in, pt_out, pv_in, o_done = (
            sem(n) for n in ("scores_in", "scores_out", "max_done", "exp_done", "probs_in", "probs_out", "pv_in", "o_done"))
        sq_done, eps_done, root_done, on_done, ot_in, ot_out, sqa = (
            sem(n) for n in ("sq_done", "eps_done", "root_done", "o_normed", "o_cols_in", "o_cols_out", "sq_each"))
        lat = slice(SEQ, TOK)

        with nc.Block() as block:
            @block.gpsimd
            def _(po):
                po.sem_clear(g.sems.other)

            @block.tensor
            def _(pe):
                for j in range(5):
                    mm = pe.matmul(sps[:, j // 4, j // 2 % 2, (j % 2) * SEQ:(j % 2 + 1) * SEQ], g.rot[:], g.S[:, Q0 + j, lat], start=True, stop=True)
                mm.then_inc(rot_in, 1)
                for i in range(TILES):
                    pe.transpose(ops[:, 1, i * P:(i + 1) * P], g.S[:, V0, i * P:(i + 1) * P], g.ident[:])
                pe.wait_ge(rope_done, 1)
                pe.matmul(ops[:, 0, :], g.swap[:], g.S[:, K0, :], start=True, stop=True).then_inc(ks_in, 1)

                def scores(n):
                    i, j = units[n]
                    if n >= 2:
                        pe.wait_ge(s_out, n - 1)
                    for h in range(2):
                        k = g.S[64 * h:64 * h + 64, K0, TOK - keys(i) if False else 0:keys(i)] if j // 2 == h else KS[64 * h:64 * h + 64, 0:keys(i)]
                        mm = pe.matmul(sps[:, n % 2, h, 0:keys(i)], g.S[64 * h:64 * h + 64, Q0 + j, i * P:(i + 1) * P], k, start=True, stop=True)
                    mm.then_inc(s_in, 1)

                def values(n):
                    i, j = units[n]
                    pe.wait_ge(exp_done, n + 1)
                    if n >= 1:
                        pe.wait_ge(pt_out, 2 * n)
                    for h in range(2):
                        for t in range(keys(i) // P):
                            mm = pe.transpose(tps[:, h, t * P:(t + 1) * P], E[:, n % 2, h, t * P:(t + 1) * P], g.ident[:])
                        mm.then_inc(pt_in, 1)
                    pe.wait_ge(pt_out, 2 * n + 2)
                    if n >= 2:
                        pe.wait_ge(o_done, n - 1)
                    for h in range(2):
                        for t in range(keys(i) // P):
                            mm = pe.matmul(ops[:, n % 2, h * 64:h * 64 + 64], PT[:, n % 2, h, t * P:(t + 1) * P],
                                           VT[:, t, 64 * (j // 2):64 * (j // 2) + 64], start=t == 0, stop=t == keys(i) // P - 1)
                    mm.then_inc(pv_in, 1)

                pe.wait_ge(kv_done, 2)
                scores(0)
                for n in range(len(units)):
                    if n + 1 < len(units):
                        scores(n + 1)
                    values(n)
                for m, i in enumerate(tiles):
                    pe.wait_ge(on_done, m + 1)
                    if m >= 2:
                        pe.wait_ge(ot_out, m - 1)
                    for j in range(4):
                        mm = pe.transpose(tps[:, m % 2, j * P:(j + 1) * P], O[:, i, j * P:(j + 1) * P], g.ident[:])
                    mm.then_inc(ot_in, 1)

            @block.scalar
            def _(ac):
                ac.wait_ge(ks_in, 1)
                ac.activation(KS[:], ops[:, 0, :], ACT.Copy).then_inc(kv_done, 1)
                ac.activation(VT[:].rearrange("p i c -> p (i c)"), ops[:, 1, :], ACT.Copy).then_inc(kv_done, 1)
                for n, (i, j) in enumerate(units):
                    b = n % 2
                    ac.wait_ge(max_done, n + 1)
                    for h in range(2):
                        ac.activation(E[:, b, h, 0:keys(i)], E[:, b, h, 0:keys(i)], ACT.Exp, bias=nm[:, b, h:h + 1], scale=SCALE,
                                      accum_out=total[:, b, h:h + 1])
                    ac.activation(es[:, b, :], es[:, b, :], ACT.Exp).then_inc(exp_done, 1)
                    ac.wait_ge(pt_in, 2 * n + 1)
                    ac.activation(PT[:, b, 0, 0:keys(i)], tps[:, 0, 0:keys(i)], ACT.Copy).then_inc(pt_out, 1)
                ac.wait_ge(o_done, len(units))
                for m, i in enumerate(tiles):
                    if m:
                        ac.wait_ge(sq_done, m)
                    ac.activation(osq[:], O[:, i, :], ACT.Square, scale=float(AT_W) ** -0.5, accum_out=ms[:, i:i + 1]).then_inc(sq_done, 1)
                ac.wait_ge(eps_done, 1)
                ac.activation(ms[:, tiles[0]:tiles[-1] + 1], ms[:, tiles[0]:tiles[-1] + 1], ACT.Sqrt).then_inc(root_done, 1)
                for m, i in enumerate(tiles):
                    ac.wait_ge(ot_in, m + 1)
                    for j in range(4):
                        r = ROWS["at_out_g"] + j
                        a = ac.activation(g.mix[:, 4 + j, i * P:(i + 1) * P], tps[:, m % 2, j * P:(j + 1) * P], ACT.Copy, scale=g.par[:, l, r:r + 1])
                    a.then_inc(ot_out, 1)

            @block.vector
            def _(ve):
                step = chained(ve, v_done)
                ve.wait_ge(rot_in, 1)
                qk = g.S[:, Q0:Q0 + 5, lat]
                step(ve.tensor_tensor(rot[:], sps[:].rearrange("p a b (c t) -> p (a b c) t", c=2)[:, 0:5, :], g.rope[:, 1, :].unsqueeze(1).to_broadcast([P, 5, SEQ]), ALU.mult))
                step(ve.tensor_tensor(qk, qk, g.rope[:, 0, :].unsqueeze(1).to_broadcast([P, 5, SEQ]), ALU.mult))
                ve.tensor_tensor(qk, qk, rot[:], ALU.add).then_inc(rope_done, 1)

                def softmax_head(n):
                    i, j = units[n]
                    b, w = n % 2, keys(i)
                    ve.wait_ge(s_in, n + 1)
                    if n >= 2:
                        ve.wait_ge(pt_in, 2 * n - 2)
                    if i >= 2:
                        ve.tensor_tensor(E[:, b, :, 0:w], sps[:, b, :, 0:w], g.band[:, i - 2, :].unsqueeze(1).to_broadcast([P, 2, TOK]), ALU.add).then_inc(s_out, 1)
                    else:
                        ve.tensor_copy(E[:, b, :, 0:w], sps[:, b, :, 0:w]).then_inc(s_out, 1)
                    ve.wait_ge(s_out, n + 1)
                    sink = g.sink[:, l, 2 * j:2 * j + 2]
                    step(ve.tensor_reduce(mx[:, b, :], E[:, b, :, 0:w], AX.X, ALU.max))
                    step(ve.tensor_tensor(mx[:, b, :], mx[:, b, :], g.sink8[:, l, 2 * j:2 * j + 2], ALU.max))
                    step(ve.tensor_scalar(nm[:, b, :], mx[:, b, :], -SCALE, None, ALU.mult))
                    ve.tensor_tensor(es[:, b, :], sink, nm[:, b, :], ALU.add).then_inc(max_done, 1)

                softmax_head(0)
                for n, (i, j) in enumerate(units):
                    b = n % 2
                    if n + 1 < len(units):
                        softmax_head(n + 1)
                    ve.wait_ge(exp_done, n + 1)
                    step(ve.tensor_tensor(rden[:, b, :], total[:, b, :], es[:, b, :], ALU.add))
                    step(ve.reciprocal(rden[:, b, :], rden[:, b, :]))
                    ve.wait_ge(pt_in, 2 * n + 2)
                    ve.tensor_copy(PT[:, b, 1, 0:keys(i)], tps[:, 1, 0:keys(i)]).then_inc(pt_out, 1)
                    ve.wait_ge(pv_in, n + 1)
                    ve.tensor_tensor(O[:, i, j * P:(j + 1) * P].rearrange("p (h c) -> p h c", h=2), ops[:, b, 0:P].rearrange("p (h c) -> p h c", h=2),
                                     rden[:, b, :].unsqueeze(2).to_broadcast([P, 2, 64]), ALU.mult).then_inc(o_done, 1)
                ve.wait_ge(sq_done, len(tiles))
                part = ms[:, tiles[0]:tiles[-1] + 1]
                ve.tensor_scalar(part, part, 1e-6, None, ALU.add).then_inc(eps_done, 1)
                ve.wait_ge(root_done, 1)
                step(ve.reciprocal(part, part))
                for i in tiles:
                    ve.tensor_scalar(O[:, i, :], O[:, i, :], ms[:, i:i + 1], None, ALU.mult).then_inc(on_done, 1)


KK, RR, KC, VC = 0, 6, 8, 10
B_AT, KD_AT, Y_AT = (2, 4), (15, 17), (12, 19)


def stage_rwkv_operands(nc, g, l):
    with ExitStack() as st:
        sem = g.sems.begin(st)
        sb = lambda name, shape: st.enter_context(nc.sbuf_tensor(g.name(name), shape, F32))
        wup, aup = sb("w_up", [P, RW_W]), sb("a_up", [P, RW_W])
        sq, lw, keep = sb("kk_sq", [P, 2, TOK]), sb("log_decay", [P, 2, 2, TOK]), sb("chunk_keep", [P, TOK])
        ps = st.enter_context(nc.psum_tensor(g.name("rwkv_ps"), [P, 8, BANK], F32))
        w_in, keep_set, sq_done, kk_in, eps_done, root_done, kk_done, lora_in, sig_done, v_done, log_done, exp_done = (
            sem(n) for n in ("w_in", "keep_set", "sq_done", "kk_in", "eps_done", "root_done", "kk_done", "lora_in", "sig_done", "v_done", "log_done", "exp_done"))
        par = lambda name, k: g.par[:, l, ROWS[name] + k:ROWS[name] + k + 1]
        kk = g.S[:, KK:KK + 2, :]
        bank = lambda d, q, p: (2 + 4 * d + 2 * q + p) % 8

        with nc.Block() as block:
            @block.sync
            def _(sp):
                sp.dma_start(wup[:], g.dram["rw_w_up"][l].rearrange("d r n -> (d r) n")).then_inc(w_in, 16)
                sp.dma_start(aup[:], g.dram["rw_a_up"][l].rearrange("d r n -> (d r) n")).then_inc(w_in, 16)

            @block.gpsimd
            def _(po):
                po.sem_clear(g.sems.other)
                po.memset(keep[:], 1.0).then_inc(keep_set, 1)
                po.wait_ge(keep_set, 1)
                po.memset(keep[:].rearrange("p (c t) -> p c t", t=CHUNK)[:, :, 0:1], 0.0).then_inc(keep_set, 1)

            @block.tensor
            def _(pe):
                pe.wait_ge(w_in, 32)
                for d in range(2):
                    if d:
                        pe.wait_ge(sq_done, 1)
                        for p in range(2):
                            mm = pe.matmul(ps[:, p, :], g.pair[:], sq[:, p, :], start=True, stop=True)
                        mm.then_inc(kk_in, 1)
                        pe.wait_ge(eps_done, 1)
                    for q, (up, src) in enumerate(((wup, LORA0), (aup, LORA0 + 1))):
                        for p in range(2):
                            mm = pe.matmul(ps[:, bank(d, q, p), :], up[64 * d:64 * d + 64, p * P:(p + 1) * P], g.S[64 * d:64 * d + 64, src, :], start=True, stop=True)
                    mm.then_inc(lora_in, 1)

            @block.scalar
            def _(ac):
                for d in range(2):
                    ac.wait_ge(lora_in, d + 1)
                    for p in range(2):
                        ac.activation(lw[:, d, p, :], ps[:, bank(d, 0, p), :], ACT.Sigmoid, bias=par("rw_w0", 2 * d + p))
                        a = ac.activation(g.S[:, B_AT[d] + p, :], ps[:, bank(d, 1, p), :], ACT.Sigmoid, bias=par("rw_a0", 2 * d + p))
                    a.then_inc(sig_done, 1)
                ac.wait_ge(eps_done, 1)
                ac.activation(sq[:], sq[:], ACT.Sqrt).then_inc(root_done, 1)
                for d in range(2):
                    ac.wait_ge(log_done, d + 1)
                    ac.activation(g.eL[:, d, :, :], g.eN[:, d, :, :], ACT.Exp).then_inc(exp_done, 1)
                    ac.wait_ge(exp_done, 3 * d + 1)
                    ac.activation(g.eN[:, d, :, :], g.eN[:, d, :, :], ACT.Exp, scale=-1.0).then_inc(exp_done, 1)
                    ac.activation(g.eP[:, d, :, :], g.eP[:, d, :, :], ACT.Exp).then_inc(exp_done, 1)

            @block.vector
            def _(ve):
                step = chained(ve, v_done)
                for p in range(2):
                    step(ve.tensor_scalar(kk[:, p, :], g.S[:, KC + p, :], par("rw_k_k", p), None, ALU.mult))
                ve.tensor_tensor(sq[:], kk, kk, ALU.mult).then_inc(sq_done, 1)
                ve.wait_ge(kk_in, 1)
                ve.tensor_scalar(sq[:], ps[:, 0:2, :], 1e-12, None, ALU.add).then_inc(eps_done, 1)
                ve.wait_ge(keep_set, 2)
                for d in range(2):
                    ve.wait_ge(sig_done, d + 1)
                    step(ve.tensor_scalar(lw[:, d, :, :], lw[:, d, :, :], -DECAY, None, ALU.mult))
                    for p in range(2):
                        src, dst = lw[:, d, p, :], g.eN[:, d, p, :]
                        if d:
                            src, dst = lw[:, d, p, ::-1], g.eN[:, d, p, ::-1]
                        step(ve.tensor_tensor_scan(dst, keep[:], src, 0.0, ALU.mult, ALU.add))
                    ve.tensor_tensor(g.eP[:, d, :, :], g.eN[:, d, :, :], lw[:, d, :, :], ALU.subtract).then_inc(log_done, 1)
                ve.wait_ge(root_done, 1)
                step(ve.reciprocal(sq[:], sq[:]))
                step(ve.tensor_tensor(kk, kk, sq[:], ALU.mult))
                for d in range(2):
                    a, k = g.S[:, B_AT[d]:B_AT[d] + 2, :], g.S[:, KD_AT[d]:KD_AT[d] + 2, :]
                    for p in range(2):
                        step(ve.tensor_scalar(k[:, p, :], a[:, p, :], par("rw_k_a", p), g.omka[:, l, p:p + 1], ALU.mult, ALU.add))
                    step(ve.tensor_tensor(k, k, g.S[:, KC:KC + 2, :], ALU.mult))
                    step(ve.tensor_tensor(a, a, kk, ALU.mult))


def stage_rwkv_chunks(nc, g, l):
    STEPS = 14
    H4 = 4
    with ExitStack() as st:
        sem = g.sems.begin(st)
        ps = [st.enter_context(nc.psum_tensor(g.name(f"chunk_ps{d}"), [P, 4, BANK], F32)) for d in range(2)]

        class Stream:
            pass
        streams = []
        for d in range(2):
            s = Stream()
            sb = lambda name, shape: st.enter_context(nc.sbuf_tensor(g.name(f"{name}{d}"), shape, F32))
            s.AR = sb("a_r", [P, 2, 2, P])
            s.bt, s.kt, s.bh, s.kh, s.v = (sb(n, [P, 2, P]) for n in ("b_in", "k_in", "b_end", "k_end", "v_col"))
            s.rows1, s.rows2 = sb("rows_a_b", [P, 4, P]), sb("rows_k_v", [P, 4, P])
            s.A, s.AT, s.A32T, s.A64T = (sb(n, [P, H4, P]) for n in ("A16_", "A16T_", "A32T_", "A64T_"))
            s.MakT, s.MrbT, s.MrkT = (sb(n, [P, H4, P]) for n in ("MakT_", "MrbT_", "MrkT_"))
            s.A2, s.A2T, s.A4, s.A4T = (sb(n, [P, H4, P]) for n in ("A2_", "A2T_", "A4_", "A4T_"))
            s.X, s.XT = (sb(n, [P, H4, P]) for n in ("X_", "XT_"))
            s.A8, s.Q, s.rhs, s.GE = s.A, s.A2, s.AT, s.A4
            s.QT, s.S = sb("QT_", [P, 2, P]), sb("state_", [P, 2, P])
            s.Phi, s.Psi = s.A4T, s.A2T
            s.pe, s.ve, s.ac = sem(f"products{d}"), sem(f"vector_out{d}"), sem(f"scalar_out{d}")
            streams.append(s)
        ready = [sem(f"operands_ready{d}") for d in range(2)]
        v_done, state_zero = sem("v_done"), sem("state_zero")
        flat = lambda t: t.rearrange("p a b -> p (a b)")
        heads = lambda t: t.rearrange("p (h s) -> p h s", h=H4)
        mask = lambda d, m: g.masks[:, (m if d == 0 else m + 5), :].unsqueeze(1).to_broadcast([P, H4, P])
        maskT = lambda d, m: g.masks[:, (m + 5 if d == 0 else m), :].unsqueeze(1).to_broadcast([P, H4, P])
        M16, M32, M64, STRICT, INCL = range(5)
        tile_of = lambda d, n: n if d == 0 else (n ^ 1)

        with nc.Block() as block:
            @block.gpsimd
            def _(po):
                po.sem_clear(g.sems.other)
                for s in streams:
                    po.memset(s.S[:], 0.0).then_inc(state_zero, 1)

            @block.tensor
            def _(pe):
                for n in range(TILES):
                    for t in range(1, STEPS + 1):
                        for d, s in enumerate(streams):
                            b = ps[d]
                            if t == 1:
                                if n == 0:
                                    pe.wait_ge(state_zero, 2)
                                pe.wait_ge(ready[d], n + 1)
                            if n or t > 1:
                                pe.wait_ge(s.ve, n * STEPS + t - 1)
                                pe.wait_ge(s.ac, n * STEPS + t - 1)
                            hp = lambda h: slice(64 * (h // 2), 64 * (h // 2) + 64)
                            if t == 1:
                                for p in range(2):
                                    pe.transpose(b[:, 0, p * P:(p + 1) * P], s.AR[:, p, 0, :], g.ident[:])
                                    pe.transpose(b[:, 0, (2 + p) * P:(3 + p) * P], s.bh[:, p, :], g.ident[:])
                                    pe.transpose(b[:, 1, p * P:(p + 1) * P], s.kh[:, p, :], g.ident[:])
                                    pe.transpose(b[:, 1, (2 + p) * P:(3 + p) * P], s.v[:, p, :], g.ident[:])
                                for h in range(H4):
                                    mm = pe.matmul(b[:, 2 + h // 2, (h % 2) * 256:(h % 2) * 256 + 256], s.bt[hp(h), h % 2, :], flat(s.AR[hp(h), h % 2, :, :]), start=True, stop=True)
                            elif t == 2:
                                for h in range(H4):
                                    pe.matmul(b[:, h // 2, (h % 2) * 256:(h % 2) * 256 + 256], s.kt[hp(h), h % 2, :], flat(s.AR[hp(h), h % 2, :, :]), start=True, stop=True)
                                for h in range(H4):
                                    mm = pe.matmul(b[:, 2 + h // 2, (h % 2) * P:(h % 2 + 1) * P], s.AR[hp(h), h % 2, 0, :], s.bt[hp(h), h % 2, :], start=True, stop=True)
                            elif t in (3, 4, 5, 6, 7, 8, 9, 10, 11):
                                todo = {3: ((0, s.AT, s.A), (1, s.A, s.AT)),
                                        4: ((0, s.A2T, s.A2), (1, s.A2, s.A2T), (2, s.XT, s.A2), (3, s.A2, s.XT)),
                                        5: ((0, s.A4T, s.A4), (2, s.XT, s.A4), (3, s.A4, s.XT)),
                                        6: ((2, s.XT, s.A8), (3, s.A8, s.XT)),
                                        7: ((0, s.A32T, s.X),),
                                        8: ((2, s.XT, s.Q), (3, s.Q, s.XT)),
                                        9: ((0, s.A64T, s.X),),
                                        10: ((3, s.Q, s.XT),),
                                        11: ((0, s.XT, s.rhs),)}[t]
                                for q, lhsT, rhs in todo:
                                    for h in range(H4):
                                        mm = pe.matmul(b[:, q, h * P:(h + 1) * P], lhsT[:, h, :], rhs[:, h, :], start=True, stop=True)
                                if t == 3:
                                    for h in range(H4):
                                        mm = pe.matmul(b[:, 2, h * 64:(h + 1) * 64], s.MakT[:, h, :], s.rows2[:, 2 + h % 2, hp(h)], start=True, stop=True)
                            elif t == 12:
                                G, E = s.GE[:, 0:2, :], s.GE[:, 2:4, :]
                                bh, kh, v = s.rows1[:, 2:4, :], s.rows2[:, 0:2, :], s.rows2[:, 2:4, :]
                                for h in range(H4):
                                    p, c = h % 2, slice((h % 2) * P, (h % 2 + 1) * P)
                                    pe.matmul(b[hp(h), 0, c], G[:, p, hp(h)], s.MrbT[:, h, :], start=True, stop=True)
                                    pe.matmul(b[hp(h), 1, c], E[:, p, hp(h)], s.MrbT[:, h, :], start=True, stop=False)
                                    pe.matmul(b[hp(h), 1, c], v[:, p, hp(h)], s.MrkT[:, h, :], start=False, stop=True)
                                for c in range(2):
                                    r = slice(64 * c, 64 * c + 64)
                                    for p in range(2):
                                        o, o2 = slice(p * P, (p + 1) * P), slice((2 + p) * P, (3 + p) * P)
                                        pe.matmul(b[:, 2 + c, o], G[r, p, :], bh[r, p, :], start=True, stop=True)
                                        pe.matmul(b[:, 2 + c, o2], bh[r, p, :], E[r, p, :], start=True, stop=False)
                                        mm = pe.matmul(b[:, 2 + c, o2], kh[r, p, :], v[r, p, :], start=False, stop=True)
                            else:
                                c = (t - 13) if d == 0 else (14 - t)
                                for p in range(2):
                                    pe.matmul(b[:, 0, p * 64:(p + 1) * 64], s.S[:, p, :], s.QT[:, p, 64 * c:64 * c + 64], start=True, stop=True)
                                    mm = pe.matmul(b[:, 1, p * P:(p + 1) * P], s.Phi[:, 2 * c + p, :], s.S[:, p, :], start=True, stop=True)
                            mm.then_inc(s.pe, 1)

            @block.scalar
            def _(ac):
                for n in range(TILES):
                    for t in range(1, STEPS + 1):
                        for d, s in enumerate(streams):
                            b = ps[d]
                            ac.wait_ge(s.pe, n * STEPS + t)
                            copies = {1: ((flat(s.rows1[:]), b[:, 0, :]), (flat(s.rows2[:]), b[:, 1, :])),
                                      3: ((flat(s.A2[:]), b[:, 0, :]), (flat(s.A2T[:]), b[:, 1, :])),
                                      4: ((flat(s.A4[:]), b[:, 0, :]), (flat(s.A4T[:]), b[:, 1, :])),
                                      5: ((flat(s.A8[:]), b[:, 0, :]),),
                                      7: ((flat(s.Q[:]), b[:, 0, :]),),
                                      9: ((flat(s.Q[:]), b[:, 0, :]),),
                                      11: tuple((s.GE[:, 2 * q:2 * q + 2, :].rearrange("p a (b c) -> p b a c", b=2),
                                                b[:, 0, :].rearrange("p (b a q c) -> p b a q c", b=2, a=2, q=2)[:, :, :, q, :]) for q in range(2))}.get(t, ())
                            if t == 12:
                                tok = slice(tile_of(d, n) * P, tile_of(d, n) * P + P)
                                copies = ((g.S[:, Y_AT[d]:Y_AT[d] + 2, tok], b[:, 1, 0:2 * P].rearrange("p (a c) -> p a c", a=2)),)
                            for dst, src in copies:
                                a = ac.activation(dst, src, ACT.Copy)
                            if copies:
                                a.then_inc(s.ac, 1)
                            else:
                                ac.sem_inc(s.ac, 1)

            @block.vector
            def _(ve):
                step = chained(ve, v_done)

                def operands(n, d):
                    s, i = streams[d], tile_of(d, n)
                    tok = slice(i * P, i * P + P)
                    if n:
                        ve.wait_ge(s.pe, (n - 1) * STEPS + 12)
                    eL, eN, eP = (x[:, d, :, tok] for x in (g.eL, g.eN, g.eP))
                    b, k = g.S[:, B_AT[d]:B_AT[d] + 2, tok], g.S[:, KD_AT[d]:KD_AT[d] + 2, tok]
                    ve.scalar_tensor_tensor(out=s.AR[:, :, 0, :], in0=g.S[:, KK:KK + 2, tok], scalar=-1.0, in1=eP, op0=ALU.mult, op1=ALU.mult)
                    ve.tensor_tensor(s.AR[:, :, 1, :], g.S[:, RR:RR + 2, tok], eL, ALU.mult)
                    ve.tensor_copy(s.v[:], g.S[:, VC:VC + 2, tok])
                    step(ve.tensor_tensor(s.bt[:], b, eN, ALU.mult))
                    step(ve.tensor_tensor(s.kt[:], k, eN, ALU.mult))
                    end = CHUNK - 1 if d == 0 else 0
                    for p in range(2):
                        pe_ = g.eL[:, d, p, i * P + end:i * P + end + CHUNK + 1:CHUNK].unsqueeze(2).to_broadcast([P, 2, CHUNK])
                        split = lambda x: x.rearrange("p (c t) -> p c t", c=2)
                        ve.tensor_tensor(split(s.bh[:, p, :]), split(s.bt[:, p, :]), pe_, ALU.mult)
                        o = ve.tensor_tensor(split(s.kh[:, p, :]), split(s.kt[:, p, :]), pe_, ALU.mult)
                    o.then_inc(ready[d], 1)

                def evacuate(n, t, d):
                    s, b = streams[d], ps[d]
                    ve.wait_ge(s.pe, n * STEPS + t)
                    two = lambda q, x: b[:, q:q + 2, :].rearrange("p a (h x c) -> p (a h) x c", h=2, x=2)[:, :, x, :]
                    idb = g.ident[:].unsqueeze(1).to_broadcast([P, H4, P])
                    if t == 1:
                        step(ve.tensor_tensor(s.AT[:], two(2, 0), maskT(d, M16), ALU.mult))
                        ve.tensor_tensor(s.A32T[:], two(2, 0), maskT(d, M32), ALU.mult)
                        ve.tensor_tensor(s.A64T[:], two(2, 0), maskT(d, M64), ALU.mult)
                        ve.tensor_tensor(s.XT[:], s.AT[:], idb, ALU.add)
                        o = ve.tensor_tensor(s.MrbT[:], two(2, 1), maskT(d, INCL), ALU.mult)
                    elif t == 2:
                        step(ve.tensor_tensor(s.A[:].rearrange("p (a h) c -> p a h c", a=2), b[:, 2:4, 0:2 * P].rearrange("p a (h c) -> p a h c", h=2),
                                              mask(d, M16).rearrange("p (a h) c -> p a h c", a=2), ALU.mult))
                        ve.tensor_tensor(s.MakT[:], two(0, 0), maskT(d, STRICT), ALU.mult)
                        ve.tensor_tensor(s.X[:], s.A[:], idb, ALU.add)
                        o = ve.tensor_tensor(s.MrkT[:], two(0, 1), maskT(d, INCL), ALU.mult)
                    elif t == 3:
                        ve.wait_ge(s.ac, n * STEPS + 1)
                        ve.tensor_copy(s.rhs[:, :, 0:64].rearrange("p (b a) c -> p b a c", b=2), s.rows1[:, 0:2, :].rearrange("p a (b c) -> p b a c", b=2))
                        o = ve.tensor_copy(s.rhs[:, :, 64:P], b[:, 2, 0:256].rearrange("p (h c) -> p h c", h=4))
                    elif t in (4, 5, 6, 8):
                        ve.tensor_tensor(s.X[:], s.X[:], heads(b[:, 2, :]), ALU.add)
                        o = ve.tensor_tensor(s.XT[:], s.XT[:], heads(b[:, 3, :]), ALU.add)
                    elif t == 10:
                        o = ve.tensor_tensor(s.XT[:], s.XT[:], heads(b[:, 3, :]), ALU.add)
                    elif t == 12:
                        i, end = tile_of(d, n), CHUNK - 1 if d == 0 else 0
                        bd = g.pair[:].unsqueeze(1).to_broadcast([P, H4, P])
                        half = lambda x: b[:, 2:4, x * 2 * P:(x + 1) * 2 * P].rearrange("p c (a k) -> p c a k", a=2)
                        cp = lambda x: x.rearrange("p (c a) k -> p c a k", c=2)
                        step(ve.tensor_tensor(cp(s.Phi[:]), half(0), cp(bd), ALU.mult))
                        ve.tensor_tensor(cp(s.Psi[:]), half(1), cp(bd), ALU.mult)
                        for c in range(2):
                            for p in range(2):
                                x = i * P + c * CHUNK + end
                                ve.scalar_tensor_tensor(out=s.Phi[:, 2 * c + p, :], in0=g.ident[:], scalar=g.eL[:, d, p, x:x + 1], in1=s.Phi[:, 2 * c + p, :],
                                                        op0=ALU.mult, op1=ALU.add)
                        o = ve.tensor_tensor(s.QT[:], s.AR[:, :, 1, :], b[:, 0, 0:2 * P].rearrange("p (a c) -> p a c", a=2), ALU.add)
                    elif t >= 13:
                        c = (t - 13) if d == 0 else (14 - t)
                        x = tile_of(d, n) * P + c * CHUNK
                        y = g.S[:, Y_AT[d]:Y_AT[d] + 2, x:x + CHUNK]
                        if t == 13:
                            ve.wait_ge(s.ac, n * STEPS + 12)
                        ve.tensor_tensor(y, y, b[:, 0, 0:P].rearrange("p (a c) -> p a c", a=2), ALU.add)
                        o = ve.tensor_tensor(s.S[:], s.Psi[:, 2 * c:2 * c + 2, :], b[:, 1, 0:2 * P].rearrange("p (a c) -> p a c", a=2), ALU.add)
                    else:
                        ve.sem_inc(s.ve, 1)
                        return
                    o.then_inc(s.ve, 1)

                operands(0, 0)
                operands(0, 1)
                for n in range(TILES):
                    for t in range(1, STEPS + 1):
                        for d in range(2):
                            evacuate(n, t, d)
                            if t == 13 and n + 1 < TILES:
                                operands(n + 1, d)


def stage_rwkv_output(nc, g, l):
    with ExitStack() as st:
        sem = g.sems.begin(st)
        sb = lambda name, shape: st.enter_context(nc.sbuf_tensor(g.name(name), shape, F32))
        gup, y, sq, t = sb("g_up", [P, RW_W]), sb("y_sum", [P, 2, TOK]), sb("y_sq", [P, 2, TOK]), sb("rk", [P, 2, TOK])
        ps = st.enter_context(nc.psum_tensor(g.name("gn_ps"), [P, 8, BANK], F32))
        w_in, v_done, y_done, mu_in, t_done, bonus_in, sq_done, var_in, eps_done, root_done, gate_in = (
            sem(n) for n in ("w_in", "v_done", "y_done", "mean_in", "rk_done", "bonus_in", "sq_done", "var_in", "eps_done", "root_done", "gate_in"))
        par = lambda name, k: g.par[:, l, ROWS[name] + k:ROWS[name] + k + 1]
        Y = lambda d: g.S[:, Y_AT[d]:Y_AT[d] + 2, :]
        KDc = lambda d: g.S[:, KD_AT[d]:KD_AT[d] + 2, :]

        with nc.Block() as block:
            @block.sync
            def _(sp):
                sp.dma_start(gup[:], g.dram["rw_g_up"][l]).then_inc(w_in, 16)

            @block.gpsimd
            def _(po):
                po.sem_clear(g.sems.other)

            @block.tensor
            def _(pe):
                def sums(first, src, done):
                    for p in range(2):
                        mm = pe.matmul(ps[:, first + p, :], g.pair[:], src[:, p, :], start=True, stop=True)
                    mm.then_inc(done, 1)
                pe.wait_ge(y_done, 1)
                sums(0, y, mu_in)
                pe.wait_ge(t_done, 1)
                sums(2, t, bonus_in)
                pe.wait_ge(w_in, 16)
                for p in range(2):
                    mm = pe.matmul(ps[:, 6 + p, :], gup[:, p * P:(p + 1) * P], g.S[:, LORA0 + 2, :], start=True, stop=True)
                mm.then_inc(gate_in, 1)
                pe.wait_ge(sq_done, 1)
                sums(4, sq, var_in)

            @block.scalar
            def _(ac):
                ac.wait_ge(eps_done, 1)
                ac.activation(sq[:], sq[:], ACT.Sqrt).then_inc(root_done, 1)

            @block.vector
            def _(ve):
                step = chained(ve, v_done)
                ve.tensor_tensor(y[:], Y(0), Y(1), ALU.add).then_inc(y_done, 1)
                step(ve.tensor_tensor(t[:], KDc(0), KDc(1), ALU.add))
                for p in range(2):
                    o = ve.scalar_tensor_tensor(out=t[:, p, :], in0=t[:, p, :], scalar=par("rw_r_k", p), in1=g.S[:, RR + p, :], op0=ALU.mult, op1=ALU.mult)
                o.then_inc(t_done, 1)
                ve.wait_ge(mu_in, 1)
                step(ve.scalar_tensor_tensor(out=y[:], in0=ps[:, 0:2, :], scalar=-1.0 / RW_HD, in1=y[:], op0=ALU.mult, op1=ALU.add))
                ve.tensor_tensor(sq[:], y[:], y[:], ALU.mult).then_inc(sq_done, 1)
                ve.wait_ge(bonus_in, 1)
                step(ve.tensor_tensor(t[:], ps[:, 2:4, :], g.S[:, VC:VC + 2, :], ALU.mult))
                ve.wait_ge(var_in, 1)
                ve.tensor_scalar(sq[:], ps[:, 4:6, :], 1.0 / RW_HD, RW_HD * 1e-5, ALU.mult, ALU.add).then_inc(eps_done, 1)
                ve.wait_ge(root_done, 1)
                step(ve.reciprocal(sq[:], sq[:]))
                step(ve.tensor_tensor(y[:], y[:], sq[:], ALU.mult))
                for p in range(2):
                    step(ve.tensor_scalar(y[:, p, :], y[:, p, :], par("rw_ln_w", p), par("rw_ln_b", p), ALU.mult, ALU.add))
                step(ve.tensor_tensor(y[:], y[:], t[:], ALU.add))
                ve.wait_ge(gate_in, 1)
                step(ve.tensor_tensor(g.mix[:, 2:4, :], y[:], ps[:, 6:8, :], ALU.mult))


def stream_of(i):
    return 0 if i >= 2 else 1


def broadcast_gate(pe, g, ps, part, w):
    row = 2 * part + w
    for j in range(2):
        mm = pe.matmul(ps[:, j, :], g.ident[0:12, row:row + 1].to_broadcast([12, P]), g.mod[:, j * BANK:(j + 1) * BANK], start=True, stop=True)
    return mm


def stage_output_projection(nc, g, l, tiles):
    with ExitStack() as st:
        sem = g.sems.begin(st)
        w = st.enter_context(nc.sbuf_tensor(g.name("w_out"), [P, KD, D], F32))
        gate = st.enter_context(nc.sbuf_tensor(g.name("gate1"), [P, 2, D], F32))
        t = st.enter_context(nc.sbuf_tensor(g.name("gated"), [P, D], F32))
        gps = st.enter_context(nc.psum_tensor(g.name("gate_ps"), [P, 2, BANK], F32))
        ps = st.enter_context(nc.psum_tensor(g.name("mixed_ps"), [P, 2, 2, BANK], F32))
        landed, gate_in, gate_out, mm_done, used, v_done = (sem(n) for n in ("w_out_landed", "gate_in", "gate_out", "mm_done", "used", "v_done"))
        halves = [sem(f"w_out_half{k}") for k in range(4)]
        wv = g.dram["w_out"][l].rearrange("(k p) n -> p k n", p=P)

        with nc.Block() as block:
            @block.sync
            def _(sp):
                for q in range(4):
                    sp.dma_start(w[:, 2 * q:2 * q + 2, :], wv[:, 2 * q:2 * q + 2, :]).then_inc(halves[q], 16)

            @block.gpsimd
            def _(po):
                po.sem_clear(g.sems.other)

            @block.tensor
            def _(pe):
                for w_ in range(2):
                    if w_:
                        pe.wait_ge(gate_out, 1)
                    broadcast_gate(pe, g, gps, 2, w_).then_inc(gate_in, 1)
                for n, i in enumerate(tiles):
                    if n >= 2:
                        pe.wait_ge(used, n - 1)
                    for k in range(KD):
                        if n == 0:
                            pe.wait_ge(halves[k // 2], 16)
                        for j in range(2):
                            mm = pe.matmul(ps[:, n % 2, j, :], g.mix[:, k, i * P:(i + 1) * P], w[:, k, j * BANK:(j + 1) * BANK], start=k == 0, stop=k == KD - 1)
                    mm.then_inc(mm_done, 1)

            @block.scalar
            def _(ac):
                for w_ in range(2):
                    ac.wait_ge(gate_in, w_ + 1)
                    ac.activation(gate[:, w_, :], gps[:].rearrange("p a b -> p (a b)"), ACT.Copy).then_inc(gate_out, 1)

            @block.vector
            def _(ve):
                step = chained(ve, v_done)
                ve.wait_ge(gate_out, 2)
                for n, i in enumerate(tiles):
                    ve.wait_ge(mm_done, n + 1)
                    o = ve.tensor_tensor(t[:], ps[:, n % 2, :, :].rearrange("p a b -> p (a b)"), gate[:, stream_of(i), :], ALU.mult)
                    o.then_inc(used, 1)
                    ve.wait_ge(used, n + 1)
                    step(ve.tensor_tensor(g.X[:, i, :], g.X[:, i, :], t[:], ALU.add))


def stage_peer_queries(nc, g, l, tiles, HT, QT, KT):
    CW, WB = 2, 3
    NT = HEADS * DQ // P
    T0 = tiles[0] * P
    with ExitStack() as st:
        sem = g.sems.begin(st)
        w = st.enter_context(nc.sbuf_tensor(g.name("wq_ring"), [P, WB, KD, CW * P], F32))
        kr = st.enter_context(nc.sbuf_tensor(g.name("key_rows"), [P, 2, HEADS, P], F32))
        ps = st.enter_context(nc.psum_tensor(g.name("q_ps"), [P, 4, BANK], F32))
        kps = st.enter_context(nc.psum_tensor(g.name("key_ps"), [P, 4, BANK], F32))
        landed = [sem(f"wq_landed{b}") for b in range(WB)]
        keys_in, key_tp, key_out, mm_done, evac = (sem(n) for n in ("keys_in", "keys_transposed", "keys_out", "mm_done", "evacuated"))
        wv = g.dram["peer_wq"][l].rearrange("(k p) n -> p k n", p=P)

        with nc.Block() as block:
            @block.sync
            def _(sp):
                for s, name in enumerate(("peer_k1", "peer_k2")):
                    sp.dma_start(kr[:, s, :, :], g.dram[name][l].rearrange("h n d -> n h d")).then_inc(keys_in, 16)
                for n in range(NT // CW):
                    if n >= WB:
                        sp.wait_ge(mm_done, (n - WB + 1) * CW)
                    sp.dma_start(w[:, n % WB, :, :], wv[:, :, n * CW * P:(n + 1) * CW * P]).then_inc(landed[n % WB], 16)

            @block.gpsimd
            def _(po):
                po.sem_clear(g.sems.other)

            @block.tensor
            def _(pe):
                pe.wait_ge(keys_in, 32)
                for c in range(NT):
                    mm = pe.transpose(kps[:, c // 4, (c % 4) * P:(c % 4 + 1) * P], kr[:, c % 2, c // 2, :], g.ident[:])
                    if c % 4 == 3:
                        mm.then_inc(key_tp, 1)
                for j in range(NT):
                    n = j // CW
                    pe.wait_ge(landed[n % WB], 16 * (n // WB + 1))
                    if j >= 4:
                        pe.wait_ge(evac, j - 3)
                    for k in range(KD):
                        mm = pe.matmul(ps[:, j % 4, 0:TOK - T0], w[:, n % WB, k, (j % CW) * P:(j % CW + 1) * P], HT[:, k, T0:TOK], start=k == 0, stop=k == KD - 1)
                    mm.then_inc(mm_done, 1)

            @block.scalar
            def _(ac):
                for j in range(NT):
                    ac.wait_ge(mm_done, j + 1)
                    ac.activation(QT[:, j, T0:TOK], ps[:, j % 4, 0:TOK - T0], ACT.Copy).then_inc(evac, 1)

            @block.vector
            def _(ve):
                for c in range(4):
                    ve.wait_ge(key_tp, c + 1)
                    ve.tensor_copy(KT[:, 4 * c:4 * c + 4, :], kps[:, c, :].rearrange("p (a b) -> p a b", a=4)).then_inc(key_out, 1)


def stage_peer_select(nc, g, l, tiles, QT, KT, gates, experts):
    HH = 2 * HEADS
    with ExitStack() as st:
        sem = g.sems.begin(st)
        sb = lambda name, shape, dt=F32: st.enter_context(nc.sbuf_tensor(g.name(name), shape, dt))
        sc = sb("scores", [P, 2, HH, P])
        val, idx_u, idx = sb("half_vals", [P, HH, 16]), sb("half_idx_u", [P, HH, 16], U32), sb("half_idx", [P, HH, 16])
        cand = sb("cand", [P, HEADS, 256])
        top, pos, part_u, part = sb("top_vals", [P, HEADS, 16]), sb("top_pos", [P, SLOTS], U32), sb("pos_part_u", [P, 2, SLOTS], U32), sb("pos_part", [P, 2, SLOTS])
        hot, found = sb("one_hot", [P, SLOTS, 16]), sb("found", [P, 2, SLOTS])
        total = sb("gate_sum", [P, HEADS])
        ps = st.enter_context(nc.psum_tensor(g.name("score_ps"), [P, 2, 4, BANK], F32))
        s_in, s_out, v_done, shifted, exped = (sem(n) for n in ("scores_in", "scores_out", "v_done", "shifted", "exped"))
        sc_used = sem("scores_used")

        with nc.Block() as block:
            @block.gpsimd
            def _(po):
                po.sem_clear(g.sems.other)

            @block.tensor
            def _(pe):
                for n, i in enumerate(tiles):
                    if n >= 2:
                        pe.wait_ge(s_out, n - 1)
                    for c in range(HH):
                        mm = pe.matmul(ps[:, n % 2, c // 4, (c % 4) * P:(c % 4 + 1) * P], QT[:, c, i * P:(i + 1) * P], KT[:, c, :], start=True, stop=True)
                    mm.then_inc(s_in, 1)

            @block.scalar
            def _(ac):
                for n, i in enumerate(tiles):
                    ac.wait_ge(s_in, n + 1)
                    if n >= 2:
                        ac.wait_ge(sc_used, n - 1)
                    for q in range(4):
                        a = ac.activation(sc[:, n % 2, 4 * q:4 * q + 4, :], ps[:, n % 2, q, :].rearrange("p (a b) -> p a b", a=4), ACT.Copy)
                    a.then_inc(s_out, 1)
                    ac.wait_ge(shifted, n + 1)
                    ac.activation(gates[:, i, :], gates[:, i, :], ACT.Exp).then_inc(exped, 1)

            @block.vector
            def _(ve):
                step = chained(ve, v_done)

                def top16(src, vals, where):
                    step(ve.max(vals[:, 0:8], src))
                    step(ve.max_index(where[:, 0:8], vals[:, 0:8], src))
                    step(ve.match_replace(src, vals[:, 0:8], src, -3.0e38))
                    step(ve.max(vals[:, 8:16], src))
                    step(ve.max_index(where[:, 8:16], vals[:, 8:16], src))

                for n, i in enumerate(tiles):
                    ve.wait_ge(s_out, n + 1)
                    for c in range(HH):
                        top16(sc[:, n % 2, c, :], val[:, c, :], idx_u[:, c, :])
                    ve.sem_inc(sc_used, 1)
                    step(ve.tensor_copy(idx[:], idx_u[:]))
                    halves = val[:].rearrange("p (h s) k -> p h s k", s=2)
                    step(ve.tensor_tensor(cand[:].rearrange("p h (a b) -> p h a b", a=16), halves[:, :, 0, :].unsqueeze(3).to_broadcast([P, HEADS, 16, 16]),
                                          halves[:, :, 1, :].unsqueeze(2).to_broadcast([P, HEADS, 16, 16]), ALU.add))
                    for h in range(HEADS):
                        top16(cand[:, h, :], top[:, h, :], pos[:, h * 16:h * 16 + 16])
                    gt = gates[:, i, :].rearrange("p (h k) -> p h k", h=HEADS)
                    ve.tensor_tensor(gt, top[:], top[:, :, 0:1].to_broadcast([P, HEADS, 16]), ALU.subtract).then_inc(shifted, 1)
                    step(ve.tensor_scalar(part_u[:, 0, :], pos[:], 4, None, ALU.logical_shift_right))
                    step(ve.tensor_scalar(part_u[:, 1, :], pos[:], 15, None, ALU.bitwise_and))
                    step(ve.tensor_copy(part[:], part_u[:]))
                    lists = idx[:].rearrange("p (h s) k -> p h s k", s=2)
                    for s in range(2):
                        step(ve.tensor_tensor(hot[:], g.iota[:].unsqueeze(1).to_broadcast([P, SLOTS, 16]), part[:, s, :].unsqueeze(2).to_broadcast([P, SLOTS, 16]), ALU.is_equal))
                        h4 = hot[:].rearrange("p (h k) j -> p h k j", h=HEADS)
                        step(ve.tensor_tensor(h4, h4, lists[:, :, s, :].unsqueeze(2).to_broadcast([P, HEADS, 16, 16]), ALU.mult))
                        step(ve.tensor_reduce(found[:, s, :], hot[:], AX.X, ALU.add))
                    step(ve.tensor_scalar(found[:, 0, :], found[:, 0, :], float(NKEYS), float(l * NEXP), ALU.mult, ALU.add))
                    step(ve.tensor_tensor(experts[:, i, :], found[:, 0, :], found[:, 1, :], ALU.add))
                    ve.wait_ge(exped, n + 1)
                    step(ve.tensor_reduce(total[:], gt, AX.X, ALU.add))
                    step(ve.reciprocal(total[:], total[:]))
                    step(ve.tensor_tensor(gt, gt, total[:].unsqueeze(2).to_broadcast([P, HEADS, 16]), ALU.mult))


def stage_peer_experts(nc, g, l, tiles, H, gates, experts):
    T0, N = tiles[0], len(tiles)
    with ExitStack() as st:
        sem = g.sems.begin(st)
        sb = lambda name, shape, dt=F32: st.enter_context(nc.sbuf_tensor(g.name(name), shape, dt))
        ring, rows = sb("expert_rows", [P, RING, D]), sb("row_numbers", [P, 2, RING], U32)
        hcur, dots8, dots = sb("h_current", [P, D]), sb("dots8", [P, RING]), sb("dots", [P, SLOTS])
        weight, diag = sb("weight", [P, SLOTS]), sb("diag", [P, RING, P])
        gate = sb("gate2", [P, 2, D])
        acc = st.enter_context(nc.psum_tensor(g.name("expert_sum"), [P, 2, BANK], F32))
        gps = st.enter_context(nc.psum_tensor(g.name("gate2_ps"), [P, 2, 2, BANK], F32))
        landed, before = g.rows_landed, g.rows_used
        g.rows_used += 2 * N * GROUPS
        free = [sem(f"free{b}") for b in range(RING)]
        rows_copied, issued, h_copied, v_go = sem("rows_copied"), sem("issued"), sem("h_copied"), sem("v_go")
        dots_kept, gelu_done, weight_done, diag_done, acc_out, pe_go = (sem(n) for n in ("dots_kept", "gelu_done", "weight_done", "diag_done", "acc_out", "pe_go"))
        gate_in, gate_out, v_done = sem("gate_in"), sem("gate_out"), sem("v_done")
        table = {0: g.dram["peer_u"].rearrange("l n d -> (l n) d"), 1: g.dram["peer_v"].rearrange("l n d -> (l n) d")}
        flat = lambda t: t.rearrange("p a b -> p (a b)")
        row_list, gate_list = flat(experts[:]), flat(gates[:])

        with nc.Block() as block:
            @block.gpsimd
            def _(po):
                po.sem_clear(g.sems.other)
                for b in range(RING):
                    po.sem_inc(free[b], 2)
                with po.Fori(0, N) as c:
                    for half in range(2):
                        with po.Fori(0, GROUPS // 2) as pair:
                            for side in range(2):
                                k = pair * 2 + side
                                use = (c * 2 + half) * GROUPS + k
                                for b in range(RING):
                                    po.wait_ge(free[b], use + 1)
                                    po.sem_inc(issued, 1)
                                po.tensor_copy(rows[:, side, :], row_list[:, bass.ds((c + T0) * SLOTS + k * RING, RING)]).then_inc(rows_copied, 1)
                                po.wait_ge(rows_copied, use + 1)
                                po.sem_inc(issued, 1)
                                for b in range(RING):
                                    po.wait_ge(free[b], use + 2)
                                    po.sem_inc(issued, 1)
                                    po.indirect_dma_start(out=ring[:, b, :], out_offset=None, in_=table[half],
                                                          in_offset=bass.IndirectOffsetOnAxis(ap=rows[:, side, b:b + 1], axis=0)).then_inc(landed[b], 16)

            @block.vector
            def _(ve):
                step = chained(ve, v_done)
                ve.sem_inc(acc_out, 1)
                with ve.Fori(0, N) as c:
                    ve.tensor_copy(hcur[:], H[:, bass.ds(c + T0, 1), :].rearrange("p a d -> p (a d)")).then_inc(h_copied, 1)
                    ve.wait_ge(h_copied, c + 1)
                    ve.sem_inc(v_go, 1)
                    with ve.Fori(0, GROUPS) as k:
                        use = c * 2 * GROUPS + k
                        for b in range(RING):
                            ve.wait_ge(landed[b], 16 * (use + before + 1))
                            ve.tensor_tensor_reduce(ring[:, b, :], ring[:, b, :], hcur[:], 1.0, 0.0, ALU.mult, ALU.add, dots8[:, b:b + 1]).then_inc(free[b], 1)
                        ve.wait_ge(free[RING - 1], use + 3)
                        ve.sem_inc(v_go, 1)
                        ve.tensor_copy(dots[:, bass.ds(k * RING, RING)], dots8[:]).then_inc(dots_kept, 1)
                        ve.wait_ge(dots_kept, c * GROUPS + k + 1)
                        ve.sem_inc(v_go, 1)
                    ve.wait_ge(gelu_done, c + 1)
                    ve.tensor_tensor(weight[:], dots[:], gate_list[:, bass.ds((c + T0) * SLOTS, SLOTS)], ALU.mult).then_inc(weight_done, 1)
                    ve.wait_ge(free[RING - 1], (2 * c + 2) * GROUPS + 2)
                    ve.sem_inc(v_go, 1)
                    ve.tensor_copy(H[:, bass.ds(c + T0, 1), :].rearrange("p a d -> p (a d)"), flat(acc[:])).then_inc(acc_out, 1)
                ve.wait_ge(acc_out, N + 1)
                ve.wait_ge(gate_out, 2)
                for i in tiles:
                    step(ve.tensor_tensor(H[:, i, :], H[:, i, :], gate[:, stream_of(i), :], ALU.mult))
                    step(ve.tensor_tensor(g.X[:, i, :], g.X[:, i, :], H[:, i, :], ALU.add))

            @block.scalar
            def _(ac):
                for w in range(2):
                    ac.wait_ge(gate_in, w + 1)
                    ac.activation(gate[:, w, :], flat(gps[:, w, :, :]), ACT.Copy).then_inc(gate_out, 1)
                with ac.Fori(0, N) as c:
                    ac.wait_ge(dots_kept, (c + 1) * GROUPS)
                    ac.activation(dots[:], dots[:], ACT.Gelu).then_inc(gelu_done, 1)
                    ac.wait_ge(weight_done, c + 1)
                    with ac.Fori(0, GROUPS) as k:
                        for b in range(RING):
                            ac.wait_ge(free[b], (2 * c + 1) * GROUPS + k + 2)
                            ac.activation(diag[:, b, :], g.ident[:], ACT.Copy, scale=weight[:, bass.ds(k * RING + b, 1)]).then_inc(diag_done, 1)

            @block.tensor
            def _(pe):
                for w in range(2):
                    broadcast_gate(pe, g, gps[:, w, :, :], 5, w).then_inc(gate_in, 1)

                def group(c, k, first, last):
                    use = (c * 2 + 1) * GROUPS + k
                    for b in range(RING):
                        pe.wait_ge(landed[b], 16 * (use + before + 1))
                        pe.wait_ge(diag_done, (c * GROUPS + k) * RING + b + 1)
                        for j in range(2):
                            mm = pe.matmul(acc[:, j, :], diag[:, b, :], ring[:, b, j * BANK:(j + 1) * BANK], start=first and b == 0, stop=last and b == RING - 1)
                        mm.then_inc(free[b], 1)
                with pe.Fori(0, N) as c:
                    pe.wait_ge(acc_out, c + 1)
                    pe.sem_inc(pe_go, 1)
                    group(c, 0, True, False)
                    with pe.Fori(1, GROUPS - 1) as k:
                        group(c, k, False, False)
                    group(c, GROUPS - 1, False, True)


def stage_final_norm(nc, g, out):
    with ExitStack() as st:
        sem = g.sems.begin(st)
        sb = lambda name, shape: st.enter_context(nc.sbuf_tensor(g.name(name), shape, F32))
        gain, sq, ms, y = sb("final_gain", [P, D]), sb("squares", [P, 2, D]), sb("mean_square", [P, 2]), sb("y", [P, 2, D])
        gain_in, ms_done, eps_done, root_done, v_done, y_done = (sem(n) for n in ("gain_in", "ms_done", "eps_done", "root_done", "v_done", "y_done"))
        rows = out[0].rearrange("(i p) d -> i p d", p=P)

        with nc.Block() as block:
            @block.sync
            def _(sp):
                sp.dma_start(gain[:], g.dram["final_g"].rearrange("(a n) -> a n", a=1).to_broadcast([P, D])).then_inc(gain_in, 16)
                for i in range(2):
                    sp.wait_ge(y_done, i + 1)
                    sp.dma_start(rows[i], y[:, i, :]).then_inc(g.stored, 16)
                sp.wait_ge(g.stored, 32)

            @block.scalar
            def _(ac):
                for i in range(2):
                    ac.activation(sq[:, i, :], g.X[:, 2 + i, :], ACT.Square, scale=float(D) ** -0.5, accum_out=ms[:, i:i + 1]).then_inc(ms_done, 1)
                ac.wait_ge(eps_done, 1)
                ac.activation(ms[:], ms[:], ACT.Sqrt).then_inc(root_done, 1)

            @block.vector
            def _(ve):
                step = chained(ve, v_done)
                ve.wait_ge(ms_done, 2)
                ve.tensor_scalar(ms[:], ms[:], 1e-6, None, ALU.add).then_inc(eps_done, 1)
                ve.wait_ge(root_done, 1)
                step(ve.reciprocal(ms[:], ms[:]))
                ve.wait_ge(gain_in, 16)
                for i in range(2):
                    ve.scalar_tensor_tensor(out=y[:, i, :], in0=g.X[:, 2 + i, :], scalar=ms[:, i:i + 1], in1=gain[:], op0=ALU.mult, op1=ALU.mult).then_inc(y_done, 1)


def program(nc, dram, out):
    with ExitStack() as st:
        g = Shared()
        g.rows_landed, g.rows_used = [st.enter_context(nc.semaphore(f"expert_rows_landed{b}")) for b in range(RING)], 0
        g.dram, g.stored, g.sems = dram, st.enter_context(nc.semaphore("output_stored")), Semaphores(nc)
        sb = lambda name, shape, dt=F32: st.enter_context(nc.sbuf_tensor(g.name(name), shape, dt))
        g.X = sb("X", [P, TILES, D])
        g.mod = sb("mod", [12, D])
        g.par = sb("par", [P, DEPTH, P])
        g.omka = sb("one_minus_k_a", [P, DEPTH, 2])
        g.cond = sb("cond", [P, KD, 2])
        g.ident, g.pair, g.rot, g.swap = (sb(n, [P, P]) for n in ("ident", "pair", "rot", "swap"))
        g.rope = sb("rope", [P, 2, SEQ])
        g.band = sb("band", [P, 2, 2 * SEQ])
        g.ones = sb("ones", [P, P])
        g.masks = sb("masks", [P, 10, P])
        g.iota = sb("iota", [P, 16])
        g.sink = sb("sink", [P, DEPTH, AT_HQ])
        g.sink8 = sb("sink8", [P, DEPTH, AT_HQ])
        stage_constants(nc, g)
        for l in range(DEPTH):
            done = [2, 3] if l == DEPTH - 1 else [0, 1, 2, 3]
            stage_modulation(nc, g, l)
            with ExitStack() as mixer:
                keep = lambda name, shape, dt=F32: mixer.enter_context(nc.sbuf_tensor(g.name(name), shape, dt))
                g.S = keep("S", [P, IN_TILES, TOK])
                with ExitStack() as front:
                    HT = front.enter_context(nc.sbuf_tensor(g.name("HT"), [P, KD, TOK], F32))
                    stage_norm(nc, g, [0, 1, 2, 3], 0, None, HT)
                    stage_input_projection(nc, g, l, HT)
                g.mix = keep("mix", [P, KD, TOK])
                stage_hyena(nc, g, l)
                stage_attention(nc, g, l, done)
                with ExitStack() as rwkv:
                    g.eL, g.eN, g.eP = (rwkv.enter_context(nc.sbuf_tensor(g.name(n), [P, 2, 2, TOK], F32)) for n in ("decay_in", "decay_out", "decay_before"))
                    stage_rwkv_operands(nc, g, l)
                    stage_rwkv_chunks(nc, g, l)
                    stage_rwkv_output(nc, g, l)
                stage_output_projection(nc, g, l, done)
            with ExitStack() as peer:
                keep = lambda name, shape, dt=F32: peer.enter_context(nc.sbuf_tensor(g.name(name), shape, dt))
                H, gates, experts = keep("H", [P, TILES, D]), keep("gates", [P, TILES, SLOTS]), keep("experts", [P, TILES, SLOTS], U32)
                with ExitStack() as front:
                    keep = lambda name, shape: front.enter_context(nc.sbuf_tensor(g.name(name), shape, F32))
                    QT, KT = keep("QT", [P, 2 * HEADS, TOK]), keep("KT", [P, 2 * HEADS, P])
                    with ExitStack() as columns:
                        HT = columns.enter_context(nc.sbuf_tensor(g.name("HT2"), [P, KD, TOK], F32))
                        stage_norm(nc, g, done, 3, H, HT)
                        stage_peer_queries(nc, g, l, done, HT, QT, KT)
                    stage_peer_select(nc, g, l, done, QT, KT, gates, experts)
                stage_peer_experts(nc, g, l, done, H, gates, experts)
        stage_final_norm(nc, g, out)


_INS = ['x', 'c', 'ctx', 'c_ctx', 'mod_w', 'mod_b', 'norm1_g', 'norm2_g', 'w_in', 'conv_w', 'conv_b', 'hy_w1', 'hy_b1',
        'hy_w2', 'hy_b2', 'hy_w3', 'hy_b3', 'hy_freq', 'hy_bias', 'rw_w0', 'rw_w_up', 'rw_a0', 'rw_a_up', 'rw_g_up',
        'rw_k_k', 'rw_k_a', 'rw_r_k', 'rw_ln_w', 'rw_ln_b', 'attn_sink', 'hy_out_g', 'at_out_g', 'w_out', 'peer_wq',
        'peer_k1', 'peer_k2', 'peer_u', 'peer_v', 'final_g']
_OUT = (1, SEQ, D)


def kernel(**inputs):
    import numpy as _np
    import concourse.bacc as _bacc
    from concourse import mybir as _mybir
    from concourse.bass_utils import run_bass_kernel_spmd as _run

    nc = _bacc.Bacc("TRN2", target_bir_lowering=False, num_devices=1)
    arrays, dram = {}, {}
    for name in _INS:
        arrays[f"in_{name}"] = _np.ascontiguousarray(inputs[name])
    for name, a in host_constants().items():
        arrays[f"in_{name}"] = a
    for name, a in arrays.items():
        dram[name[3:]] = nc.dram_tensor(name, a.shape, _mybir.dt.from_np(a.dtype), kind="ExternalInput").ap()
    out = nc.dram_tensor("out_0", _OUT, _mybir.dt.float32, kind="ExternalOutput").ap()
    program(nc, dram, out)
    r = _run(nc, [arrays], core_ids=[0])
    return r.results[0]["out_0"]
```

```python
from contextlib import ExitStack

import numpy as np

import concourse.bass as bass
from concourse import mybir

F32 = mybir.dt.float32
U32 = mybir.dt.uint32
I32 = mybir.dt.int32
ALU = mybir.AluOpType
ACT = mybir.ActivationFunctionType
AX = mybir.AxisListType

P = 128
D = 1024
DEPTH = 2
SEQ = 256
TOK = 2 * SEQ
TILES = TOK // P
KD = D // P
BANK = 512

HY_CH, HY_EMB, HY_HID = 256, 33, 64
RW_W, RW_HD = 256, 64
AT_HQ, AT_HD, AT_W = 8, 64, 512
IN_W = 2688
IN_TILES = IN_W // P
CONV_TILES = 12
LORA0, Q0, K0, V0 = 12, 15, 19, 20
CHUNK = 64
NCHUNK = TOK // CHUNK
DECAY = float(np.exp(-0.5))
HEADS, NKEYS, TOPK, DQ = 8, 128, 16, 256
NEXP = NKEYS * NKEYS
SLOTS = HEADS * TOPK
RING = 8
GROUPS = SLOTS // RING
BY_PE = 6
BIG = 1e30
TWO_PI = 2.0 * float(np.pi)
PI_BELOW = 3.1415925

ROWS = {}
_n = 0
for _name, _count in (("conv_w", 36), ("conv_b", 12), ("rw_w0", 4), ("rw_a0", 4), ("rw_k_k", 2), ("rw_k_a", 2),
                      ("rw_r_k", 2), ("rw_ln_w", 2), ("rw_ln_b", 2), ("hy_bias", 2), ("hy_out_g", 2),
                      ("at_out_g", 4), ("hy_b1", 1), ("hy_b2", 1), ("hy_freq", 2)):
    ROWS[_name] = _n
    _n += _count
NROWS = _n


def host_constants():
    f = np.float64
    j = np.arange(SEQ, dtype=f)
    t32 = np.arange(SEQ, dtype=np.float32) / np.float32(SEQ - 1)
    bands = np.linspace(1e-4, (HY_EMB - 1) // 2 - 1, (HY_EMB - 1) // 2, dtype=np.float32)
    ang = (np.float32(TWO_PI) * np.arange(SEQ, dtype=np.float32)[:, None] * bands[None, :] / np.float32(SEQ)).astype(f)
    emb = np.concatenate([t32[:, None].astype(f), np.cos(ang), -np.sin(ang)], axis=1).T
    deltas = np.abs(np.linspace(np.log(1e-2) / 1.5, np.log(1e-2) / 0.3, HY_CH, dtype=np.float32)).astype(f)
    window = np.exp(-t32.astype(f)[:, None] * deltas[None, :]) + 0.05
    w = (np.arange(SEQ, dtype=f) + 0.5) * TWO_PI / (2 * SEQ)
    cos, sin = np.cos(j[:, None] * w[None, :]), np.sin(j[:, None] * w[None, :])
    two_sided = np.stack([window, np.where(j[:, None] == 0, 0.0, window)], axis=1)
    tiles = lambda m: m.reshape(2, P, SEQ).transpose(1, 0, 2)
    dft = np.stack([tiles(cos), tiles(sin), tiles(cos.T / SEQ), tiles(sin.T / SEQ)], axis=1)
    t, s = np.meshgrid(np.arange(P), np.arange(P), indexing="ij")
    same = lambda n: (t // n) == (s // n)
    low = (s < t) & same(64)
    masks = [low & same(16), low & same(32) & ~same(16), low & ~same(32), low, (s <= t) & same(64)]
    masks = np.stack([m for m in masks] + [m.T for m in masks], axis=1).astype(f)
    head_pair = (t // 64 == s // 64).astype(f)
    d = np.arange(P) % 64
    inv = (10000.0 ** (-np.arange(16, dtype=np.float32) / np.float32(16))).astype(f)[d % 16]
    pos = np.where((d < 32)[:, None], (np.arange(SEQ) // 64)[None, :], (np.arange(SEQ) % 64)[None, :])
    rope = np.stack([np.cos(pos * inv[:, None]), np.sin(pos * inv[:, None])], axis=1)
    rot = np.zeros((P, P), f)
    for m in range(P):
        rot[m + 16 if m % 32 < 16 else m - 16, m] = -1.0 if m % 32 < 16 else 1.0
    swap = np.zeros((P, P), f)
    swap[(np.arange(P) + 64) % P, np.arange(P)] = 1.0
    q, k = np.arange(SEQ).reshape(2, P), np.arange(SEQ)
    band = np.where(np.abs(q[:, :, None] - k[None, None, :]) <= 128, 0.0, -BIG).transpose(1, 0, 2)
    band = np.concatenate([np.zeros_like(band), band], axis=2)
    one = np.zeros((8, 2), f)
    one[2:4, 0], one[4:6, 1] = 1.0, 1.0
    iota16 = np.tile(np.arange(16, dtype=f), (P, 1))
    out = dict(k_emb=emb, k_window=two_sided.reshape(2, P, 2 * HY_CH).transpose(1, 0, 2), k_dft=dft, k_masks=masks,
               k_pair=head_pair, k_rope=rope, k_rot=rot, k_swap=swap, k_band=band, k_iota=iota16, k_one=one,
               k_ident=np.eye(P))
    return {n: np.ascontiguousarray(a.astype(np.float32)) for n, a in out.items()}


class Semaphores:

    def __init__(self, nc, per_bank=70):
        self.nc, self.turn = nc, 0
        first = min(nc.free_semaphores)
        self.banks = [range(first, first + per_bank), range(first + per_bank, first + 2 * per_bank)]

    def begin(self, stack):
        mine, self.other = self.banks[self.turn], self.banks[1 - self.turn]
        self.turn = 1 - self.turn
        nums = iter(mine)

        def sem(name):
            s = self.nc.alloc_semaphore(name, num=next(nums))
            stack.callback(self.nc.release_semaphore, s)
            return s
        return sem


def chained(eng, done):
    count = [0]

    def step(instruction):
        count[0] += 1
        instruction.then_inc(done, 1)
        eng.wait_ge(done, count[0])
    return step


class Shared:

    def __init__(self):
        self.uses = {}

    def name(self, base):
        self.uses[base] = self.uses.get(base, 0) + 1
        return f"{base}_{self.uses[base]}"


def stage_constants(nc, g):
    with ExitStack() as st:
        sem = g.sems.begin(st)
        rows = st.enter_context(nc.sbuf_tensor(g.name("param_rows"), [P, DEPTH, P], F32))
        crow = st.enter_context(nc.sbuf_tensor(g.name("cond_rows"), [2 * KD, P], F32))
        ps = st.enter_context(nc.psum_tensor(g.name("param_cols_ps"), [P, 4, BANK], F32))
        mod_ps = st.enter_context(nc.psum_tensor(g.name("mod_ps"), [P, BANK], F32))
        mod = Modulation(nc, g, st, sem, 0, 0, mod_ps[0:2, :], buffers=3)
        cond_done = sem("cond_done")
        loaded, zeroed, rows_in, tp_done = sem("loaded"), sem("zeroed"), sem("rows_in"), sem("tp_done")
        v_done, silu_done = sem("v_done"), sem("silu_done")
        consts = [(g.ident, "k_ident"), (g.masks, "k_masks"),
                  (g.pair, "k_pair"), (g.rope, "k_rope"), (g.rot, "k_rot"), (g.swap, "k_swap"), (g.band, "k_band"),
                  (g.iota, "k_iota"), (g.one, "k_one")]
        wide = []
        for l in range(DEPTH):
            for name, r in ROWS.items():
                src = g.dram[name][l]
                if name in ("hy_b1", "hy_b2"):
                    wide.append((rows[r:r + 1, l, 0:64], src.rearrange("(a n) -> a n", a=1)))
                elif name == "hy_freq":
                    wide.append((rows[r:r + 2, l, 0:64], src))
                else:
                    if name == "conv_w":
                        flat = src.rearrange("k (a n) -> (k a) n", n=P)
                    elif name in ("rw_w0", "rw_a0"):
                        flat = src.rearrange("k (a n) -> (k a) n", n=P)
                    elif name == "rw_r_k":
                        flat = src.rearrange("(a h) n -> a (h n)", h=2)
                    else:
                        flat = src.rearrange("(a n) -> a n", n=P)
                    wide.append((rows[r:r + flat.shape[0], l, :], flat))
        wide.append((crow[0:KD, :], g.dram["c"].rearrange("b (a n) -> (b a) n", n=P)))
        wide.append((crow[KD:2 * KD, :], g.dram["c_ctx"].rearrange("(a n) -> a n", n=P)))

        with nc.Block() as block:
            @block.sync
            def _(sp):
                sp.dma_start(g.ident[:], g.dram["k_ident"]).then_inc(rows_in, 16)
                sp.wait_ge(zeroed, 1)
                for dst, src in wide[0::2]:
                    sp.dma_start(dst, src).then_inc(rows_in, 16)
                mod.traffic(sp)

            @block.scalar
            def _(ac):
                ac.wait_ge(zeroed, 1)
                for dst, src in wide[1::2]:
                    ac.dma_start(dst, src).then_inc(rows_in, 16)
                ac.dma_start(g.X[:, 0:2, :], g.dram["ctx"][0].rearrange("(i p) d -> p i d", p=P)).then_inc(loaded, 16)
                ac.dma_start(g.X[:, 2:4, :], g.dram["x"][0].rearrange("(i p) d -> p i d", p=P)).then_inc(loaded, 16)
                for dst, name in consts[1:]:
                    ac.dma_start(dst[:], g.dram[name]).then_inc(loaded, 16)
                for l in range(DEPTH):
                    ac.dma_start(g.sink[:, l, :], g.dram["attn_sink"][l:l + 1, :].to_broadcast([P, AT_HQ])).then_inc(loaded, 16)
                ac.wait_ge(tp_done, 1)
                ac.activation(g.cond[:], ps[:, DEPTH, 0:2 * KD].rearrange("p (w k) -> p k w", w=2), ACT.Sigmoid).then_inc(silu_done, 1)
                for n in range(mod.count):
                    mod.take(ac, n)

            @block.gpsimd
            def _(po):
                po.sem_clear(g.sems.other)
                mod.gain_ones(po)
                po.memset(rows[:], 0.0).then_inc(zeroed, 1)
                po.memset(g.ones[:], 1.0)

            @block.tensor
            def _(pe):
                pe.wait_ge(rows_in, 16 * (len(wide) + 1))
                pe.transpose(ps[:, DEPTH, 0:2 * KD], crow[:, :], g.ident[0:2 * KD, 0:2 * KD]).then_inc(tp_done, 1)
                for l in range(DEPTH):
                    pe.transpose(ps[:, l, 0:P], rows[:, l, :], g.ident[:]).then_inc(tp_done, 1)
                pe.wait_ge(cond_done, 1)
                for n in range(mod.count):
                    mod.product(pe, n)

            @block.vector
            def _(ve):
                step = chained(ve, v_done)
                for l in range(DEPTH):
                    ve.wait_ge(tp_done, 2 + l)
                    step(ve.tensor_copy(g.par[:, l, :], ps[:, l, 0:P]))
                ve.wait_ge(silu_done, 1)
                (ve.tensor_tensor(g.cond[:], g.cond[:], ps[:, DEPTH, 0:2 * KD].rearrange("p (w k) -> p k w", w=2), ALU.mult)).then_inc(cond_done, 1)
                for l in range(DEPTH):
                    a = ROWS["rw_k_a"]
                    step(ve.tensor_scalar(g.omka[:, l, :], g.par[:, l, a:a + 2], -1.0, 1.0, ALU.mult, ALU.add))
                ve.wait_ge(loaded, 16 * (2 + len(consts) - 1 + DEPTH))
                step(ve.tensor_scalar(g.sink8[:], g.sink[:], float(AT_HD) ** 0.5, None, ALU.mult))
                mod.finish(ve)


class Modulation:

    def __init__(self, nc, g, st, sem, l, which, ps, buffers=2):
        self.g, self.l, self.which, self.ps, self.WB = g, l, which, ps, buffers
        self.first = (0, 2 * D // BANK)[which]
        self.count = (2 * D // BANK, 4 * D // BANK)[which]
        self.rows = K = (4, 8)[which]
        sb = lambda name, shape: st.enter_context(nc.sbuf_tensor(g.name(name), shape, F32))
        self.w = sb("mod_w_ring", [P, buffers, KD, BANK])
        self.bias, self.gain, self.pair = sb("mod_bias", [K, D]), sb("mod_gain", [K, D]), sb("mod_pair", [2, 2, BANK])
        self.out = g.mod[l][which]
        self.landed = [sem(f"mod_w_landed{b}") for b in range(buffers)]
        self.moved = [sem(f"mod_moved{b}") for b in range(2)]
        self.ones_set, self.rows_in, self.product_done, self.taken, self.finished = (
            sem(n) for n in ("mod_ones_set", "mod_rows_in", "mod_product_done", "mod_taken", "mod_finished"))

    def gain_ones(self, eng):
        eng.memset(self.gain[:], 1.0).then_inc(self.ones_set, 1)

    def load_rows(self, dma):
        part = 0 if self.which == 0 else 2
        for q in range(self.rows // 2):
            src = self.g.dram["mod_b"][self.l:self.l + 1, (part + q) * D:(part + q + 1) * D]
            dma.dma_start(self.bias[2 * q:2 * q + 2, :], src.to_broadcast([2, D])).then_inc(self.rows_in, 16)
        r = (2, 4)[self.which]
        dma.wait_ge(self.ones_set, 1)
        dma.dma_start(self.gain[r:r + 2, :], self.g.dram[f"norm{self.which + 1}_g"][self.l:self.l + 1, :].to_broadcast([2, D])).then_inc(self.rows_in, 16)

    def load(self, dma, n):
        if n >= self.WB:
            dma.wait_ge(self.product_done, n - self.WB + 1)
        wv = self.g.dram["mod_w"][self.l].rearrange("(k p) n -> p k n", p=P)
        c = (self.first + n) * BANK
        dma.dma_start(self.w[:, n % self.WB, :, :], wv[:, :, c:c + BANK]).then_inc(self.landed[n % self.WB], 16)

    def product(self, pe, n):
        pe.wait_ge(self.landed[n % self.WB], 16 * (n // self.WB + 1))
        if n:
            pe.wait_ge(self.taken, n)
        for k in range(KD):
            mm = pe.matmul(self.ps, self.g.cond[:, k, :], self.w[:, n % self.WB, k, :], start=k == 0, stop=k == KD - 1)
        mm.then_inc(self.product_done, 1)

    def take(self, ac, n):
        ac.wait_ge(self.product_done, n + 1)
        if n >= 2:
            ac.wait_ge(self.moved[n % 2], 16 * (n // 2))
        ac.activation(self.pair[:, n % 2, :], self.ps, ACT.Copy).then_inc(self.taken, 1)

    def move(self, dma, n):
        dma.wait_ge(self.taken, n + 1)
        q, half = n // 2, n % 2
        dma.dma_start(self.out[2 * q:2 * q + 2, half * BANK:(half + 1) * BANK], self.pair[:, n % 2, :]).then_inc(self.moved[n % 2], 16)

    def traffic(self, dma):
        for n in range(min(self.WB, self.count)):
            self.load(dma, n)
        self.load_rows(dma)
        for n in range(self.count):
            self.move(dma, n)
            if n + self.WB < self.count:
                self.load(dma, n + self.WB)

    def finish(self, ve):
        ve.wait_ge(self.rows_in, 16 * (self.rows // 2 + 1))
        for b in range(2):
            ve.wait_ge(self.moved[b], 16 * (self.count // 2))
        K = self.rows
        ve.scalar_tensor_tensor(out=self.out[:], in0=self.out[:], scalar=self.g.one[0:K, self.which:self.which + 1], in1=self.bias[:],
                                op0=ALU.add, op1=ALU.add).then_inc(self.finished, 1)
        ve.wait_ge(self.finished, 1)
        ve.tensor_tensor(self.out[:], self.out[:], self.gain[:], ALU.mult).then_inc(self.finished, 1)


def broadcast_row(pe, g, l, ps, part, w):
    which, K = (0, 4) if part < 2 else (1, 8)
    row = 2 * (part - 2 * which) + w
    for j in range(2):
        mm = pe.matmul(ps[:, j, :], g.ident[0:K, row:row + 1].to_broadcast([K, P]), g.mod[l][which][:, j * BANK:(j + 1) * BANK], start=True, stop=True)
    return mm


def stage_norm(nc, g, l, tiles, part, H, HT):
    with ExitStack() as st:
        sem = g.sems.begin(st)
        h = H if H is not None else st.enter_context(nc.sbuf_tensor(g.name("h_rows"), [P, TILES, D], F32))
        sq = st.enter_context(nc.sbuf_tensor(g.name("squares"), [P, 2, D], F32))
        ms = st.enter_context(nc.sbuf_tensor(g.name("mean_square"), [P, TILES], F32))
        bc = st.enter_context(nc.psum_tensor(g.name("mod_bc"), [P, 4, BANK], F32))
        tp = st.enter_context(nc.psum_tensor(g.name("h_tp"), [P, 4, BANK], F32))
        ms_done, root_done, bc_done, v_done, h_done = sem("ms_done"), sem("root_done"), sem("bc_done"), sem("v_done"), sem("h_done")
        tp_done, tp_out = sem("tp_done"), sem("tp_out")
        streams = [w for w in (0, 1) if any((i < 2) == (w == 0) for i in tiles)]
        mine = lambda w: [i for i in tiles if (i < 2) == (w == 0)]

        with nc.Block() as block:
            @block.gpsimd
            def _(po):
                po.sem_clear(g.sems.other)

            @block.scalar
            def _(ac):
                for n, i in enumerate(tiles):
                    if n >= 2:
                        ac.wait_ge(ms_done, n - 1)
                    ac.activation(sq[:, n % 2, :], g.X[:, i, :], ACT.Square, scale=float(D) ** -0.5,
                                  accum_out=ms[:, i:i + 1]).then_inc(ms_done, 1)
                ac.wait_ge(v_done, 1)
                ac.activation(ms[:, tiles[0]:tiles[-1] + 1], ms[:, tiles[0]:tiles[-1] + 1], ACT.Sqrt).then_inc(root_done, 1)
                for n in range(2 * len(tiles)):
                    i, half = tiles[n // 2], n % 2
                    ac.wait_ge(tp_done, n + 1)
                    ac.activation(HT[:, half * 4:half * 4 + 4, i * P:(i + 1) * P],
                                  tp[:, n % 4, :].rearrange("p (k t) -> p k t", k=4), ACT.Copy).then_inc(tp_out, 1)

            @block.tensor
            def _(pe):
                n = 0
                for s, w in enumerate(streams):
                    if s:
                        pe.wait_ge(h_done, len(mine(streams[0])))
                    for q in range(2):
                        mm = broadcast_row(pe, g, l, bc[:, 2 * q:2 * q + 2, :], part + 1 - q, 1 - w)
                    mm.then_inc(bc_done, 1)
                    for i in mine(w):
                        pe.wait_ge(h_done, n // 2 + 1)
                        for half in range(2):
                            if n >= 4:
                                pe.wait_ge(tp_out, n - 3)
                            for k in range(4):
                                mm = pe.transpose(tp[:, n % 4, k * P:(k + 1) * P], h[:, i, (half * 4 + k) * P:(half * 4 + k + 1) * P], g.ident[:])
                            mm.then_inc(tp_done, 1)
                            n += 1

            @block.vector
            def _(ve):
                step = chained(ve, v_done)
                ve.wait_ge(ms_done, len(tiles))
                t0, t1 = tiles[0], tiles[-1] + 1
                step(ve.tensor_scalar(ms[:, t0:t1], ms[:, t0:t1], 1e-6, None, ALU.add))
                ve.wait_ge(root_done, 1)
                step(ve.reciprocal(ms[:, t0:t1], ms[:, t0:t1]))
                for s, w in enumerate(streams):
                    ve.wait_ge(bc_done, s + 1)
                    for i in mine(w):
                        step(ve.scalar_tensor_tensor(out=h[:, i, :], in0=g.X[:, i, :], scalar=ms[:, i:i + 1],
                                                     in1=bc[:, 0:2, :].rearrange("p a b -> p (a b)"), op0=ALU.mult, op1=ALU.mult))
                        ve.tensor_tensor(h[:, i, :], h[:, i, :], bc[:, 2:4, :].rearrange("p a b -> p (a b)"), ALU.add).then_inc(h_done, 1)


def stage_input_projection(nc, g, l, HT):
    CW, WB, ZB = 3, 3, 3
    with ExitStack() as st:
        sem = g.sems.begin(st)
        w = st.enter_context(nc.sbuf_tensor(g.name("w_in_ring"), [P, WB, KD, CW * P], F32))
        z = st.enter_context(nc.sbuf_tensor(g.name("z_padded"), [P, ZB, 2, SEQ + 2], F32))
        ps = st.enter_context(nc.psum_tensor(g.name("z_ps"), [P, 4, BANK], F32))
        landed = [sem(f"w_in_landed{b}") for b in range(WB)]
        padded, mm_done, evac, conv_done, v_done = sem("padded"), sem("mm_done"), sem("evacuated"), sem("conv_done"), sem("v_done")
        wv = g.dram["w_in"][l].rearrange("(k p) n -> p k n", p=P)
        cw, cb = ROWS["conv_w"], ROWS["conv_b"]

        with nc.Block() as block:
            @block.sync
            def _(sp):
                for n in range(IN_TILES // CW):
                    if n >= WB:
                        sp.wait_ge(mm_done, (n - WB + 1) * CW)
                    sp.dma_start(w[:, n % WB, :, :], wv[:, :, n * CW * P:(n + 1) * CW * P]).then_inc(landed[n % WB], 16)

            @block.gpsimd
            def _(po):
                po.sem_clear(g.sems.other)
                po.memset(z[:], 0.0).then_inc(padded, 1)

            @block.tensor
            def _(pe):
                for j in range(IN_TILES):
                    n = j // CW
                    pe.wait_ge(landed[n % WB], 16 * (n // WB + 1))
                    if j >= 4:
                        pe.wait_ge(evac, j - 3)
                    for k in range(KD):
                        mm = pe.matmul(ps[:, j % 4, :], w[:, n % WB, k, (j % CW) * P:(j % CW + 1) * P], HT[:, k, :], start=k == 0, stop=k == KD - 1)
                    mm.then_inc(mm_done, 1)

            @block.scalar
            def _(ac):
                ac.wait_ge(padded, 1)
                for j in range(IN_TILES):
                    ac.wait_ge(mm_done, j + 1)
                    if j < CONV_TILES:
                        if j >= ZB:
                            ac.wait_ge(conv_done, j - ZB + 1)
                        ac.activation(z[:, j % ZB, :, 1:SEQ + 1], ps[:, j % 4, :].rearrange("p (s t) -> p s t", s=2), ACT.Copy)
                        ac.activation(g.S[:, j, :], ps[:, j % 4, :], ACT.Identity, scale=g.par[:, l, cw + 12 + j:cw + 13 + j],
                                      bias=g.par[:, l, cb + j:cb + j + 1]).then_inc(evac, 1)
                    else:
                        f = {LORA0: ACT.Tanh, LORA0 + 2: ACT.Sigmoid}.get(j, ACT.Copy)
                        ac.activation(g.S[:, j, :], ps[:, j % 4, :], f).then_inc(evac, 1)

            @block.vector
            def _(ve):
                step = chained(ve, v_done)
                for j in range(CONV_TILES):
                    ve.wait_ge(evac, j + 1)
                    s = g.S[:, j, :].rearrange("p (s t) -> p s t", s=2)
                    step(ve.scalar_tensor_tensor(out=s, in0=z[:, j % ZB, :, 0:SEQ], scalar=g.par[:, l, cw + j:cw + j + 1], in1=s, op0=ALU.mult, op1=ALU.add))
                    ve.scalar_tensor_tensor(out=s, in0=z[:, j % ZB, :, 2:SEQ + 2], scalar=g.par[:, l, cw + 24 + j:cw + 25 + j], in1=s,
                                            op0=ALU.mult, op1=ALU.add).then_inc(conv_done, 1)


def stage_hyena(nc, g, l):
    FR = 2
    with ExitStack() as st:
        sem = g.sems.begin(st)
        sb = lambda name, shape: st.enter_context(nc.sbuf_tensor(g.name(name), shape, F32))
        w1, w2, w3, b3 = sb("hy_w1", [HY_EMB, HY_HID]), sb("hy_w2", [HY_HID, HY_HID]), sb("hy_w3", [HY_HID, 512]), sb("hy_b3", [1, 512])
        emb, window, dft = sb("emb", [HY_EMB, SEQ]), sb("window", [P, 2, 512]), sb("dft", [P, 4, 2, SEQ])
        arg, turns, hid = sb("hy_arg", [HY_HID, 2, SEQ]), sb("hy_turns", [HY_HID, 2, SEQ]), sb("hy_hid", [HY_HID, 2, SEQ])
        F, sq = sb("filter", [P, 2, 512]), sb("filter_sq", [P, 2, 512])
        even, odd, rk = sb("filter_even", [P, 2, HY_CH]), sb("filter_odd", [P, 2, HY_CH]), sb("filter_rnorm", [P, HY_CH])
        K = sb("filter_spectrum", [P, FR, 2, HY_CH])
        u, U = sb("u_cols", [P, 2, TOK]), sb("u_rows", [P, 2, 512])
        Yc, Yn, tmp = sb("y_cos", [P, FR, 512]), sb("y_sin", [P, FR, 512]), sb("y_tmp", [P, 512])
        hy, hsq, rs = sb("hy", [P, 2, TOK]), sb("hy_sq", [P, 2, TOK]), sb("hy_rnorm", [P, TOK])
        ps = st.enter_context(nc.psum_tensor(g.name("hy_ps"), [P, 8, BANK], F32))
        w_in, v_done, t_done, a_done = sem("w_in"), sem("v_done"), sem("t_done"), sem("a_done")
        layer_in, sin_done, filt_in, F_done, norm_sum, rk_ready, K_in, K_done = (
            sem(n) for n in ("layer_arg_in", "sin_done", "filter_in", "filter_done", "norm_sum", "norm_ready", "spectrum_in", "spectrum_done"))
        arg_ready, root_done, eps_done, u_done, ut_in, U_done, Uf_in, Y_done, y_in, hy_done, ms_in = (
            sem(n) for n in ("arg_ready", "root_done", "eps_done", "u_done", "u_transposed", "u_rows_done", "u_spectrum_in", "y_spectrum_done", "y_in", "hy_done", "hy_ms_in"))
        R = ROWS
        par = lambda name, k=0, p=P: g.par[0:p, l, R[name] + k:R[name] + k + 1]
        C = lambda t, f: dft[:, 0, t, f * P:(f + 1) * P]
        Sn = lambda t, f: dft[:, 1, t, f * P:(f + 1) * P]

        with nc.Block() as block:
            @block.sync
            def _(sp):
                for dst, name in ((w1, "hy_w1"), (w2, "hy_w2"), (w3, "hy_w3")):
                    sp.dma_start(dst[:], g.dram[name][l]).then_inc(w_in, 16)
                sp.dma_start(b3[:], g.dram["hy_b3"][l:l + 1, :]).then_inc(w_in, 16)
                for dst, name in ((emb, "k_emb"), (window, "k_window"), (dft, "k_dft")):
                    sp.dma_start(dst[:], g.dram[name]).then_inc(w_in, 16)

            @block.gpsimd
            def _(po):
                po.sem_clear(g.sems.other)

            @block.tensor
            def _(pe):
                pe.wait_ge(w_in, 16 * 7)
                pe.matmul(ps[0:HY_HID, 0, 0:SEQ], w1[:], emb[:], start=True, stop=True).then_inc(layer_in, 1)
                pe.wait_ge(u_done, 1)
                for t in range(2):
                    for s in range(2):
                        for c in range(2):
                            mm = pe.transpose(ps[:, 5 + t, s * 256 + c * P:s * 256 + (c + 1) * P], u[:, c, (2 * s + t) * P:(2 * s + t + 1) * P], g.ident[:])
                mm.then_inc(ut_in, 1)
                pe.wait_ge(sin_done, 1)
                pe.matmul(ps[0:HY_HID, 1, 0:SEQ], w2[:], hid[:, 0, :], start=True, stop=True).then_inc(layer_in, 1)
                pe.wait_ge(sin_done, 2)
                for t in range(2):
                    pe.matmul(ps[:, 2 + t, :], hid[:, 1, t * P:(t + 1) * P], w3[:], start=True, stop=False)
                    mm = pe.matmul(ps[:, 2 + t, :], g.ones[0:1, :], b3[:], start=False, stop=True)
                mm.then_inc(filt_in, 1)
                pe.wait_ge(U_done, 1)
                for f in range(FR):
                    for q, basis in ((0, C), (1, Sn)):
                        for t in range(2):
                            mm = pe.matmul(ps[:, 4 + 2 * f + q, :], basis(t, f), U[:, t, :], start=t == 0, stop=t == 1)
                mm.then_inc(Uf_in, 1)
                pe.wait_ge(F_done, 1)
                for n in range(4):
                    mm = pe.matmul(ps[:, 0, 0:HY_CH], g.ones[:], sq[:, n // 2, (n % 2) * HY_CH:(n % 2 + 1) * HY_CH], start=n == 0, stop=n == 3)
                mm.then_inc(norm_sum, 1)
                pe.wait_ge(F_done, 2)
                for f in range(FR):
                    for q, (basis, part) in enumerate(((C, even), (Sn, odd))):
                        for t in range(2):
                            mm = pe.matmul(ps[:, 2 + f, q * HY_CH:(q + 1) * HY_CH], basis(t, f), part[:, t, :], start=t == 0, stop=t == 1)
                mm.then_inc(K_in, 1)
                pe.wait_ge(Y_done, 1)
                for c in range(2):
                    for s in range(2):
                        cols = slice(s * 256 + c * P, s * 256 + (c + 1) * P)
                        for f in range(FR):
                            pe.matmul(ps[:, c, s * 256:(s + 1) * 256], Yc[:, f, cols], dft[:, 2, f, :], start=f == 0, stop=False)
                            mm = pe.matmul(ps[:, c, s * 256:(s + 1) * 256], Yn[:, f, cols], dft[:, 3, f, :], start=False, stop=f == FR - 1)
                mm.then_inc(y_in, 1)
                pe.wait_ge(hy_done, 1)
                for c in range(2):
                    mm = pe.matmul(ps[:, 2, :], g.ones[:], hsq[:, c, :], start=c == 0, stop=c == 1)
                mm.then_inc(ms_in, 1)

            @block.scalar
            def _(ac):
                for k in range(2):
                    ac.wait_ge(arg_ready, k + 1)
                    ac.activation(hid[:, k, :], arg[:, k, :], ACT.Sin).then_inc(sin_done, 1)
                for k, t in enumerate((rk, rs)):
                    ac.wait_ge(eps_done, k + 1)
                    ac.activation(t[:], t[:], ACT.Sqrt).then_inc(root_done, 1)

            @block.vector
            def _(ve):
                step = chained(ve, v_done)
                step(ve.tensor_tensor(u[:], g.S[:, 2:4, :], g.S[:, 4:6, :], ALU.mult))
                ve.sem_inc(u_done, 1)
                for k in range(2):
                    ve.wait_ge(layer_in, k + 1)
                    a, n = arg[:, k, :], turns[:, k, :]
                    step(ve.tensor_scalar(a, ps[0:HY_HID, k, 0:SEQ], par(f"hy_b{k + 1}", 0, HY_HID), par("hy_freq", k, HY_HID), ALU.add, ALU.mult))
                    step(ve.tensor_scalar(n, a, 1.0 / TWO_PI, 12582912.0, ALU.mult, ALU.add))
                    step(ve.tensor_scalar(n, n, 12582912.0, None, ALU.subtract))
                    step(ve.scalar_tensor_tensor(out=a, in0=n, scalar=-TWO_PI, in1=a, op0=ALU.mult, op1=ALU.add))
                    ve.tensor_scalar(a, a, PI_BELOW, -PI_BELOW, ALU.min, ALU.max).then_inc(arg_ready, 1)
                    if k == 0:
                        ve.wait_ge(ut_in, 1)
                        ve.tensor_copy(U[:], ps[:, 5:7, :]).then_inc(U_done, 1)
                ve.wait_ge(filt_in, 1)
                step(ve.tensor_tensor(F[:], ps[:, 2:4, :], window[:], ALU.mult))
                ve.tensor_tensor(sq[:], F[:], F[:], ALU.mult).then_inc(F_done, 1)
                step(ve.tensor_tensor(even[:], F[:, :, 0:HY_CH], F[:, :, HY_CH:512], ALU.add))
                ve.tensor_tensor(odd[:], F[:, :, HY_CH:512], F[:, :, 0:HY_CH], ALU.subtract).then_inc(F_done, 1)
                ve.wait_ge(norm_sum, 1)
                ve.tensor_scalar(rk[:], ps[:, 0, 0:HY_CH], 1e-6, None, ALU.add).then_inc(eps_done, 1)
                ve.wait_ge(root_done, 1)
                step(ve.reciprocal(rk[:], rk[:]))
                ve.wait_ge(K_in, 1)
                for f in range(FR):
                    step(ve.tensor_tensor(K[:, f, :, :], ps[:, 2 + f, :].rearrange("p (q c) -> p q c", q=2), rk[:].unsqueeze(1).to_broadcast([P, 2, HY_CH]), ALU.mult))
                ve.wait_ge(Uf_in, 1)
                for f in range(FR):
                    view = lambda x: x.rearrange("p (s c) -> p s c", s=2)
                    uc, us = view(ps[:, 4 + 2 * f, :]), view(ps[:, 5 + 2 * f, :])
                    kr, ki = (K[:, f, q, :].unsqueeze(1).to_broadcast([P, 2, HY_CH]) for q in range(2))
                    for dst, a, b, op in ((Yc, (uc, kr), (us, ki), ALU.add), (Yn, (us, kr), (uc, ki), ALU.subtract)):
                        step(ve.tensor_tensor(view(dst[:, f, :]), *a, ALU.mult))
                        step(ve.tensor_tensor(view(tmp[:]), *b, ALU.mult))
                        step(ve.tensor_tensor(dst[:, f, :], dst[:, f, :], tmp[:], op))
                ve.sem_inc(Y_done, 1)
                ve.wait_ge(y_in, 1)
                for c in range(2):
                    step(ve.scalar_tensor_tensor(out=hy[:, c, :], in0=u[:, c, :], scalar=par("hy_bias", c), in1=ps[:, c, :], op0=ALU.mult, op1=ALU.add))
                step(ve.tensor_tensor(hy[:], hy[:], g.S[:, 0:2, :], ALU.mult))
                ve.tensor_tensor(hsq[:], hy[:], hy[:], ALU.mult).then_inc(hy_done, 1)
                ve.wait_ge(ms_in, 1)
                ve.tensor_scalar(rs[:], ps[:, 2, :], 1.0 / HY_CH, 1e-6, ALU.mult, ALU.add).then_inc(eps_done, 1)
                ve.wait_ge(root_done, 2)
                step(ve.reciprocal(rs[:], rs[:]))
                for c in range(2):
                    step(ve.scalar_tensor_tensor(out=g.mix[:, c, :], in0=hy[:, c, :], scalar=par("hy_out_g", c), in1=rs[:], op0=ALU.mult, op1=ALU.mult))


def stage_attention(nc, g, l, tiles):
    SCALE = float(AT_HD) ** -0.5
    units = [(i, j) for i in tiles for j in range(4)]
    keys = lambda i: TOK if i >= 2 else SEQ
    with ExitStack() as st:
        sem = g.sems.begin(st)
        sb = lambda name, shape: st.enter_context(nc.sbuf_tensor(g.name(name), shape, F32))
        rot, KS, VT = sb("rotated", [P, 5, SEQ]), sb("k_swapped", [P, TOK]), sb("v_rows", [P, TILES, P])
        E, PT = sb("scores", [P, 2, 2, TOK]), sb("probs_cols", [P, 2, 2, TOK])
        mx, nm, total, es, rden = (sb(n, [P, 2, 2]) for n in ("row_max", "neg_max", "row_sum", "sink_exp", "rden"))
        O, osq, ms = sb("attn_rows", [P, TILES, AT_W]), sb("attn_sq", [P, AT_W]), sb("attn_ms", [P, TILES])
        sps = st.enter_context(nc.psum_tensor(g.name("scores_ps"), [P, 2, 2, BANK], F32))
        tps = st.enter_context(nc.psum_tensor(g.name("probs_ps"), [P, 2, BANK], F32))
        out_ps = st.enter_context(nc.psum_tensor(g.name("out_ps"), [P, BANK], F32))
        mod_ps = st.enter_context(nc.psum_tensor(g.name("mod_ps"), [P, BANK], F32))
        mod = Modulation(nc, g, st, sem, l, 1, mod_ps[0:2, :])
        rot_in, rope_done, ks_in, kv_done, v_done = (sem(n) for n in ("rot_in", "rope_done", "kv_in", "kv_done", "v_done"))
        s_in, s_out, max_done, exp_done, pt_in, pt_out, pv_in, o_done = (
            sem(n) for n in ("scores_in", "scores_out", "max_done", "exp_done", "probs_in", "probs_out", "pv_in", "o_done"))
        sq_done, eps_done, root_done, on_done, ot_in, ot_out, sqa = (
            sem(n) for n in ("sq_done", "eps_done", "root_done", "o_normed", "o_cols_in", "o_cols_out", "sq_each"))
        lat = slice(SEQ, TOK)

        every = len(units) // mod.count

        with nc.Block() as block:
            @block.sync
            def _(sp):
                mod.traffic(sp)

            @block.gpsimd
            def _(po):
                po.sem_clear(g.sems.other)
                mod.gain_ones(po)

            @block.tensor
            def _(pe):
                for j in range(5):
                    mm = pe.matmul(sps[:, j // 4, j // 2 % 2, (j % 2) * SEQ:(j % 2 + 1) * SEQ], g.rot[:], g.S[:, Q0 + j, lat], start=True, stop=True)
                mm.then_inc(rot_in, 1)
                for i in range(TILES):
                    pe.transpose(tps[:, 1, i * P:(i + 1) * P], g.S[:, V0, i * P:(i + 1) * P], g.ident[:])
                pe.wait_ge(rope_done, 1)
                pe.matmul(tps[:, 0, :], g.swap[:], g.S[:, K0, :], start=True, stop=True).then_inc(ks_in, 1)

                def scores(n):
                    i, j = units[n]
                    if n >= 2:
                        pe.wait_ge(s_out, n - 1)
                    for h in range(2):
                        k = g.S[64 * h:64 * h + 64, K0, 0:keys(i)] if j // 2 == h else KS[64 * h:64 * h + 64, 0:keys(i)]
                        mm = pe.matmul(sps[:, n % 2, h, 0:keys(i)], g.S[64 * h:64 * h + 64, Q0 + j, i * P:(i + 1) * P], k, start=True, stop=True)
                    mm.then_inc(s_in, 1)

                def turn(n):
                    i, j = units[n]
                    pe.wait_ge(exp_done, n + 1)
                    if n >= 1:
                        pe.wait_ge(pt_out, 2 * n)
                    for h in range(2):
                        for t in range(keys(i) // P):
                            mm = pe.transpose(tps[:, h, t * P:(t + 1) * P], E[:, n % 2, h, t * P:(t + 1) * P], g.ident[:])
                        mm.then_inc(pt_in, 1)

                def values(n):
                    i, j = units[n]
                    pe.wait_ge(pt_out, 2 * n + 2)
                    if n:
                        pe.wait_ge(o_done, n)
                    for h in range(2):
                        for t in range(keys(i) // P):
                            mm = pe.matmul(out_ps[:, h * 64:h * 64 + 64], PT[:, n % 2, h, t * P:(t + 1) * P],
                                           VT[:, t, 64 * (j // 2):64 * (j // 2) + 64], start=t == 0, stop=t == keys(i) // P - 1)
                    mm.then_inc(pv_in, 1)

                pe.wait_ge(kv_done, 2)
                scores(0)
                for n in range(len(units)):
                    if n + 1 < len(units):
                        scores(n + 1)
                    if n % every == 0:
                        mod.product(pe, n // every)
                    turn(n)
                    if n:
                        values(n - 1)
                values(len(units) - 1)
                for m, i in enumerate(tiles):
                    pe.wait_ge(on_done, m + 1)
                    if m >= 2:
                        pe.wait_ge(ot_out, m - 1)
                    for j in range(4):
                        mm = pe.transpose(tps[:, m % 2, j * P:(j + 1) * P], O[:, i, j * P:(j + 1) * P], g.ident[:])
                    mm.then_inc(ot_in, 1)

            @block.scalar
            def _(ac):
                ac.wait_ge(ks_in, 1)
                ac.activation(KS[:], tps[:, 0, :], ACT.Copy).then_inc(kv_done, 1)
                ac.activation(VT[:].rearrange("p i c -> p (i c)"), tps[:, 1, :], ACT.Copy).then_inc(kv_done, 1)
                def exps(n):
                    i, j = units[n]
                    b = n % 2
                    ac.wait_ge(max_done, n + 1)
                    for h in range(2):
                        ac.activation(E[:, b, h, 0:keys(i)], E[:, b, h, 0:keys(i)], ACT.Exp, bias=nm[:, b, h:h + 1], scale=SCALE,
                                      accum_out=total[:, b, h:h + 1])
                    ac.activation(es[:, b, :], es[:, b, :], ACT.Exp).then_inc(exp_done, 1)

                exps(0)
                for n, (i, j) in enumerate(units):
                    b = n % 2
                    if n + 1 < len(units):
                        exps(n + 1)
                    ac.wait_ge(pt_in, 2 * n + 1)
                    if n >= 2:
                        ac.wait_ge(pv_in, n - 1)
                    ac.activation(PT[:, b, 0, 0:keys(i)], tps[:, 0, 0:keys(i)], ACT.Copy).then_inc(pt_out, 1)
                    if n % every == 0:
                        mod.take(ac, n // every)
                ac.wait_ge(o_done, len(units))
                for m, i in enumerate(tiles):
                    if m:
                        ac.wait_ge(sq_done, m)
                    ac.activation(osq[:], O[:, i, :], ACT.Square, scale=float(AT_W) ** -0.5, accum_out=ms[:, i:i + 1]).then_inc(sq_done, 1)
                ac.wait_ge(eps_done, 1)
                ac.activation(ms[:, tiles[0]:tiles[-1] + 1], ms[:, tiles[0]:tiles[-1] + 1], ACT.Sqrt).then_inc(root_done, 1)
                for m, i in enumerate(tiles):
                    ac.wait_ge(ot_in, m + 1)
                    for j in range(4):
                        r = ROWS["at_out_g"] + j
                        a = ac.activation(g.mix[:, 4 + j, i * P:(i + 1) * P], tps[:, m % 2, j * P:(j + 1) * P], ACT.Copy, scale=g.par[:, l, r:r + 1])
                    a.then_inc(ot_out, 1)

            @block.vector
            def _(ve):
                step = chained(ve, v_done)
                ve.wait_ge(rot_in, 1)
                qk = g.S[:, Q0:Q0 + 5, lat]
                step(ve.tensor_tensor(rot[:], sps[:].rearrange("p a b (c t) -> p (a b c) t", c=2)[:, 0:5, :], g.rope[:, 1, :].unsqueeze(1).to_broadcast([P, 5, SEQ]), ALU.mult))
                step(ve.tensor_tensor(qk, qk, g.rope[:, 0, :].unsqueeze(1).to_broadcast([P, 5, SEQ]), ALU.mult))
                ve.tensor_tensor(qk, qk, rot[:], ALU.add).then_inc(rope_done, 1)

                def softmax_head(n):
                    i, j = units[n]
                    b, w = n % 2, keys(i)
                    ve.wait_ge(s_in, n + 1)
                    if n >= 2:
                        ve.wait_ge(pt_in, 2 * n - 2)
                    if i >= 2:
                        ve.tensor_tensor(E[:, b, :, 0:w], sps[:, b, :, 0:w], g.band[:, i - 2, :].unsqueeze(1).to_broadcast([P, 2, TOK]), ALU.add).then_inc(s_out, 1)
                    else:
                        ve.tensor_copy(E[:, b, :, 0:w], sps[:, b, :, 0:w]).then_inc(s_out, 1)
                    ve.wait_ge(s_out, n + 1)
                    sink = g.sink[:, l, 2 * j:2 * j + 2]
                    step(ve.tensor_reduce(mx[:, b, :], E[:, b, :, 0:w], AX.X, ALU.max))
                    step(ve.tensor_tensor(mx[:, b, :], mx[:, b, :], g.sink8[:, l, 2 * j:2 * j + 2], ALU.max))
                    step(ve.tensor_scalar(nm[:, b, :], mx[:, b, :], -SCALE, None, ALU.mult))
                    ve.tensor_tensor(es[:, b, :], sink, nm[:, b, :], ALU.add).then_inc(max_done, 1)

                def weigh(n):
                    i, j = units[n]
                    b = n % 2
                    ve.wait_ge(pv_in, n + 1)
                    ve.tensor_tensor(O[:, i, j * P:(j + 1) * P].rearrange("p (h c) -> p h c", h=2), out_ps[:, 0:P].rearrange("p (h c) -> p h c", h=2),
                                     rden[:, b, :].unsqueeze(2).to_broadcast([P, 2, 64]), ALU.mult).then_inc(o_done, 1)

                softmax_head(0)
                for n, (i, j) in enumerate(units):
                    b = n % 2
                    if n + 1 < len(units):
                        softmax_head(n + 1)
                    ve.wait_ge(exp_done, n + 1)
                    if n >= 2:
                        ve.wait_ge(o_done, n - 1)
                    step(ve.tensor_tensor(rden[:, b, :], total[:, b, :], es[:, b, :], ALU.add))
                    step(ve.reciprocal(rden[:, b, :], rden[:, b, :]))
                    ve.wait_ge(pt_in, 2 * n + 2)
                    if n >= 2:
                        ve.wait_ge(pv_in, n - 1)
                    ve.tensor_copy(PT[:, b, 1, 0:keys(i)], tps[:, 1, 0:keys(i)]).then_inc(pt_out, 1)
                    if n:
                        weigh(n - 1)
                weigh(len(units) - 1)
                mod.finish(ve)
                ve.wait_ge(sq_done, len(tiles))
                part = ms[:, tiles[0]:tiles[-1] + 1]
                ve.tensor_scalar(part, part, 1e-6, None, ALU.add).then_inc(eps_done, 1)
                ve.wait_ge(root_done, 1)
                step(ve.reciprocal(part, part))
                for i in tiles:
                    ve.tensor_scalar(O[:, i, :], O[:, i, :], ms[:, i:i + 1], None, ALU.mult).then_inc(on_done, 1)


KK, RR, KC, VC = 0, 6, 8, 10
B_AT, KD_AT, Y_AT = (2, 4), (15, 17), (12, 19)


def stage_rwkv_operands(nc, g, l):
    with ExitStack() as st:
        sem = g.sems.begin(st)
        sb = lambda name, shape: st.enter_context(nc.sbuf_tensor(g.name(name), shape, F32))
        wup, aup = sb("w_up", [P, RW_W]), sb("a_up", [P, RW_W])
        sq, lw, keep = sb("kk_sq", [P, 2, TOK]), sb("log_decay", [P, 2, 2, TOK]), sb("chunk_keep", [P, TOK])
        ps = st.enter_context(nc.psum_tensor(g.name("rwkv_ps"), [P, 8, BANK], F32))
        w_in, keep_set, sq_done, kk_in, eps_done, root_done, kk_done, lora_in, sig_done, v_done, log_done, exp_done = (
            sem(n) for n in ("w_in", "keep_set", "sq_done", "kk_in", "eps_done", "root_done", "kk_done", "lora_in", "sig_done", "v_done", "log_done", "exp_done"))
        par = lambda name, k: g.par[:, l, ROWS[name] + k:ROWS[name] + k + 1]
        kk = g.S[:, KK:KK + 2, :]
        bank = lambda d, q, p: (2 + 4 * d + 2 * q + p) % 8

        with nc.Block() as block:
            @block.sync
            def _(sp):
                sp.dma_start(wup[:], g.dram["rw_w_up"][l].rearrange("d r n -> (d r) n")).then_inc(w_in, 16)
                sp.dma_start(aup[:], g.dram["rw_a_up"][l].rearrange("d r n -> (d r) n")).then_inc(w_in, 16)

            @block.gpsimd
            def _(po):
                po.sem_clear(g.sems.other)
                po.memset(keep[:], 1.0).then_inc(keep_set, 1)
                po.wait_ge(keep_set, 1)
                po.memset(keep[:].rearrange("p (c t) -> p c t", t=CHUNK)[:, :, 0:1], 0.0).then_inc(keep_set, 1)

            @block.tensor
            def _(pe):
                pe.wait_ge(w_in, 32)
                for d in range(2):
                    if d:
                        pe.wait_ge(sq_done, 1)
                        for p in range(2):
                            mm = pe.matmul(ps[:, p, :], g.pair[:], sq[:, p, :], start=True, stop=True)
                        mm.then_inc(kk_in, 1)
                        pe.wait_ge(eps_done, 1)
                    for q, (up, src) in enumerate(((wup, LORA0), (aup, LORA0 + 1))):
                        for p in range(2):
                            mm = pe.matmul(ps[:, bank(d, q, p), :], up[64 * d:64 * d + 64, p * P:(p + 1) * P], g.S[64 * d:64 * d + 64, src, :], start=True, stop=True)
                    mm.then_inc(lora_in, 1)

            @block.scalar
            def _(ac):
                for d in range(2):
                    ac.wait_ge(lora_in, d + 1)
                    for p in range(2):
                        ac.activation(lw[:, d, p, :], ps[:, bank(d, 0, p), :], ACT.Sigmoid, bias=par("rw_w0", 2 * d + p))
                        a = ac.activation(g.S[:, B_AT[d] + p, :], ps[:, bank(d, 1, p), :], ACT.Sigmoid, bias=par("rw_a0", 2 * d + p))
                    a.then_inc(sig_done, 1)
                ac.wait_ge(eps_done, 1)
                ac.activation(sq[:], sq[:], ACT.Sqrt).then_inc(root_done, 1)
                for d in range(2):
                    ac.wait_ge(log_done, d + 1)
                    ac.activation(g.eL[:, d, :, :], g.eN[:, d, :, :], ACT.Exp).then_inc(exp_done, 1)
                    ac.wait_ge(exp_done, 3 * d + 1)
                    ac.activation(g.eN[:, d, :, :], g.eN[:, d, :, :], ACT.Exp, scale=-1.0).then_inc(exp_done, 1)
                    ac.activation(g.eP[:, d, :, :], g.eP[:, d, :, :], ACT.Exp).then_inc(exp_done, 1)

            @block.vector
            def _(ve):
                step = chained(ve, v_done)
                for p in range(2):
                    step(ve.tensor_scalar(kk[:, p, :], g.S[:, KC + p, :], par("rw_k_k", p), None, ALU.mult))
                ve.tensor_tensor(sq[:], kk, kk, ALU.mult).then_inc(sq_done, 1)
                ve.wait_ge(kk_in, 1)
                ve.tensor_scalar(sq[:], ps[:, 0:2, :], 1e-12, None, ALU.add).then_inc(eps_done, 1)
                ve.wait_ge(keep_set, 2)
                for d in range(2):
                    ve.wait_ge(sig_done, d + 1)
                    step(ve.tensor_scalar(lw[:, d, :, :], lw[:, d, :, :], -DECAY, None, ALU.mult))
                    for p in range(2):
                        src, dst = lw[:, d, p, :], g.eN[:, d, p, :]
                        if d:
                            src, dst = lw[:, d, p, ::-1], g.eN[:, d, p, ::-1]
                        step(ve.tensor_tensor_scan(dst, keep[:], src, 0.0, ALU.mult, ALU.add))
                    ve.tensor_tensor(g.eP[:, d, :, :], g.eN[:, d, :, :], lw[:, d, :, :], ALU.subtract).then_inc(log_done, 1)
                ve.wait_ge(root_done, 1)
                step(ve.reciprocal(sq[:], sq[:]))
                step(ve.tensor_tensor(kk, kk, sq[:], ALU.mult))
                for d in range(2):
                    a, k = g.S[:, B_AT[d]:B_AT[d] + 2, :], g.S[:, KD_AT[d]:KD_AT[d] + 2, :]
                    for p in range(2):
                        step(ve.tensor_scalar(k[:, p, :], a[:, p, :], par("rw_k_a", p), g.omka[:, l, p:p + 1], ALU.mult, ALU.add))
                    step(ve.tensor_tensor(k, k, g.S[:, KC:KC + 2, :], ALU.mult))
                    step(ve.tensor_tensor(a, a, kk, ALU.mult))


def stage_rwkv_chunks(nc, g, l):
    STEPS = 14
    H4 = 4
    with ExitStack() as st:
        sem = g.sems.begin(st)
        ps = [st.enter_context(nc.psum_tensor(g.name(f"chunk_ps{d}"), [P, 4, BANK], F32)) for d in range(2)]

        class Stream:
            pass
        streams = []
        for d in range(2):
            s = Stream()
            sb = lambda name, shape: st.enter_context(nc.sbuf_tensor(g.name(f"{name}{d}"), shape, F32))
            s.AR = sb("a_r", [P, 2, 2, P])
            s.bt, s.kt, s.bh, s.kh, s.v = (sb(n, [P, 2, P]) for n in ("b_in", "k_in", "b_end", "k_end", "v_col"))
            s.rows1, s.rows2 = sb("rows_a_b", [P, 4, P]), sb("rows_k_v", [P, 4, P])
            s.A, s.AT, s.A32T, s.A64T = (sb(n, [P, H4, P]) for n in ("A16_", "A16T_", "A32T_", "A64T_"))
            s.MakT, s.MrbT, s.MrkT = (sb(n, [P, H4, P]) for n in ("MakT_", "MrbT_", "MrkT_"))
            s.A2, s.A2T, s.A4, s.A4T = (sb(n, [P, H4, P]) for n in ("A2_", "A2T_", "A4_", "A4T_"))
            s.X, s.XT = (sb(n, [P, H4, P]) for n in ("X_", "XT_"))
            s.A8, s.Q, s.rhs, s.GE = s.A, s.A2, s.AT, s.A4
            s.QT, s.S = sb("QT_", [P, 2, P]), sb("state_", [P, 2, P])
            s.Phi, s.Psi = s.A4T, s.A2T
            s.pe, s.ve, s.ac = sem(f"products{d}"), sem(f"vector_out{d}"), sem(f"scalar_out{d}")
            streams.append(s)
        ready = [sem(f"operands_ready{d}") for d in range(2)]
        v_done, state_zero = sem("v_done"), sem("state_zero")
        flat = lambda t: t.rearrange("p a b -> p (a b)")
        heads = lambda t: t.rearrange("p (h s) -> p h s", h=H4)
        mask = lambda d, m: g.masks[:, (m if d == 0 else m + 5), :].unsqueeze(1).to_broadcast([P, H4, P])
        maskT = lambda d, m: g.masks[:, (m + 5 if d == 0 else m), :].unsqueeze(1).to_broadcast([P, H4, P])
        M16, M32, M64, STRICT, INCL = range(5)
        tile_of = lambda d, n: n if d == 0 else (n ^ 1)

        with nc.Block() as block:
            @block.gpsimd
            def _(po):
                po.sem_clear(g.sems.other)
                for s in streams:
                    po.memset(s.S[:], 0.0).then_inc(state_zero, 1)

            @block.tensor
            def _(pe):
                for n in range(TILES):
                    for t in range(1, STEPS + 1):
                        for d, s in enumerate(streams):
                            b = ps[d]
                            if t == 1:
                                if n == 0:
                                    pe.wait_ge(state_zero, 2)
                                pe.wait_ge(ready[d], n + 1)
                            if n or t > 1:
                                pe.wait_ge(s.ve, n * STEPS + t - 1)
                                pe.wait_ge(s.ac, n * STEPS + t - 1)
                            hp = lambda h: slice(64 * (h // 2), 64 * (h // 2) + 64)
                            if t == 1:
                                for p in range(2):
                                    pe.transpose(b[:, 0, p * P:(p + 1) * P], s.AR[:, p, 0, :], g.ident[:])
                                    pe.transpose(b[:, 0, (2 + p) * P:(3 + p) * P], s.bh[:, p, :], g.ident[:])
                                    pe.transpose(b[:, 1, p * P:(p + 1) * P], s.kh[:, p, :], g.ident[:])
                                    pe.transpose(b[:, 1, (2 + p) * P:(3 + p) * P], s.v[:, p, :], g.ident[:])
                                for h in range(H4):
                                    mm = pe.matmul(b[:, 2 + h // 2, (h % 2) * 256:(h % 2) * 256 + 256], s.bt[hp(h), h % 2, :], flat(s.AR[hp(h), h % 2, :, :]), start=True, stop=True)
                            elif t == 2:
                                for h in range(H4):
                                    pe.matmul(b[:, h // 2, (h % 2) * 256:(h % 2) * 256 + 256], s.kt[hp(h), h % 2, :], flat(s.AR[hp(h), h % 2, :, :]), start=True, stop=True)
                                for h in range(H4):
                                    mm = pe.matmul(b[:, 2 + h // 2, (h % 2) * P:(h % 2 + 1) * P], s.AR[hp(h), h % 2, 0, :], s.bt[hp(h), h % 2, :], start=True, stop=True)
                            elif t in (3, 4, 5, 6, 7, 8, 9, 10, 11):
                                todo = {3: ((0, s.AT, s.A), (1, s.A, s.AT)),
                                        4: ((0, s.A2T, s.A2), (1, s.A2, s.A2T), (2, s.XT, s.A2), (3, s.A2, s.XT)),
                                        5: ((0, s.A4T, s.A4), (2, s.XT, s.A4), (3, s.A4, s.XT)),
                                        6: ((2, s.XT, s.A8), (3, s.A8, s.XT)),
                                        7: ((0, s.A32T, s.X),),
                                        8: ((2, s.XT, s.Q), (3, s.Q, s.XT)),
                                        9: ((0, s.A64T, s.X),),
                                        10: ((3, s.Q, s.XT),),
                                        11: ((0, s.XT, s.rhs),)}[t]
                                for q, lhsT, rhs in todo:
                                    for h in range(H4):
                                        mm = pe.matmul(b[:, q, h * P:(h + 1) * P], lhsT[:, h, :], rhs[:, h, :], start=True, stop=True)
                                if t == 3:
                                    for h in range(H4):
                                        mm = pe.matmul(b[:, 2, h * 64:(h + 1) * 64], s.MakT[:, h, :], s.rows2[:, 2 + h % 2, hp(h)], start=True, stop=True)
                            elif t == 12:
                                G, E = s.GE[:, 0:2, :], s.GE[:, 2:4, :]
                                bh, kh, v = s.rows1[:, 2:4, :], s.rows2[:, 0:2, :], s.rows2[:, 2:4, :]
                                for h in range(H4):
                                    p, c = h % 2, slice((h % 2) * P, (h % 2 + 1) * P)
                                    pe.matmul(b[hp(h), 0, c], G[:, p, hp(h)], s.MrbT[:, h, :], start=True, stop=True)
                                    pe.matmul(b[hp(h), 1, c], E[:, p, hp(h)], s.MrbT[:, h, :], start=True, stop=False)
                                    pe.matmul(b[hp(h), 1, c], v[:, p, hp(h)], s.MrkT[:, h, :], start=False, stop=True)
                                for c in range(2):
                                    r = slice(64 * c, 64 * c + 64)
                                    for p in range(2):
                                        o, o2 = slice(p * P, (p + 1) * P), slice((2 + p) * P, (3 + p) * P)
                                        pe.matmul(b[:, 2 + c, o], G[r, p, :], bh[r, p, :], start=True, stop=True)
                                        pe.matmul(b[:, 2 + c, o2], bh[r, p, :], E[r, p, :], start=True, stop=False)
                                        mm = pe.matmul(b[:, 2 + c, o2], kh[r, p, :], v[r, p, :], start=False, stop=True)
                            else:
                                c = (t - 13) if d == 0 else (14 - t)
                                for p in range(2):
                                    pe.matmul(b[:, 0, p * 64:(p + 1) * 64], s.S[:, p, :], s.QT[:, p, 64 * c:64 * c + 64], start=True, stop=True)
                                    mm = pe.matmul(b[:, 1, p * P:(p + 1) * P], s.Phi[:, 2 * c + p, :], s.S[:, p, :], start=True, stop=True)
                            mm.then_inc(s.pe, 1)

            @block.scalar
            def _(ac):
                for n in range(TILES):
                    for t in range(1, STEPS + 1):
                        for d, s in enumerate(streams):
                            b = ps[d]
                            ac.wait_ge(s.pe, n * STEPS + t)
                            copies = {1: ((flat(s.rows1[:]), b[:, 0, :]), (flat(s.rows2[:]), b[:, 1, :])),
                                      3: ((flat(s.A2[:]), b[:, 0, :]), (flat(s.A2T[:]), b[:, 1, :])),
                                      4: ((flat(s.A4[:]), b[:, 0, :]), (flat(s.A4T[:]), b[:, 1, :])),
                                      5: ((flat(s.A8[:]), b[:, 0, :]),),
                                      7: ((flat(s.Q[:]), b[:, 0, :]),),
                                      9: ((flat(s.Q[:]), b[:, 0, :]),),
                                      11: tuple((s.GE[:, 2 * q:2 * q + 2, :].rearrange("p a (b c) -> p b a c", b=2),
                                                b[:, 0, :].rearrange("p (b a q c) -> p b a q c", b=2, a=2, q=2)[:, :, :, q, :]) for q in range(2))}.get(t, ())
                            if t == 12:
                                tok = slice(tile_of(d, n) * P, tile_of(d, n) * P + P)
                                copies = ((g.S[:, Y_AT[d]:Y_AT[d] + 2, tok], b[:, 1, 0:2 * P].rearrange("p (a c) -> p a c", a=2)),)
                            for dst, src in copies:
                                a = ac.activation(dst, src, ACT.Copy)
                            if copies:
                                a.then_inc(s.ac, 1)
                            else:
                                ac.sem_inc(s.ac, 1)

            @block.vector
            def _(ve):
                step = chained(ve, v_done)

                def operands(n, d):
                    s, i = streams[d], tile_of(d, n)
                    tok = slice(i * P, i * P + P)
                    if n:
                        ve.wait_ge(s.pe, (n - 1) * STEPS + 12)
                    eL, eN, eP = (x[:, d, :, tok] for x in (g.eL, g.eN, g.eP))
                    b, k = g.S[:, B_AT[d]:B_AT[d] + 2, tok], g.S[:, KD_AT[d]:KD_AT[d] + 2, tok]
                    ve.scalar_tensor_tensor(out=s.AR[:, :, 0, :], in0=g.S[:, KK:KK + 2, tok], scalar=-1.0, in1=eP, op0=ALU.mult, op1=ALU.mult)
                    ve.tensor_tensor(s.AR[:, :, 1, :], g.S[:, RR:RR + 2, tok], eL, ALU.mult)
                    ve.tensor_copy(s.v[:], g.S[:, VC:VC + 2, tok])
                    step(ve.tensor_tensor(s.bt[:], b, eN, ALU.mult))
                    step(ve.tensor_tensor(s.kt[:], k, eN, ALU.mult))
                    end = CHUNK - 1 if d == 0 else 0
                    for p in range(2):
                        pe_ = g.eL[:, d, p, i * P + end:i * P + end + CHUNK + 1:CHUNK].unsqueeze(2).to_broadcast([P, 2, CHUNK])
                        split = lambda x: x.rearrange("p (c t) -> p c t", c=2)
                        ve.tensor_tensor(split(s.bh[:, p, :]), split(s.bt[:, p, :]), pe_, ALU.mult)
                        o = ve.tensor_tensor(split(s.kh[:, p, :]), split(s.kt[:, p, :]), pe_, ALU.mult)
                    o.then_inc(ready[d], 1)

                def evacuate(n, t, d):
                    s, b = streams[d], ps[d]
                    ve.wait_ge(s.pe, n * STEPS + t)
                    two = lambda q, x: b[:, q:q + 2, :].rearrange("p a (h x c) -> p (a h) x c", h=2, x=2)[:, :, x, :]
                    idb = g.ident[:].unsqueeze(1).to_broadcast([P, H4, P])
                    if t == 1:
                        step(ve.tensor_tensor(s.AT[:], two(2, 0), maskT(d, M16), ALU.mult))
                        ve.tensor_tensor(s.A32T[:], two(2, 0), maskT(d, M32), ALU.mult)
                        ve.tensor_tensor(s.A64T[:], two(2, 0), maskT(d, M64), ALU.mult)
                        ve.tensor_tensor(s.XT[:], s.AT[:], idb, ALU.add)
                        o = ve.tensor_tensor(s.MrbT[:], two(2, 1), maskT(d, INCL), ALU.mult)
                    elif t == 2:
                        step(ve.tensor_tensor(s.A[:].rearrange("p (a h) c -> p a h c", a=2), b[:, 2:4, 0:2 * P].rearrange("p a (h c) -> p a h c", h=2),
                                              mask(d, M16).rearrange("p (a h) c -> p a h c", a=2), ALU.mult))
                        ve.tensor_tensor(s.MakT[:], two(0, 0), maskT(d, STRICT), ALU.mult)
                        ve.tensor_tensor(s.X[:], s.A[:], idb, ALU.add)
                        o = ve.tensor_tensor(s.MrkT[:], two(0, 1), maskT(d, INCL), ALU.mult)
                    elif t == 3:
                        ve.wait_ge(s.ac, n * STEPS + 1)
                        ve.tensor_copy(s.rhs[:, :, 0:64].rearrange("p (b a) c -> p b a c", b=2), s.rows1[:, 0:2, :].rearrange("p a (b c) -> p b a c", b=2))
                        o = ve.tensor_copy(s.rhs[:, :, 64:P], b[:, 2, 0:256].rearrange("p (h c) -> p h c", h=4))
                    elif t in (4, 5, 6, 8):
                        ve.tensor_tensor(s.X[:], s.X[:], heads(b[:, 2, :]), ALU.add)
                        o = ve.tensor_tensor(s.XT[:], s.XT[:], heads(b[:, 3, :]), ALU.add)
                    elif t == 10:
                        o = ve.tensor_tensor(s.XT[:], s.XT[:], heads(b[:, 3, :]), ALU.add)
                    elif t == 12:
                        i, end = tile_of(d, n), CHUNK - 1 if d == 0 else 0
                        bd = g.pair[:].unsqueeze(1).to_broadcast([P, H4, P])
                        half = lambda x: b[:, 2:4, x * 2 * P:(x + 1) * 2 * P].rearrange("p c (a k) -> p c a k", a=2)
                        cp = lambda x: x.rearrange("p (c a) k -> p c a k", c=2)
                        step(ve.tensor_tensor(cp(s.Phi[:]), half(0), cp(bd), ALU.mult))
                        ve.tensor_tensor(cp(s.Psi[:]), half(1), cp(bd), ALU.mult)
                        for c in range(2):
                            for p in range(2):
                                x = i * P + c * CHUNK + end
                                ve.scalar_tensor_tensor(out=s.Phi[:, 2 * c + p, :], in0=g.ident[:], scalar=g.eL[:, d, p, x:x + 1], in1=s.Phi[:, 2 * c + p, :],
                                                        op0=ALU.mult, op1=ALU.add)
                        o = ve.tensor_tensor(s.QT[:], s.AR[:, :, 1, :], b[:, 0, 0:2 * P].rearrange("p (a c) -> p a c", a=2), ALU.add)
                    elif t >= 13:
                        c = (t - 13) if d == 0 else (14 - t)
                        x = tile_of(d, n) * P + c * CHUNK
                        y = g.S[:, Y_AT[d]:Y_AT[d] + 2, x:x + CHUNK]
                        if t == 13:
                            ve.wait_ge(s.ac, n * STEPS + 12)
                        ve.tensor_tensor(y, y, b[:, 0, 0:P].rearrange("p (a c) -> p a c", a=2), ALU.add)
                        o = ve.tensor_tensor(s.S[:], s.Psi[:, 2 * c:2 * c + 2, :], b[:, 1, 0:2 * P].rearrange("p (a c) -> p a c", a=2), ALU.add)
                    else:
                        ve.sem_inc(s.ve, 1)
                        return
                    o.then_inc(s.ve, 1)

                operands(0, 0)
                operands(0, 1)
                for n in range(TILES):
                    for t in range(1, STEPS + 1):
                        for d in range(2):
                            evacuate(n, t, d)
                            if t == 13 and n + 1 < TILES:
                                operands(n + 1, d)


def stage_rwkv_output(nc, g, l):
    with ExitStack() as st:
        sem = g.sems.begin(st)
        sb = lambda name, shape: st.enter_context(nc.sbuf_tensor(g.name(name), shape, F32))
        gup, y, sq, t = sb("g_up", [P, RW_W]), sb("y_sum", [P, 2, TOK]), sb("y_sq", [P, 2, TOK]), sb("rk", [P, 2, TOK])
        ps = st.enter_context(nc.psum_tensor(g.name("gn_ps"), [P, 8, BANK], F32))
        w_in, v_done, y_done, mu_in, t_done, bonus_in, sq_done, var_in, eps_done, root_done, gate_in = (
            sem(n) for n in ("w_in", "v_done", "y_done", "mean_in", "rk_done", "bonus_in", "sq_done", "var_in", "eps_done", "root_done", "gate_in"))
        par = lambda name, k: g.par[:, l, ROWS[name] + k:ROWS[name] + k + 1]
        Y = lambda d: g.S[:, Y_AT[d]:Y_AT[d] + 2, :]
        KDc = lambda d: g.S[:, KD_AT[d]:KD_AT[d] + 2, :]

        with nc.Block() as block:
            @block.sync
            def _(sp):
                sp.dma_start(gup[:], g.dram["rw_g_up"][l]).then_inc(w_in, 16)

            @block.gpsimd
            def _(po):
                po.sem_clear(g.sems.other)

            @block.tensor
            def _(pe):
                def sums(first, src, done):
                    for p in range(2):
                        mm = pe.matmul(ps[:, first + p, :], g.pair[:], src[:, p, :], start=True, stop=True)
                    mm.then_inc(done, 1)
                pe.wait_ge(y_done, 1)
                sums(0, y, mu_in)
                pe.wait_ge(t_done, 1)
                sums(2, t, bonus_in)
                pe.wait_ge(w_in, 16)
                for p in range(2):
                    mm = pe.matmul(ps[:, 6 + p, :], gup[:, p * P:(p + 1) * P], g.S[:, LORA0 + 2, :], start=True, stop=True)
                mm.then_inc(gate_in, 1)
                pe.wait_ge(sq_done, 1)
                sums(4, sq, var_in)

            @block.scalar
            def _(ac):
                ac.wait_ge(eps_done, 1)
                ac.activation(sq[:], sq[:], ACT.Sqrt).then_inc(root_done, 1)

            @block.vector
            def _(ve):
                step = chained(ve, v_done)
                ve.tensor_tensor(y[:], Y(0), Y(1), ALU.add).then_inc(y_done, 1)
                step(ve.tensor_tensor(t[:], KDc(0), KDc(1), ALU.add))
                for p in range(2):
                    o = ve.scalar_tensor_tensor(out=t[:, p, :], in0=t[:, p, :], scalar=par("rw_r_k", p), in1=g.S[:, RR + p, :], op0=ALU.mult, op1=ALU.mult)
                o.then_inc(t_done, 1)
                ve.wait_ge(mu_in, 1)
                step(ve.scalar_tensor_tensor(out=y[:], in0=ps[:, 0:2, :], scalar=-1.0 / RW_HD, in1=y[:], op0=ALU.mult, op1=ALU.add))
                ve.tensor_tensor(sq[:], y[:], y[:], ALU.mult).then_inc(sq_done, 1)
                ve.wait_ge(bonus_in, 1)
                step(ve.tensor_tensor(t[:], ps[:, 2:4, :], g.S[:, VC:VC + 2, :], ALU.mult))
                ve.wait_ge(var_in, 1)
                ve.tensor_scalar(sq[:], ps[:, 4:6, :], 1.0 / RW_HD, RW_HD * 1e-5, ALU.mult, ALU.add).then_inc(eps_done, 1)
                ve.wait_ge(root_done, 1)
                step(ve.reciprocal(sq[:], sq[:]))
                step(ve.tensor_tensor(y[:], y[:], sq[:], ALU.mult))
                for p in range(2):
                    step(ve.tensor_scalar(y[:, p, :], y[:, p, :], par("rw_ln_w", p), par("rw_ln_b", p), ALU.mult, ALU.add))
                step(ve.tensor_tensor(y[:], y[:], t[:], ALU.add))
                ve.wait_ge(gate_in, 1)
                step(ve.tensor_tensor(g.mix[:, 2:4, :], y[:], ps[:, 6:8, :], ALU.mult))


def stream_of(i):
    return 0 if i >= 2 else 1


def stage_output_projection(nc, g, l, tiles):
    with ExitStack() as st:
        sem = g.sems.begin(st)
        w = st.enter_context(nc.sbuf_tensor(g.name("w_out"), [P, KD, D], F32))
        gate = st.enter_context(nc.sbuf_tensor(g.name("gate1"), [P, 2, D], F32))
        t = st.enter_context(nc.sbuf_tensor(g.name("gated"), [P, D], F32))
        gps = st.enter_context(nc.psum_tensor(g.name("gate_ps"), [P, 2, BANK], F32))
        ps = st.enter_context(nc.psum_tensor(g.name("mixed_ps"), [P, 2, 2, BANK], F32))
        landed, gate_in, gate_out, mm_done, used, v_done = (sem(n) for n in ("w_out_landed", "gate_in", "gate_out", "mm_done", "used", "v_done"))
        halves = [sem(f"w_out_half{k}") for k in range(4)]
        wv = g.dram["w_out"][l].rearrange("(k p) n -> p k n", p=P)

        with nc.Block() as block:
            @block.sync
            def _(sp):
                for q in range(4):
                    sp.dma_start(w[:, 2 * q:2 * q + 2, :], wv[:, 2 * q:2 * q + 2, :]).then_inc(halves[q], 16)

            @block.gpsimd
            def _(po):
                po.sem_clear(g.sems.other)

            @block.tensor
            def _(pe):
                for w_ in range(2):
                    if w_:
                        pe.wait_ge(gate_out, 1)
                    broadcast_row(pe, g, l, gps, 2, w_).then_inc(gate_in, 1)
                for n, i in enumerate(tiles):
                    if n >= 2:
                        pe.wait_ge(used, n - 1)
                    for k in range(KD):
                        if n == 0:
                            pe.wait_ge(halves[k // 2], 16)
                        for j in range(2):
                            mm = pe.matmul(ps[:, n % 2, j, :], g.mix[:, k, i * P:(i + 1) * P], w[:, k, j * BANK:(j + 1) * BANK], start=k == 0, stop=k == KD - 1)
                    mm.then_inc(mm_done, 1)

            @block.scalar
            def _(ac):
                for w_ in range(2):
                    ac.wait_ge(gate_in, w_ + 1)
                    ac.activation(gate[:, w_, :], gps[:].rearrange("p a b -> p (a b)"), ACT.Copy).then_inc(gate_out, 1)

            @block.vector
            def _(ve):
                step = chained(ve, v_done)
                ve.wait_ge(gate_out, 2)
                for n, i in enumerate(tiles):
                    ve.wait_ge(mm_done, n + 1)
                    o = ve.tensor_tensor(t[:], ps[:, n % 2, :, :].rearrange("p a b -> p (a b)"), gate[:, stream_of(i), :], ALU.mult)
                    o.then_inc(used, 1)
                    ve.wait_ge(used, n + 1)
                    step(ve.tensor_tensor(g.X[:, i, :], g.X[:, i, :], t[:], ALU.add))


def stage_peer_queries(nc, g, l, tiles, HT, QT, KT):
    CW, WB = 2, 3
    NT = HEADS * DQ // P
    T0 = tiles[0] * P
    with ExitStack() as st:
        sem = g.sems.begin(st)
        w = st.enter_context(nc.sbuf_tensor(g.name("wq_ring"), [P, WB, KD, CW * P], F32))
        kr = st.enter_context(nc.sbuf_tensor(g.name("key_rows"), [P, 2, HEADS, P], F32))
        ps = st.enter_context(nc.psum_tensor(g.name("q_ps"), [P, 4, BANK], F32))
        kps = st.enter_context(nc.psum_tensor(g.name("key_ps"), [P, 4, BANK], F32))
        landed = [sem(f"wq_landed{b}") for b in range(WB)]
        keys_in, key_tp, key_out, mm_done, evac = (sem(n) for n in ("keys_in", "keys_transposed", "keys_out", "mm_done", "evacuated"))
        wv = g.dram["peer_wq"][l].rearrange("(k p) n -> p k n", p=P)

        with nc.Block() as block:
            @block.sync
            def _(sp):
                for s, name in enumerate(("peer_k1", "peer_k2")):
                    sp.dma_start(kr[:, s, :, :], g.dram[name][l].rearrange("h n d -> n h d")).then_inc(keys_in, 16)
                for n in range(NT // CW):
                    if n >= WB:
                        sp.wait_ge(mm_done, (n - WB + 1) * CW)
                    sp.dma_start(w[:, n % WB, :, :], wv[:, :, n * CW * P:(n + 1) * CW * P]).then_inc(landed[n % WB], 16)

            @block.gpsimd
            def _(po):
                po.sem_clear(g.sems.other)

            @block.tensor
            def _(pe):
                pe.wait_ge(keys_in, 32)
                for c in range(NT):
                    mm = pe.transpose(kps[:, c // 4, (c % 4) * P:(c % 4 + 1) * P], kr[:, c % 2, c // 2, :], g.ident[:])
                    if c % 4 == 3:
                        mm.then_inc(key_tp, 1)
                for j in range(NT):
                    n = j // CW
                    pe.wait_ge(landed[n % WB], 16 * (n // WB + 1))
                    if j >= 4:
                        pe.wait_ge(evac, j - 3)
                    for k in range(KD):
                        mm = pe.matmul(ps[:, j % 4, 0:TOK - T0], w[:, n % WB, k, (j % CW) * P:(j % CW + 1) * P], HT[:, k, T0:TOK], start=k == 0, stop=k == KD - 1)
                    mm.then_inc(mm_done, 1)

            @block.scalar
            def _(ac):
                for j in range(NT):
                    ac.wait_ge(mm_done, j + 1)
                    ac.activation(QT[:, j, T0:TOK], ps[:, j % 4, 0:TOK - T0], ACT.Copy).then_inc(evac, 1)

            @block.vector
            def _(ve):
                for c in range(4):
                    ve.wait_ge(key_tp, c + 1)
                    ve.tensor_copy(KT[:, 4 * c:4 * c + 4, :], kps[:, c, :].rearrange("p (a b) -> p a b", a=4)).then_inc(key_out, 1)


def stage_peer(nc, g, l, tiles, H, QT, KT):
    HH = 2 * HEADS
    N = len(tiles)
    with ExitStack() as st:
        sem = g.sems.begin(st)
        sb = lambda name, shape, dt=F32: st.enter_context(nc.sbuf_tensor(g.name(name), shape, dt))
        sc = sb("scores", [P, HH, P])
        val, idx_u, idx = sb("half_vals", [P, HH, 16]), sb("half_idx_u", [P, HH, 16], U32), sb("half_idx", [P, HH, 16])
        cand = sb("cand", [P, HEADS, 256])
        top, pos, part_u, part = sb("top_vals", [P, HEADS, 16]), sb("top_pos", [P, SLOTS], U32), sb("pos_part_u", [P, 2, SLOTS], U32), sb("pos_part", [P, 2, SLOTS])
        found, total = sb("found", [P, 2, SLOTS]), sb("gate_sum", [P, HEADS])
        gates, experts = sb("gates", [P, 2, SLOTS]), sb("experts", [P, 2, SLOTS], U32)
        ring, rows = sb("expert_rows", [P, RING, D]), sb("row_numbers", [P, 2, RING], U32)
        dots8, dots, weight, diag = sb("dots8", [P, RING]), sb("dots", [P, SLOTS]), sb("weight", [P, SLOTS]), sb("diag", [P, BY_PE, P])
        gate, side_sum = sb("gate2", [P, 2, D]), sb("side_sum", [P, D])
        hot = cand[:].rearrange("p h (k j) -> p (h k) j", j=16)
        gated = cand[:, 0:4, :].rearrange("p a b -> p (a b)")
        sps = st.enter_context(nc.psum_tensor(g.name("score_ps"), [P, 4, BANK], F32))
        acc = st.enter_context(nc.psum_tensor(g.name("expert_sum"), [P, 2, BANK], F32))
        gps = st.enter_context(nc.psum_tensor(g.name("gate2_ps"), [P, 2, BANK], F32))
        ahead = Modulation(nc, g, st, sem, l + 1, 0, gps[0:2, 0, :], buffers=1) if l + 1 < DEPTH else None
        landed, before = g.rows_landed, g.rows_used
        g.rows_used += 2 * N * GROUPS
        free = [sem(f"free{b}") for b in range(RING)]
        s_in, s_out, shifted, exped, selected, gated_done = (sem(n) for n in ("scores_in", "scores_out", "shifted", "exped", "selected", "gates_done"))
        rows_copied, issued, v_go = sem("rows_copied"), sem("issued"), sem("v_go")
        dots_kept, gelu_done, weight_done, diag_done, acc_read = (sem(n) for n in ("dots_kept", "gelu_done", "weight_done", "diag_done", "acc_read"))
        gate_in, gate_out, v_done = sem("gate_in"), sem("gate_out"), sem("v_done")
        table = {0: g.dram["peer_u"].rearrange("l n d -> (l n) d"), 1: g.dram["peer_v"].rearrange("l n d -> (l n) d")}
        flat = lambda t: t.rearrange("p a b -> p (a b)")

        with nc.Block() as block:
            @block.sync
            def _(sp):
                if ahead:
                    ahead.traffic(sp)

            @block.gpsimd
            def _(po):
                po.sem_clear(g.sems.other)
                if ahead:
                    ahead.gain_ones(po)
                for b in range(RING):
                    po.sem_inc(free[b], 2)
                for n in range(N):
                    po.wait_ge(selected, n + 1)
                    for half in range(2):
                        with po.Fori(0, GROUPS // 2) as pair:
                            for side in range(2):
                                k = pair * 2 + side
                                use = k + (n * 2 + half) * GROUPS
                                for b in range(RING):
                                    po.wait_ge(free[b], use + 1)
                                    po.sem_inc(issued, 1)
                                po.tensor_copy(rows[:, side, :], experts[:, n % 2, bass.ds(k * RING, RING)]).then_inc(rows_copied, 1)
                                po.wait_ge(rows_copied, use + 1)
                                po.sem_inc(issued, 1)
                                for b in range(RING):
                                    po.wait_ge(free[b], use + 2)
                                    po.sem_inc(issued, 1)
                                    po.indirect_dma_start(out=ring[:, b, :], out_offset=None, in_=table[half],
                                                          in_offset=bass.IndirectOffsetOnAxis(ap=rows[:, side, b:b + 1], axis=0)).then_inc(landed[b], 16)

            @block.vector
            def _(ve):
                step = chained(ve, v_done)

                def top16(src, vals, where):
                    step(ve.max(vals[:, 0:8], src))
                    step(ve.max_index(where[:, 0:8], vals[:, 0:8], src))
                    step(ve.match_replace(src, vals[:, 0:8], src, -3.0e38))
                    step(ve.max(vals[:, 8:16], src))
                    step(ve.max_index(where[:, 8:16], vals[:, 8:16], src))

                def select_half(c):
                    top16(sc[:, c, :], val[:, c, :], idx_u[:, c, :])

                def select_head(h):
                    if h == 0:
                        step(ve.tensor_copy(idx[:], idx_u[:]))
                        halves = val[:].rearrange("p (h s) k -> p h s k", s=2)
                        step(ve.tensor_tensor(cand[:].rearrange("p h (a b) -> p h a b", a=16), halves[:, :, 0, :].unsqueeze(3).to_broadcast([P, HEADS, 16, 16]),
                                              halves[:, :, 1, :].unsqueeze(2).to_broadcast([P, HEADS, 16, 16]), ALU.add))
                    top16(cand[:, h, :], top[:, h, :], pos[:, h * 16:h * 16 + 16])

                def select_rows(n):
                    gt = gates[:, n % 2, :].rearrange("p (h k) -> p h k", h=HEADS)
                    ve.tensor_tensor(gt, top[:], top[:, :, 0:1].to_broadcast([P, HEADS, 16]), ALU.subtract).then_inc(shifted, 1)
                    step(ve.tensor_scalar(part_u[:, 0, :], pos[:], 4, None, ALU.logical_shift_right))
                    step(ve.tensor_scalar(part_u[:, 1, :], pos[:], 15, None, ALU.bitwise_and))
                    step(ve.tensor_copy(part[:], part_u[:]))
                    lists = idx[:].rearrange("p (h s) k -> p h s k", s=2)
                    for s in range(2):
                        step(ve.tensor_tensor(hot, g.iota[:].unsqueeze(1).to_broadcast([P, SLOTS, 16]), part[:, s, :].unsqueeze(2).to_broadcast([P, SLOTS, 16]), ALU.is_equal))
                        h4 = hot.rearrange("p (h k) j -> p h k j", h=HEADS)
                        step(ve.tensor_tensor(h4, h4, lists[:, :, s, :].unsqueeze(2).to_broadcast([P, HEADS, 16, 16]), ALU.mult))
                        step(ve.tensor_reduce(found[:, s, :], hot, AX.X, ALU.add))
                    step(ve.tensor_scalar(found[:, 0, :], found[:, 0, :], float(NKEYS), float(l * NEXP), ALU.mult, ALU.add))
                    if n >= 2:
                        ve.wait_ge(rows_copied, (n - 1) * 2 * GROUPS)
                    ve.tensor_tensor(experts[:, n % 2, :], found[:, 0, :], found[:, 1, :], ALU.add).then_inc(selected, 1)

                def select_piece(n, k):
                    if k == 0:
                        ve.wait_ge(s_out, n + 1)
                    for c in range(3 * k, min(3 * k + 3, HH)):
                        select_half(c)
                    for h in range(2 * (k - 6), min(2 * (k - 6) + 2, HEADS)) if k >= 6 else ():
                        select_head(h)
                    if k == 10:
                        select_rows(n)

                def softmax(n):
                    gt = gates[:, n % 2, :].rearrange("p (h k) -> p h k", h=HEADS)
                    ve.wait_ge(exped, n + 1)
                    step(ve.tensor_reduce(total[:], gt, AX.X, ALU.add))
                    step(ve.reciprocal(total[:], total[:]))
                    step(ve.tensor_tensor(gt, gt, total[:].unsqueeze(2).to_broadcast([P, HEADS, 16]), ALU.mult))

                for k in range(GROUPS):
                    select_piece(0, k)
                softmax(0)
                ve.wait_ge(gate_out, 2)
                for n, i in enumerate(tiles):
                    with ve.Fori(0, GROUPS) as k:
                        use = k + n * 2 * GROUPS
                        for b in range(RING):
                            ve.wait_ge(landed[b], 16 * (use + before + 1))
                            ve.tensor_tensor_reduce(ring[:, b, :], ring[:, b, :], H[:, i, :], 1.0, 0.0, ALU.mult, ALU.add, dots8[:, b:b + 1]).then_inc(free[b], 1)
                        ve.wait_ge(free[RING - 1], use + 3)
                        ve.sem_inc(v_go, 1)
                        ve.tensor_copy(dots[:, bass.ds(k * RING, RING)], dots8[:]).then_inc(dots_kept, 1)
                        ve.wait_ge(dots_kept, k + n * GROUPS + 1)
                        ve.sem_inc(v_go, 1)
                    ve.wait_ge(gelu_done, n + 1)
                    ve.tensor_tensor(weight[:], dots[:], gates[:, n % 2, :], ALU.mult).then_inc(weight_done, 1)
                    ve.wait_ge(weight_done, n + 1)
                    for k in range(GROUPS):
                        if n + 1 < N:
                            select_piece(n + 1, k)
                        use = k + (2 * n + 1) * GROUPS
                        for b in range(BY_PE, RING):
                            ve.wait_ge(landed[b], 16 * (use + before + 1))
                            w = weight[:, k * RING + b:k * RING + b + 1]
                            if k == 0 and b == BY_PE:
                                o = ve.tensor_scalar(side_sum[:], ring[:, b, :], w, None, ALU.mult)
                            else:
                                o = ve.scalar_tensor_tensor(out=side_sum[:], in0=ring[:, b, :], scalar=w, in1=side_sum[:], op0=ALU.mult, op1=ALU.add)
                            o.then_inc(free[b], 1)
                            ve.wait_ge(free[b], use + 3)
                    if ahead and n == 0:
                        ahead.finish(ve)
                    ve.wait_ge(free[BY_PE - 1], (2 * n + 2) * GROUPS + 2)
                    ve.tensor_tensor(gated, flat(acc[:]), side_sum[:], ALU.add).then_inc(acc_read, 1)
                    ve.wait_ge(acc_read, n + 1)
                    step(ve.tensor_tensor(gated, gated, gate[:, stream_of(i), :], ALU.mult))
                    step(ve.tensor_tensor(g.X[:, i, :], g.X[:, i, :], gated, ALU.add))
                    if n + 1 < N:
                        softmax(n + 1)

            @block.scalar
            def _(ac):
                def scores_out(n):
                    ac.wait_ge(s_in, n + 1)
                    if n:
                        ac.wait_ge(selected, n)
                    for q in range(4):
                        a = ac.activation(sc[:, 4 * q:4 * q + 4, :], sps[:, q, :].rearrange("p (a b) -> p a b", a=4), ACT.Copy)
                    a.then_inc(s_out, 1)

                def exps(n):
                    ac.wait_ge(shifted, n + 1)
                    ac.activation(gates[:, n % 2, :], gates[:, n % 2, :], ACT.Exp).then_inc(exped, 1)

                scores_out(0)
                exps(0)
                for w in range(2):
                    ac.wait_ge(gate_in, w + 1)
                    ac.activation(gate[:, w, :], flat(gps[:]), ACT.Copy).then_inc(gate_out, 1)
                for n in range(N):
                    if n + 1 < N:
                        scores_out(n + 1)
                    if ahead and n == 0:
                        for m in range(ahead.count):
                            ahead.take(ac, m)
                    ac.wait_ge(dots_kept, (n + 1) * GROUPS)
                    ac.activation(dots[:], dots[:], ACT.Gelu).then_inc(gelu_done, 1)
                    ac.wait_ge(weight_done, n + 1)
                    with ac.Fori(0, GROUPS) as k:
                        for b in range(BY_PE):
                            ac.wait_ge(free[b], k + (2 * n + 1) * GROUPS + 2)
                            ac.activation(diag[:, b, :], g.ident[:], ACT.Copy, scale=weight[:, bass.ds(k * RING + b, 1)]).then_inc(diag_done, 1)
                    if n + 1 < N:
                        exps(n + 1)

            @block.tensor
            def _(pe):
                def scores(n):
                    if n:
                        pe.wait_ge(s_out, n)
                    for c in range(HH):
                        mm = pe.matmul(sps[:, c // 4, (c % 4) * P:(c % 4 + 1) * P], QT[:, c, tiles[n] * P:(tiles[n] + 1) * P], KT[:, c, :], start=True, stop=True)
                    mm.then_inc(s_in, 1)

                def group(n, k, first, last):
                    use = k + (n * 2 + 1) * GROUPS
                    for b in range(BY_PE):
                        pe.wait_ge(landed[b], 16 * (use + before + 1))
                        pe.wait_ge(diag_done, (k + n * GROUPS) * BY_PE + b + 1)
                        for j in range(2):
                            mm = pe.matmul(acc[:, j, :], diag[:, b, :], ring[:, b, j * BANK:(j + 1) * BANK], start=first and b == 0, stop=last and b == BY_PE - 1)
                        mm.then_inc(free[b], 1)

                scores(0)
                for w in range(2):
                    if w:
                        pe.wait_ge(gate_out, 1)
                    broadcast_row(pe, g, l, gps, 5, w).then_inc(gate_in, 1)
                for n in range(N):
                    if n + 1 < N:
                        scores(n + 1)
                    if ahead and n == 0:
                        pe.wait_ge(gate_out, 2)
                        for m in range(ahead.count):
                            ahead.product(pe, m)
                    if n:
                        pe.wait_ge(acc_read, n)
                    group(n, 0, True, False)
                    with pe.Fori(1, GROUPS - 1) as k:
                        group(n, k, False, False)
                    group(n, GROUPS - 1, False, True)


def stage_final_norm(nc, g, out):
    with ExitStack() as st:
        sem = g.sems.begin(st)
        sb = lambda name, shape: st.enter_context(nc.sbuf_tensor(g.name(name), shape, F32))
        gain, sq, ms, y = sb("final_gain", [P, D]), sb("squares", [P, 2, D]), sb("mean_square", [P, 2]), sb("y", [P, 2, D])
        gain_in, ms_done, eps_done, root_done, v_done, y_done = (sem(n) for n in ("gain_in", "ms_done", "eps_done", "root_done", "v_done", "y_done"))
        rows = out[0].rearrange("(i p) d -> i p d", p=P)

        with nc.Block() as block:
            @block.sync
            def _(sp):
                sp.dma_start(gain[:], g.dram["final_g"].rearrange("(a n) -> a n", a=1).to_broadcast([P, D])).then_inc(gain_in, 16)
                for i in range(2):
                    sp.wait_ge(y_done, i + 1)
                    sp.dma_start(rows[i], y[:, i, :]).then_inc(g.stored, 16)
                sp.wait_ge(g.stored, 32)

            @block.scalar
            def _(ac):
                for i in range(2):
                    ac.activation(sq[:, i, :], g.X[:, 2 + i, :], ACT.Square, scale=float(D) ** -0.5, accum_out=ms[:, i:i + 1]).then_inc(ms_done, 1)
                ac.wait_ge(eps_done, 1)
                ac.activation(ms[:], ms[:], ACT.Sqrt).then_inc(root_done, 1)

            @block.vector
            def _(ve):
                step = chained(ve, v_done)
                ve.wait_ge(ms_done, 2)
                ve.tensor_scalar(ms[:], ms[:], 1e-6, None, ALU.add).then_inc(eps_done, 1)
                ve.wait_ge(root_done, 1)
                step(ve.reciprocal(ms[:], ms[:]))
                ve.wait_ge(gain_in, 16)
                for i in range(2):
                    ve.scalar_tensor_tensor(out=y[:, i, :], in0=g.X[:, 2 + i, :], scalar=ms[:, i:i + 1], in1=gain[:], op0=ALU.mult, op1=ALU.mult).then_inc(y_done, 1)


def program(nc, dram, out):
    with ExitStack() as st:
        g = Shared()
        g.rows_landed, g.rows_used = [st.enter_context(nc.semaphore(f"expert_rows_landed{b}")) for b in range(RING)], 0
        g.dram, g.stored, g.sems = dram, st.enter_context(nc.semaphore("output_stored")), Semaphores(nc)
        sb = lambda name, shape, dt=F32: st.enter_context(nc.sbuf_tensor(g.name(name), shape, dt))
        g.X = sb("X", [P, TILES, D])
        g.mod = [[sb("mod_a", [4, D]), sb("mod_b", [8, D])] for _ in range(DEPTH)]
        g.one = sb("one", [8, 2])
        g.par = sb("par", [P, DEPTH, P])
        g.omka = sb("one_minus_k_a", [P, DEPTH, 2])
        g.cond = sb("cond", [P, KD, 2])
        g.ident, g.pair, g.rot, g.swap = (sb(n, [P, P]) for n in ("ident", "pair", "rot", "swap"))
        g.rope = sb("rope", [P, 2, SEQ])
        g.band = sb("band", [P, 2, 2 * SEQ])
        g.ones = sb("ones", [P, P])
        g.masks = sb("masks", [P, 10, P])
        g.iota = sb("iota", [P, 16])
        g.sink = sb("sink", [P, DEPTH, AT_HQ])
        g.sink8 = sb("sink8", [P, DEPTH, AT_HQ])
        stage_constants(nc, g)
        for l in range(DEPTH):
            done = [2, 3] if l == DEPTH - 1 else [0, 1, 2, 3]
            with ExitStack() as mixer:
                keep = lambda name, shape, dt=F32: mixer.enter_context(nc.sbuf_tensor(g.name(name), shape, dt))
                g.S = keep("S", [P, IN_TILES, TOK])
                with ExitStack() as front:
                    HT = front.enter_context(nc.sbuf_tensor(g.name("HT"), [P, KD, TOK], F32))
                    stage_norm(nc, g, l, [0, 1, 2, 3], 0, None, HT)
                    stage_input_projection(nc, g, l, HT)
                g.mix = keep("mix", [P, KD, TOK])
                stage_hyena(nc, g, l)
                stage_attention(nc, g, l, done)
                with ExitStack() as rwkv:
                    g.eL, g.eN, g.eP = (rwkv.enter_context(nc.sbuf_tensor(g.name(n), [P, 2, 2, TOK], F32)) for n in ("decay_in", "decay_out", "decay_before"))
                    stage_rwkv_operands(nc, g, l)
                    stage_rwkv_chunks(nc, g, l)
                    stage_rwkv_output(nc, g, l)
                stage_output_projection(nc, g, l, done)
            with ExitStack() as peer:
                keep = lambda name, shape: peer.enter_context(nc.sbuf_tensor(g.name(name), shape, F32))
                H, QT, KT = keep("H", [P, TILES, D]), keep("QT", [P, 2 * HEADS, TOK]), keep("KT", [P, 2 * HEADS, P])
                with ExitStack() as columns:
                    HT = columns.enter_context(nc.sbuf_tensor(g.name("HT2"), [P, KD, TOK], F32))
                    stage_norm(nc, g, l, done, 3, H, HT)
                    stage_peer_queries(nc, g, l, done, HT, QT, KT)
                stage_peer(nc, g, l, done, H, QT, KT)
        stage_final_norm(nc, g, out)


_INS = ['x', 'c', 'ctx', 'c_ctx', 'mod_w', 'mod_b', 'norm1_g', 'norm2_g', 'w_in', 'conv_w', 'conv_b', 'hy_w1', 'hy_b1',
        'hy_w2', 'hy_b2', 'hy_w3', 'hy_b3', 'hy_freq', 'hy_bias', 'rw_w0', 'rw_w_up', 'rw_a0', 'rw_a_up', 'rw_g_up',
        'rw_k_k', 'rw_k_a', 'rw_r_k', 'rw_ln_w', 'rw_ln_b', 'attn_sink', 'hy_out_g', 'at_out_g', 'w_out', 'peer_wq',
        'peer_k1', 'peer_k2', 'peer_u', 'peer_v', 'final_g']
_OUT = (1, SEQ, D)


def kernel(**inputs):
    import numpy as _np
    import concourse.bacc as _bacc
    from concourse import mybir as _mybir
    from concourse.bass_utils import run_bass_kernel_spmd as _run

    nc = _bacc.Bacc("TRN2", target_bir_lowering=False, num_devices=1)
    arrays, dram = {}, {}
    for name in _INS:
        arrays[f"in_{name}"] = _np.ascontiguousarray(inputs[name])
    for name, a in host_constants().items():
        arrays[f"in_{name}"] = a
    for name, a in arrays.items():
        dram[name[3:]] = nc.dram_tensor(name, a.shape, _mybir.dt.from_np(a.dtype), kind="ExternalInput").ap()
    out = nc.dram_tensor("out_0", _OUT, _mybir.dt.float32, kind="ExternalOutput").ap()
    program(nc, dram, out)
    r = _run(nc, [arrays], core_ids=[0])
    return r.results[0]["out_0"]
```

```python
from contextlib import ExitStack

import numpy as np

import concourse.bass as bass
from concourse import mybir

F32 = mybir.dt.float32
U32 = mybir.dt.uint32
I32 = mybir.dt.int32
ALU = mybir.AluOpType
ACT = mybir.ActivationFunctionType
AX = mybir.AxisListType

P = 128
D = 1024
DEPTH = 2
SEQ = 256
TOK = 2 * SEQ
TILES = TOK // P
KD = D // P
BANK = 512

HY_CH, HY_EMB, HY_HID = 256, 33, 64
RW_W, RW_HD = 256, 64
AT_HQ, AT_HD, AT_W = 8, 64, 512
IN_W = 2688
IN_TILES = IN_W // P
CONV_TILES = 12
LORA0, Q0, K0, V0 = 12, 15, 19, 20
CHUNK = 64
NCHUNK = TOK // CHUNK
DECAY = float(np.exp(-0.5))
HEADS, NKEYS, TOPK, DQ = 8, 128, 16, 256
NEXP = NKEYS * NKEYS
SLOTS = HEADS * TOPK
RING = 8
GROUPS = SLOTS // RING
BY_PE = 6
BIG = 1e30
TWO_PI = 2.0 * float(np.pi)
PI_BELOW = 3.1415925

ROWS = {}
_n = 0
for _name, _count in (("conv_w", 36), ("conv_b", 12), ("rw_w0", 4), ("rw_a0", 4), ("rw_k_k", 2), ("rw_k_a", 2),
                      ("rw_r_k", 2), ("rw_ln_w", 2), ("rw_ln_b", 2), ("hy_bias", 2), ("hy_out_g", 2),
                      ("at_out_g", 4), ("hy_b1", 1), ("hy_b2", 1), ("hy_freq", 2)):
    ROWS[_name] = _n
    _n += _count
NROWS = _n


def host_constants():
    f = np.float64
    j = np.arange(SEQ, dtype=f)
    t32 = np.arange(SEQ, dtype=np.float32) / np.float32(SEQ - 1)
    bands = np.linspace(1e-4, (HY_EMB - 1) // 2 - 1, (HY_EMB - 1) // 2, dtype=np.float32)
    ang = (np.float32(TWO_PI) * np.arange(SEQ, dtype=np.float32)[:, None] * bands[None, :] / np.float32(SEQ)).astype(f)
    emb = np.concatenate([t32[:, None].astype(f), np.cos(ang), -np.sin(ang)], axis=1).T
    deltas = np.abs(np.linspace(np.log(1e-2) / 1.5, np.log(1e-2) / 0.3, HY_CH, dtype=np.float32)).astype(f)
    window = np.exp(-t32.astype(f)[:, None] * deltas[None, :]) + 0.05
    w = (np.arange(SEQ, dtype=f) + 0.5) * TWO_PI / (2 * SEQ)
    cos, sin = np.cos(j[:, None] * w[None, :]), np.sin(j[:, None] * w[None, :])
    two_sided = np.stack([window, np.where(j[:, None] == 0, 0.0, window)], axis=1)
    tiles = lambda m: m.reshape(2, P, SEQ).transpose(1, 0, 2)
    dft = np.stack([tiles(cos), tiles(sin), tiles(cos.T / SEQ), tiles(sin.T / SEQ)], axis=1)
    t, s = np.meshgrid(np.arange(P), np.arange(P), indexing="ij")
    same = lambda n: (t // n) == (s // n)
    low = (s < t) & same(64)
    masks = [low & same(16), low & same(32) & ~same(16), low & ~same(32), low, (s <= t) & same(64)]
    masks = np.stack([m for m in masks] + [m.T for m in masks], axis=1).astype(f)
    head_pair = (t // 64 == s // 64).astype(f)
    d = np.arange(P) % 64
    inv = (10000.0 ** (-np.arange(16, dtype=np.float32) / np.float32(16))).astype(f)[d % 16]
    pos = np.where((d < 32)[:, None], (np.arange(SEQ) // 64)[None, :], (np.arange(SEQ) % 64)[None, :])
    rope = np.stack([np.cos(pos * inv[:, None]), np.sin(pos * inv[:, None])], axis=1)
    rot = np.zeros((P, P), f)
    for m in range(P):
        rot[m + 16 if m % 32 < 16 else m - 16, m] = -1.0 if m % 32 < 16 else 1.0
    swap = np.zeros((P, P), f)
    swap[(np.arange(P) + 64) % P, np.arange(P)] = 1.0
    q, k = np.arange(SEQ).reshape(2, P), np.arange(SEQ)
    band = np.where(np.abs(q[:, :, None] - k[None, None, :]) <= 128, 0.0, -BIG).transpose(1, 0, 2)
    band = np.concatenate([np.zeros_like(band), band], axis=2)
    one = np.zeros((8, 2), f)
    one[2:4, 0], one[4:6, 1] = 1.0, 1.0
    iota16 = np.tile(np.arange(16, dtype=f), (P, 1))
    out = dict(k_emb=emb, k_window=two_sided.reshape(2, P, 2 * HY_CH).transpose(1, 0, 2), k_dft=dft, k_masks=masks,
               k_pair=head_pair, k_rope=rope, k_rot=rot, k_swap=swap, k_band=band, k_iota=iota16, k_one=one,
               k_ident=np.eye(P))
    return {n: np.ascontiguousarray(a.astype(np.float32)) for n, a in out.items()}


class Semaphores:

    def __init__(self, nc, per_bank=70):
        self.nc, self.turn = nc, 0
        first = min(nc.free_semaphores)
        self.banks = [range(first, first + per_bank), range(first + per_bank, first + 2 * per_bank)]

    def begin(self, stack):
        mine, self.other = self.banks[self.turn], self.banks[1 - self.turn]
        self.turn = 1 - self.turn
        nums = iter(mine)

        def sem(name):
            s = self.nc.alloc_semaphore(name, num=next(nums))
            stack.callback(self.nc.release_semaphore, s)
            return s
        return sem


def chained(eng, done):
    count = [0]

    def step(instruction, lag=0):
        count[0] += 1
        instruction.then_inc(done, 1)
        if count[0] > lag:
            eng.wait_ge(done, count[0] - lag)
    step.settle = lambda: eng.wait_ge(done, count[0])
    return step


class Shared:

    def __init__(self):
        self.uses = {}

    def name(self, base):
        self.uses[base] = self.uses.get(base, 0) + 1
        return f"{base}_{self.uses[base]}"


def stage_constants(nc, g):
    with ExitStack() as st:
        sem = g.sems.begin(st)
        rows = st.enter_context(nc.sbuf_tensor(g.name("param_rows"), [P, DEPTH, P], F32))
        crow = st.enter_context(nc.sbuf_tensor(g.name("cond_rows"), [2 * KD, P], F32))
        ps = st.enter_context(nc.psum_tensor(g.name("param_cols_ps"), [P, 4, BANK], F32))
        mod_ps = st.enter_context(nc.psum_tensor(g.name("mod_ps"), [P, BANK], F32))
        mod_w = st.enter_context(nc.sbuf_tensor(g.name("mod_w"), [P, 3, KD, BANK], F32))
        mod = Modulation(nc, g, st, sem, 0, 0, mod_ps[0:2, :], mod_w[:])
        cond_in, cond_done = sem("cond_in"), sem("cond_done")
        loaded, zeroed, rows_in, tp_done = sem("loaded"), sem("zeroed"), sem("rows_in"), sem("tp_done")
        v_done, silu_done = sem("v_done"), sem("silu_done")
        consts = [(g.ident, "k_ident"), (g.masks, "k_masks"),
                  (g.pair, "k_pair"), (g.rope, "k_rope"), (g.rot, "k_rot"), (g.swap, "k_swap"), (g.band, "k_band"),
                  (g.iota, "k_iota"), (g.one, "k_one")]
        wide = []
        for l in range(DEPTH):
            for name, r in ROWS.items():
                src = g.dram[name][l]
                if name in ("hy_b1", "hy_b2"):
                    wide.append((rows[r:r + 1, l, 0:64], src.rearrange("(a n) -> a n", a=1)))
                elif name == "hy_freq":
                    wide.append((rows[r:r + 2, l, 0:64], src))
                else:
                    if name == "conv_w":
                        flat = src.rearrange("k (a n) -> (k a) n", n=P)
                    elif name in ("rw_w0", "rw_a0"):
                        flat = src.rearrange("k (a n) -> (k a) n", n=P)
                    elif name == "rw_r_k":
                        flat = src.rearrange("(a h) n -> a (h n)", h=2)
                    else:
                        flat = src.rearrange("(a n) -> a n", n=P)
                    wide.append((rows[r:r + flat.shape[0], l, :], flat))
        cond_rows = [(crow[0:KD, :], g.dram["c"].rearrange("b (a n) -> (b a) n", n=P)),
                     (crow[KD:2 * KD, :], g.dram["c_ctx"].rearrange("(a n) -> a n", n=P))]

        with nc.Block() as block:
            @block.sync
            def _(sp):
                sp.dma_start(g.ident[:], g.dram["k_ident"]).then_inc(cond_in, 16)
                for dst, src in cond_rows:
                    sp.dma_start(dst, src).then_inc(cond_in, 16)
                mod.first_loads(sp)
                sp.wait_ge(zeroed, 1)
                for dst, src in wide:
                    sp.dma_start(dst, src).then_inc(rows_in, 16)
                mod.later_traffic(sp)

            @block.scalar
            def _(ac):
                ac.wait_ge(tp_done, 1)
                ac.activation(g.cond[:], ps[:, DEPTH, 0:2 * KD].rearrange("p (w k) -> p k w", w=2), ACT.Sigmoid).then_inc(silu_done, 1)
                ac.dma_start(g.X[:, 0:2, :], g.dram["ctx"][0].rearrange("(i p) d -> p i d", p=P)).then_inc(loaded, 16)
                ac.dma_start(g.X[:, 2:4, :], g.dram["x"][0].rearrange("(i p) d -> p i d", p=P)).then_inc(loaded, 16)
                for dst, name in consts[1:]:
                    ac.dma_start(dst[:], g.dram[name]).then_inc(loaded, 16)
                for l in range(DEPTH):
                    ac.dma_start(g.sink[:, l, :], g.dram["attn_sink"][l:l + 1, :].to_broadcast([P, AT_HQ])).then_inc(loaded, 16)
                for n in range(mod.count):
                    mod.take(ac, n)

            @block.gpsimd
            def _(po):
                po.sem_clear(g.sems.other)
                mod.gain_ones(po)
                po.memset(rows[:], 0.0).then_inc(zeroed, 1)
                po.memset(g.ones[:], 1.0)

            @block.tensor
            def _(pe):
                pe.wait_ge(cond_in, 16 * (len(cond_rows) + 1))
                pe.transpose(ps[:, DEPTH, 0:2 * KD], crow[:, :], g.ident[0:2 * KD, 0:2 * KD]).then_inc(tp_done, 1)
                pe.wait_ge(cond_done, 1)
                for n in range(mod.count):
                    mod.product(pe, n)
                pe.wait_ge(rows_in, 16 * len(wide))
                for l in range(DEPTH):
                    pe.transpose(ps[:, l, 0:P], rows[:, l, :], g.ident[:]).then_inc(tp_done, 1)

            @block.vector
            def _(ve):
                step = chained(ve, v_done)
                ve.wait_ge(silu_done, 1)
                (ve.tensor_tensor(g.cond[:], g.cond[:], ps[:, DEPTH, 0:2 * KD].rearrange("p (w k) -> p k w", w=2), ALU.mult)).then_inc(cond_done, 1)
                for l in range(DEPTH):
                    ve.wait_ge(tp_done, 2 + l)
                    step(ve.tensor_copy(g.par[:, l, :], ps[:, l, 0:P]))
                for l in range(DEPTH):
                    a = ROWS["rw_k_a"]
                    step(ve.tensor_scalar(g.omka[:, l, :], g.par[:, l, a:a + 2], -1.0, 1.0, ALU.mult, ALU.add))
                ve.wait_ge(loaded, 16 * (2 + len(consts) - 1 + DEPTH))
                step(ve.tensor_scalar(g.sink8[:], g.sink[:], float(AT_HD) ** 0.5, None, ALU.mult))
                mod.finish(ve)


class Modulation:

    def __init__(self, nc, g, st, sem, l, which, ps, w):
        self.g, self.l, self.which, self.ps, self.w, self.WB = g, l, which, ps, w, w.shape[1]
        self.first = (0, 2 * D // BANK)[which]
        self.count = (2 * D // BANK, 4 * D // BANK)[which]
        self.rows = K = (4, 8)[which]
        sb = lambda name, shape: st.enter_context(nc.sbuf_tensor(g.name(name), shape, F32))
        self.bias, self.gain, self.pair = sb("mod_bias", [K, D]), sb("mod_gain", [K, D]), sb("mod_pair", [2, 2, BANK])
        self.out = g.mod[l][which]
        self.landed = [sem(f"mod_w_landed{b}") for b in range(self.WB)]
        self.moved = [sem(f"mod_moved{b}") for b in range(2)]
        self.ones_set, self.rows_in, self.product_done, self.taken, self.finished = (
            sem(n) for n in ("mod_ones_set", "mod_rows_in", "mod_product_done", "mod_taken", "mod_finished"))

    def gain_ones(self, eng):
        eng.memset(self.gain[:], 1.0).then_inc(self.ones_set, 1)

    def load_rows(self, dma):
        part = 0 if self.which == 0 else 2
        for q in range(self.rows // 2):
            src = self.g.dram["mod_b"][self.l:self.l + 1, (part + q) * D:(part + q + 1) * D]
            dma.dma_start(self.bias[2 * q:2 * q + 2, :], src.to_broadcast([2, D])).then_inc(self.rows_in, 16)
        r = (2, 4)[self.which]
        dma.wait_ge(self.ones_set, 1)
        dma.dma_start(self.gain[r:r + 2, :], self.g.dram[f"norm{self.which + 1}_g"][self.l:self.l + 1, :].to_broadcast([2, D])).then_inc(self.rows_in, 16)

    def load(self, dma, n):
        if n >= self.WB:
            dma.wait_ge(self.product_done, n - self.WB + 1)
        wv = self.g.dram["mod_w"][self.l].rearrange("(k p) n -> p k n", p=P)
        c = (self.first + n) * BANK
        dma.dma_start(self.w[:, n % self.WB, :, :], wv[:, :, c:c + BANK]).then_inc(self.landed[n % self.WB], 16)

    def product(self, pe, n):
        pe.wait_ge(self.landed[n % self.WB], 16 * (n // self.WB + 1))
        if n:
            pe.wait_ge(self.taken, n)
        for k in range(KD):
            mm = pe.matmul(self.ps, self.g.cond[:, k, :], self.w[:, n % self.WB, k, :], start=k == 0, stop=k == KD - 1)
        mm.then_inc(self.product_done, 1)

    def take(self, ac, n):
        ac.wait_ge(self.product_done, n + 1)
        if n >= 2:
            ac.wait_ge(self.moved[n % 2], 16 * (n // 2))
        ac.activation(self.pair[:, n % 2, :], self.ps, ACT.Copy).then_inc(self.taken, 1)

    def move(self, dma, n):
        dma.wait_ge(self.taken, n + 1)
        q, half = n // 2, n % 2
        dma.dma_start(self.out[2 * q:2 * q + 2, half * BANK:(half + 1) * BANK], self.pair[:, n % 2, :]).then_inc(self.moved[n % 2], 16)

    def traffic(self, dma):
        self.first_loads(dma)
        self.later_traffic(dma)

    def first_loads(self, dma):
        for n in range(min(self.WB, self.count)):
            self.load(dma, n)
        self.load_rows(dma)

    def later_traffic(self, dma):
        for n in range(self.count):
            self.move(dma, n)
            if n + self.WB < self.count:
                self.load(dma, n + self.WB)

    def finish(self, ve):
        ve.wait_ge(self.rows_in, 16 * (self.rows // 2 + 1))
        for b in range(2):
            ve.wait_ge(self.moved[b], 16 * (self.count // 2))
        K = self.rows
        ve.scalar_tensor_tensor(out=self.out[:], in0=self.out[:], scalar=self.g.one[0:K, self.which:self.which + 1], in1=self.bias[:],
                                op0=ALU.add, op1=ALU.add).then_inc(self.finished, 1)
        ve.wait_ge(self.finished, 1)
        ve.tensor_tensor(self.out[:], self.out[:], self.gain[:], ALU.mult).then_inc(self.finished, 1)


def broadcast_row(pe, g, l, ps, part, w):
    which, K = (0, 4) if part < 2 else (1, 8)
    row = 2 * (part - 2 * which) + w
    for j in range(2):
        mm = pe.matmul(ps[:, j, :], g.ident[0:K, row:row + 1].to_broadcast([K, P]), g.mod[l][which][:, j * BANK:(j + 1) * BANK], start=True, stop=True)
    return mm


def stage_norm(nc, g, l, tiles, part, H, HT):
    with ExitStack() as st:
        sem = g.sems.begin(st)
        h = H if H is not None else st.enter_context(nc.sbuf_tensor(g.name("h_rows"), [P, TILES, D], F32))
        sq = st.enter_context(nc.sbuf_tensor(g.name("squares"), [P, 2, D], F32))
        ms = st.enter_context(nc.sbuf_tensor(g.name("mean_square"), [P, TILES], F32))
        bc = st.enter_context(nc.psum_tensor(g.name("mod_bc"), [P, 4, BANK], F32))
        tp = st.enter_context(nc.psum_tensor(g.name("h_tp"), [P, 4, BANK], F32))
        ms_done, root_done, bc_done, v_done, h_done = sem("ms_done"), sem("root_done"), sem("bc_done"), sem("v_done"), sem("h_done")
        tp_done, tp_out = sem("tp_done"), sem("tp_out")
        streams = [w for w in (0, 1) if any((i < 2) == (w == 0) for i in tiles)]
        mine = lambda w: [i for i in tiles if (i < 2) == (w == 0)]

        with nc.Block() as block:
            @block.gpsimd
            def _(po):
                po.sem_clear(g.sems.other)

            @block.scalar
            def _(ac):
                for n, i in enumerate(tiles):
                    if n >= 2:
                        ac.wait_ge(ms_done, n - 1)
                    ac.activation(sq[:, n % 2, :], g.X[:, i, :], ACT.Square, scale=float(D) ** -0.5,
                                  accum_out=ms[:, i:i + 1]).then_inc(ms_done, 1)
                ac.wait_ge(v_done, 1)
                ac.activation(ms[:, tiles[0]:tiles[-1] + 1], ms[:, tiles[0]:tiles[-1] + 1], ACT.Sqrt).then_inc(root_done, 1)
                for n in range(2 * len(tiles)):
                    i, half = tiles[n // 2], n % 2
                    ac.wait_ge(tp_done, n + 1)
                    ac.activation(HT[:, half * 4:half * 4 + 4, i * P:(i + 1) * P],
                                  tp[:, n % 4, :].rearrange("p (k t) -> p k t", k=4), ACT.Copy).then_inc(tp_out, 1)

            @block.tensor
            def _(pe):
                n = 0
                for s, w in enumerate(streams):
                    if s:
                        pe.wait_ge(h_done, len(mine(streams[0])))
                    for q in range(2):
                        mm = broadcast_row(pe, g, l, bc[:, 2 * q:2 * q + 2, :], part + 1 - q, 1 - w)
                    mm.then_inc(bc_done, 1)
                    for i in mine(w):
                        pe.wait_ge(h_done, n // 2 + 1)
                        for half in range(2):
                            if n >= 4:
                                pe.wait_ge(tp_out, n - 3)
                            for k in range(4):
                                mm = pe.transpose(tp[:, n % 4, k * P:(k + 1) * P], h[:, i, (half * 4 + k) * P:(half * 4 + k + 1) * P], g.ident[:])
                            mm.then_inc(tp_done, 1)
                            n += 1

            @block.vector
            def _(ve):
                step = chained(ve, v_done)
                ve.wait_ge(ms_done, len(tiles))
                t0, t1 = tiles[0], tiles[-1] + 1
                step(ve.tensor_scalar(ms[:, t0:t1], ms[:, t0:t1], 1e-6, None, ALU.add))
                ve.wait_ge(root_done, 1)
                step(ve.reciprocal(ms[:, t0:t1], ms[:, t0:t1]))
                for s, w in enumerate(streams):
                    ve.wait_ge(bc_done, s + 1)
                    for i in mine(w):
                        step(ve.scalar_tensor_tensor(out=h[:, i, :], in0=g.X[:, i, :], scalar=ms[:, i:i + 1],
                                                     in1=bc[:, 0:2, :].rearrange("p a b -> p (a b)"), op0=ALU.mult, op1=ALU.mult))
                        ve.tensor_tensor(h[:, i, :], h[:, i, :], bc[:, 2:4, :].rearrange("p a b -> p (a b)"), ALU.add).then_inc(h_done, 1)


def stage_input_projection(nc, g, l, HT):
    CW, WB, ZB = 3, 3, 3
    with ExitStack() as st:
        sem = g.sems.begin(st)
        w = st.enter_context(nc.sbuf_tensor(g.name("w_in_ring"), [P, WB, KD, CW * P], F32))
        z = st.enter_context(nc.sbuf_tensor(g.name("z_padded"), [P, ZB, 2, SEQ + 2], F32))
        ps = st.enter_context(nc.psum_tensor(g.name("z_ps"), [P, 4, BANK], F32))
        landed = [sem(f"w_in_landed{b}") for b in range(WB)]
        padded, mm_done, evac, conv_done, v_done = sem("padded"), sem("mm_done"), sem("evacuated"), sem("conv_done"), sem("v_done")
        wv = g.dram["w_in"][l].rearrange("(k p) n -> p k n", p=P)
        cw, cb = ROWS["conv_w"], ROWS["conv_b"]
        streams = lambda j: needed_streams(l) if j < 6 or Q0 <= j < K0 else (0, 1)
        part = lambda j: slice(streams(j)[0] * SEQ, TOK)
        padded_at = lambda j, t: z[:, j % ZB, streams(j)[0]:2, t:t + SEQ]

        with nc.Block() as block:
            @block.sync
            def _(sp):
                for n in range(IN_TILES // CW):
                    if n >= WB:
                        sp.wait_ge(mm_done, (n - WB + 1) * CW)
                    sp.dma_start(w[:, n % WB, :, :], wv[:, :, n * CW * P:(n + 1) * CW * P]).then_inc(landed[n % WB], 16)

            @block.gpsimd
            def _(po):
                po.sem_clear(g.sems.other)
                po.memset(z[:], 0.0).then_inc(padded, 1)

            @block.tensor
            def _(pe):
                for j in range(IN_TILES):
                    n = j // CW
                    pe.wait_ge(landed[n % WB], 16 * (n // WB + 1))
                    if j >= 4:
                        pe.wait_ge(evac, j - 3)
                    for k in range(KD):
                        mm = pe.matmul(ps[:, j % 4, part(j)], w[:, n % WB, k, (j % CW) * P:(j % CW + 1) * P], HT[:, k, part(j)], start=k == 0, stop=k == KD - 1)
                    mm.then_inc(mm_done, 1)

            @block.scalar
            def _(ac):
                ac.wait_ge(padded, 1)
                for j in range(IN_TILES):
                    ac.wait_ge(mm_done, j + 1)
                    if j < CONV_TILES:
                        if j >= ZB:
                            ac.wait_ge(conv_done, j - ZB + 1)
                        ac.activation(padded_at(j, 1), ps[:, j % 4, part(j)].rearrange("p (s t) -> p s t", t=SEQ), ACT.Copy)
                        ac.activation(g.S[:, j, part(j)], ps[:, j % 4, part(j)], ACT.Identity, scale=g.par[:, l, cw + 12 + j:cw + 13 + j],
                                      bias=g.par[:, l, cb + j:cb + j + 1]).then_inc(evac, 1)
                    else:
                        f = {LORA0: ACT.Tanh, LORA0 + 2: ACT.Sigmoid}.get(j, ACT.Copy)
                        ac.activation(g.S[:, j, part(j)], ps[:, j % 4, part(j)], f).then_inc(evac, 1)

            @block.vector
            def _(ve):
                step = chained(ve, v_done)
                for j in range(CONV_TILES):
                    ve.wait_ge(evac, j + 1)
                    s = g.S[:, j, part(j)].rearrange("p (s t) -> p s t", t=SEQ)
                    step(ve.scalar_tensor_tensor(out=s, in0=padded_at(j, 0), scalar=g.par[:, l, cw + j:cw + j + 1], in1=s, op0=ALU.mult, op1=ALU.add))
                    ve.scalar_tensor_tensor(out=s, in0=padded_at(j, 2), scalar=g.par[:, l, cw + 24 + j:cw + 25 + j], in1=s,
                                            op0=ALU.mult, op1=ALU.add).then_inc(conv_done, 1)



def needed_streams(l):
    return (1,) if l == DEPTH - 1 else (0, 1)


def stage_hyena(nc, g, l):
    streams = needed_streams(l)
    part, NS = slice(streams[0] * SEQ, TOK), len(streams)
    FR = 2
    with ExitStack() as st:
        sem = g.sems.begin(st)
        sb = lambda name, shape: st.enter_context(nc.sbuf_tensor(g.name(name), shape, F32))
        w1, w2, w3, b3 = sb("hy_w1", [HY_EMB, HY_HID]), sb("hy_w2", [HY_HID, HY_HID]), sb("hy_w3", [HY_HID, 512]), sb("hy_b3", [1, 512])
        emb, window, dft = sb("emb", [HY_EMB, SEQ]), sb("window", [P, 2, 512]), sb("dft", [P, 4, 2, SEQ])
        arg, turns, hid = sb("hy_arg", [HY_HID, 2, SEQ]), sb("hy_turns", [HY_HID, 2, SEQ]), sb("hy_hid", [HY_HID, 2, SEQ])
        F, sq = sb("filter", [P, 2, 512]), sb("filter_sq", [P, 2, 512])
        even, odd, rk = sb("filter_even", [P, 2, HY_CH]), sb("filter_odd", [P, 2, HY_CH]), sb("filter_rnorm", [P, HY_CH])
        K = sb("filter_spectrum", [P, FR, 2, HY_CH])
        u, U = sb("u_cols", [P, 2, TOK]), sb("u_rows", [P, 2, 512])
        Yc, Yn, tmp = sb("y_cos", [P, FR, 512]), sb("y_sin", [P, FR, 512]), sb("y_tmp", [P, 512])
        hy, hsq, rs = sb("hy", [P, 2, TOK]), sb("hy_sq", [P, 2, TOK]), sb("hy_rnorm", [P, TOK])
        ps = st.enter_context(nc.psum_tensor(g.name("hy_ps"), [P, 8, BANK], F32))
        w_in, v_done = sem("w_in"), sem("v_done")
        layer_in, sin_done, filt_in, F_done, norm_sum, rk_ready, K_in, K_done = (
            sem(n) for n in ("layer_arg_in", "sin_done", "filter_in", "filter_done", "norm_sum", "norm_ready", "spectrum_in", "spectrum_done"))
        arg_ready, root_done, eps_done, u_done, ut_in, U_done, Uf_in, Y_done, y_in, hy_done, ms_in = (
            sem(n) for n in ("arg_ready", "root_done", "eps_done", "u_done", "u_transposed", "u_rows_done", "u_spectrum_in", "y_spectrum_done", "y_in", "hy_done", "hy_ms_in"))
        R = ROWS
        par = lambda name, k=0, p=P: g.par[0:p, l, R[name] + k:R[name] + k + 1]
        C = lambda t, f: dft[:, 0, t, f * P:(f + 1) * P]
        Sn = lambda t, f: dft[:, 1, t, f * P:(f + 1) * P]

        with nc.Block() as block:
            @block.sync
            def _(sp):
                for dst, name in ((w1, "hy_w1"), (w2, "hy_w2"), (w3, "hy_w3")):
                    sp.dma_start(dst[:], g.dram[name][l]).then_inc(w_in, 16)
                sp.dma_start(b3[:], g.dram["hy_b3"][l:l + 1, :]).then_inc(w_in, 16)
                for dst, name in ((emb, "k_emb"), (window, "k_window"), (dft, "k_dft")):
                    sp.dma_start(dst[:], g.dram[name]).then_inc(w_in, 16)

            @block.gpsimd
            def _(po):
                po.sem_clear(g.sems.other)

            @block.tensor
            def _(pe):
                pe.wait_ge(w_in, 16 * 7)
                pe.matmul(ps[0:HY_HID, 0, 0:SEQ], w1[:], emb[:], start=True, stop=True).then_inc(layer_in, 1)
                pe.wait_ge(u_done, 1)
                for t in range(2):
                    for s in streams:
                        for c in range(2):
                            mm = pe.transpose(ps[:, 5 + t, s * 256 + c * P:s * 256 + (c + 1) * P], u[:, c, (2 * s + t) * P:(2 * s + t + 1) * P], g.ident[:])
                mm.then_inc(ut_in, 1)
                pe.wait_ge(sin_done, 1)
                pe.matmul(ps[0:HY_HID, 1, 0:SEQ], w2[:], hid[:, 0, :], start=True, stop=True).then_inc(layer_in, 1)
                pe.wait_ge(sin_done, 2)
                for t in range(2):
                    pe.matmul(ps[:, 2 + t, :], hid[:, 1, t * P:(t + 1) * P], w3[:], start=True, stop=False)
                    mm = pe.matmul(ps[:, 2 + t, :], g.ones[0:1, :], b3[:], start=False, stop=True)
                mm.then_inc(filt_in, 1)
                pe.wait_ge(U_done, 1)
                for f in range(FR):
                    for q, basis in ((0, C), (1, Sn)):
                        for t in range(2):
                            mm = pe.matmul(ps[:, 4 + 2 * f + q, part], basis(t, f), U[:, t, part], start=t == 0, stop=t == 1)
                mm.then_inc(Uf_in, 1)
                pe.wait_ge(F_done, 1)
                for n in range(4):
                    mm = pe.matmul(ps[:, 0, 0:HY_CH], g.ones[:], sq[:, n // 2, (n % 2) * HY_CH:(n % 2 + 1) * HY_CH], start=n == 0, stop=n == 3)
                mm.then_inc(norm_sum, 1)
                pe.wait_ge(F_done, 2)
                for f in range(FR):
                    for q, (basis, side) in enumerate(((C, even), (Sn, odd))):
                        for t in range(2):
                            mm = pe.matmul(ps[:, 2 + f, q * HY_CH:(q + 1) * HY_CH], basis(t, f), side[:, t, :], start=t == 0, stop=t == 1)
                mm.then_inc(K_in, 1)
                pe.wait_ge(Y_done, 1)
                for c in range(2):
                    for s in streams:
                        cols = slice(s * 256 + c * P, s * 256 + (c + 1) * P)
                        for f in range(FR):
                            pe.matmul(ps[:, c, s * 256:(s + 1) * 256], Yc[:, f, cols], dft[:, 2, f, :], start=f == 0, stop=False)
                            mm = pe.matmul(ps[:, c, s * 256:(s + 1) * 256], Yn[:, f, cols], dft[:, 3, f, :], start=False, stop=f == FR - 1)
                mm.then_inc(y_in, 1)
                pe.wait_ge(hy_done, 1)
                for c in range(2):
                    mm = pe.matmul(ps[:, 2, part], g.ones[:], hsq[:, c, part], start=c == 0, stop=c == 1)
                mm.then_inc(ms_in, 1)

            @block.scalar
            def _(ac):
                for k in range(2):
                    ac.wait_ge(arg_ready, k + 1)
                    ac.activation(hid[:, k, :], arg[:, k, :], ACT.Sin).then_inc(sin_done, 1)
                for k, t in enumerate((rk[:], rs[:, part])):
                    ac.wait_ge(eps_done, k + 1)
                    ac.activation(t, t, ACT.Sqrt).then_inc(root_done, 1)

            @block.vector
            def _(ve):
                step = chained(ve, v_done)
                step(ve.tensor_tensor(u[:, :, part], g.S[:, 2:4, part], g.S[:, 4:6, part], ALU.mult))
                ve.sem_inc(u_done, 1)
                for k in range(2):
                    ve.wait_ge(layer_in, k + 1)
                    a, n = arg[:, k, :], turns[:, k, :]
                    step(ve.tensor_scalar(a, ps[0:HY_HID, k, 0:SEQ], par(f"hy_b{k + 1}", 0, HY_HID), par("hy_freq", k, HY_HID), ALU.add, ALU.mult))
                    step(ve.tensor_scalar(n, a, 1.0 / TWO_PI, 12582912.0, ALU.mult, ALU.add))
                    step(ve.tensor_scalar(n, n, 12582912.0, None, ALU.subtract))
                    step(ve.scalar_tensor_tensor(out=a, in0=n, scalar=-TWO_PI, in1=a, op0=ALU.mult, op1=ALU.add))
                    ve.tensor_scalar(a, a, PI_BELOW, -PI_BELOW, ALU.min, ALU.max).then_inc(arg_ready, 1)
                    if k == 0:
                        ve.wait_ge(ut_in, 1)
                        ve.tensor_copy(U[:, :, part], ps[:, 5:7, part]).then_inc(U_done, 1)
                ve.wait_ge(filt_in, 1)
                step(ve.tensor_tensor(F[:], ps[:, 2:4, :], window[:], ALU.mult))
                ve.tensor_tensor(sq[:], F[:], F[:], ALU.mult).then_inc(F_done, 1)
                step(ve.tensor_tensor(even[:], F[:, :, 0:HY_CH], F[:, :, HY_CH:512], ALU.add))
                ve.tensor_tensor(odd[:], F[:, :, HY_CH:512], F[:, :, 0:HY_CH], ALU.subtract).then_inc(F_done, 1)
                ve.wait_ge(norm_sum, 1)
                ve.tensor_scalar(rk[:], ps[:, 0, 0:HY_CH], 1e-6, None, ALU.add).then_inc(eps_done, 1)
                ve.wait_ge(root_done, 1)
                step(ve.reciprocal(rk[:], rk[:]))
                ve.wait_ge(K_in, 1)
                for f in range(FR):
                    step(ve.tensor_tensor(K[:, f, :, :], ps[:, 2 + f, :].rearrange("p (q c) -> p q c", q=2), rk[:].unsqueeze(1).to_broadcast([P, 2, HY_CH]), ALU.mult))
                ve.wait_ge(Uf_in, 1)
                for f in range(FR):
                    view = lambda x: x[:, part].rearrange("p (s c) -> p s c", s=NS)
                    uc, us = view(ps[:, 4 + 2 * f, :]), view(ps[:, 5 + 2 * f, :])
                    kr, ki = (K[:, f, q, :].unsqueeze(1).to_broadcast([P, NS, HY_CH]) for q in range(2))
                    for dst, a, b, op in ((Yc, (uc, kr), (us, ki), ALU.add), (Yn, (us, kr), (uc, ki), ALU.subtract)):
                        step(ve.tensor_tensor(view(dst[:, f, :]), *a, ALU.mult))
                        step(ve.tensor_tensor(view(tmp[:]), *b, ALU.mult))
                        step(ve.tensor_tensor(dst[:, f, part], dst[:, f, part], tmp[:, part], op))
                ve.sem_inc(Y_done, 1)
                ve.wait_ge(y_in, 1)
                for c in range(2):
                    step(ve.scalar_tensor_tensor(out=hy[:, c, part], in0=u[:, c, part], scalar=par("hy_bias", c), in1=ps[:, c, part], op0=ALU.mult, op1=ALU.add))
                step(ve.tensor_tensor(hy[:, :, part], hy[:, :, part], g.S[:, 0:2, part], ALU.mult))
                ve.tensor_tensor(hsq[:, :, part], hy[:, :, part], hy[:, :, part], ALU.mult).then_inc(hy_done, 1)
                ve.wait_ge(ms_in, 1)
                ve.tensor_scalar(rs[:, part], ps[:, 2, part], 1.0 / HY_CH, 1e-6, ALU.mult, ALU.add).then_inc(eps_done, 1)
                ve.wait_ge(root_done, 2)
                step(ve.reciprocal(rs[:, part], rs[:, part]))
                for c in range(2):
                    step(ve.scalar_tensor_tensor(out=g.mix[:, c, part], in0=hy[:, c, part], scalar=par("hy_out_g", c), in1=rs[:, part], op0=ALU.mult, op1=ALU.mult))


def stage_attention(nc, g, l, tiles):
    SCALE = float(AT_HD) ** -0.5
    units = [(i, j) for i in tiles for j in range(4)]
    keys = lambda i: TOK if i >= 2 else SEQ
    with ExitStack() as st:
        sem = g.sems.begin(st)
        sb = lambda name, shape: st.enter_context(nc.sbuf_tensor(g.name(name), shape, F32))
        rot, KS, VT = sb("rotated", [P, 5, SEQ]), sb("k_swapped", [P, TOK]), sb("v_rows", [P, TILES, P])
        E, PT = sb("scores", [P, 2, 2, TOK]), sb("probs_cols", [P, 2, 2, TOK])
        mx, nm, total, es, rden = (sb(n, [P, 2, 2]) for n in ("row_max", "neg_max", "row_sum", "sink_exp", "rden"))
        O, osq, ms = sb("attn_rows", [P, TILES, AT_W]), sb("attn_sq", [P, AT_W]), sb("attn_ms", [P, TILES])
        sps = st.enter_context(nc.psum_tensor(g.name("scores_ps"), [P, 2, 2, BANK], F32))
        tps = st.enter_context(nc.psum_tensor(g.name("probs_ps"), [P, 2, BANK], F32))
        out_ps = st.enter_context(nc.psum_tensor(g.name("out_ps"), [P, BANK], F32))
        mod_ps = st.enter_context(nc.psum_tensor(g.name("mod_ps"), [P, BANK], F32))
        mod = Modulation(nc, g, st, sem, l, 1, mod_ps[0:2, :], sb("mod_w", [P, 2, KD, BANK])[:])
        rot_in, rope_done, ks_in, kv_done, v_done = (sem(n) for n in ("rot_in", "rope_done", "kv_in", "kv_done", "v_done"))
        s_in, s_out, max_done, exp_done, pt_in, pt_out, pv_in, o_done = (
            sem(n) for n in ("scores_in", "scores_out", "max_done", "exp_done", "probs_in", "probs_out", "pv_in", "o_done"))
        sq_done, eps_done, root_done, on_done, ot_in, ot_out, sqa = (
            sem(n) for n in ("sq_done", "eps_done", "root_done", "o_normed", "o_cols_in", "o_cols_out", "sq_each"))
        lat = slice(SEQ, TOK)

        every = len(units) // mod.count

        with nc.Block() as block:
            @block.sync
            def _(sp):
                mod.traffic(sp)

            @block.gpsimd
            def _(po):
                po.sem_clear(g.sems.other)
                mod.gain_ones(po)

            @block.tensor
            def _(pe):
                for j in range(5):
                    mm = pe.matmul(sps[:, j // 4, j // 2 % 2, (j % 2) * SEQ:(j % 2 + 1) * SEQ], g.rot[:], g.S[:, Q0 + j, lat], start=True, stop=True)
                mm.then_inc(rot_in, 1)
                for i in range(TILES):
                    pe.transpose(tps[:, 1, i * P:(i + 1) * P], g.S[:, V0, i * P:(i + 1) * P], g.ident[:])
                pe.wait_ge(rope_done, 1)
                pe.matmul(tps[:, 0, :], g.swap[:], g.S[:, K0, :], start=True, stop=True).then_inc(ks_in, 1)

                def scores(n):
                    i, j = units[n]
                    if n >= 2:
                        pe.wait_ge(s_out, n - 1)
                    for h in range(2):
                        k = g.S[64 * h:64 * h + 64, K0, 0:keys(i)] if j // 2 == h else KS[64 * h:64 * h + 64, 0:keys(i)]
                        mm = pe.matmul(sps[:, n % 2, h, 0:keys(i)], g.S[64 * h:64 * h + 64, Q0 + j, i * P:(i + 1) * P], k, start=True, stop=True)
                    mm.then_inc(s_in, 1)

                def turn(n):
                    i, j = units[n]
                    pe.wait_ge(exp_done, n + 1)
                    if n >= 1:
                        pe.wait_ge(pt_out, 2 * n)
                    for h in range(2):
                        for t in range(keys(i) // P):
                            mm = pe.transpose(tps[:, h, t * P:(t + 1) * P], E[:, n % 2, h, t * P:(t + 1) * P], g.ident[:])
                        mm.then_inc(pt_in, 1)

                def values(n):
                    i, j = units[n]
                    pe.wait_ge(pt_out, 2 * n + 2)
                    if n:
                        pe.wait_ge(o_done, n)
                    for h in range(2):
                        for t in range(keys(i) // P):
                            mm = pe.matmul(out_ps[:, h * 64:h * 64 + 64], PT[:, n % 2, h, t * P:(t + 1) * P],
                                           VT[:, t, 64 * (j // 2):64 * (j // 2) + 64], start=t == 0, stop=t == keys(i) // P - 1)
                    mm.then_inc(pv_in, 1)

                pe.wait_ge(kv_done, 2)
                scores(0)
                for n in range(len(units)):
                    if n + 1 < len(units):
                        scores(n + 1)
                    if n % every == 0:
                        mod.product(pe, n // every)
                    turn(n)
                    if n:
                        values(n - 1)
                values(len(units) - 1)
                for m, i in enumerate(tiles):
                    pe.wait_ge(on_done, m + 1)
                    if m >= 2:
                        pe.wait_ge(ot_out, m - 1)
                    for j in range(4):
                        mm = pe.transpose(tps[:, m % 2, j * P:(j + 1) * P], O[:, i, j * P:(j + 1) * P], g.ident[:])
                    mm.then_inc(ot_in, 1)

            @block.scalar
            def _(ac):
                ac.wait_ge(ks_in, 1)
                ac.activation(KS[:], tps[:, 0, :], ACT.Copy).then_inc(kv_done, 1)
                ac.activation(VT[:].rearrange("p i c -> p (i c)"), tps[:, 1, :], ACT.Copy).then_inc(kv_done, 1)
                def exps(n):
                    i, j = units[n]
                    b = n % 2
                    ac.wait_ge(max_done, n + 1)
                    for h in range(2):
                        ac.activation(E[:, b, h, 0:keys(i)], E[:, b, h, 0:keys(i)], ACT.Exp, bias=nm[:, b, h:h + 1], scale=SCALE,
                                      accum_out=total[:, b, h:h + 1])
                    ac.activation(es[:, b, :], es[:, b, :], ACT.Exp).then_inc(exp_done, 1)

                exps(0)
                for n, (i, j) in enumerate(units):
                    b = n % 2
                    if n + 1 < len(units):
                        exps(n + 1)
                    ac.wait_ge(pt_in, 2 * n + 1)
                    if n >= 2:
                        ac.wait_ge(pv_in, n - 1)
                    ac.activation(PT[:, b, 0, 0:keys(i)], tps[:, 0, 0:keys(i)], ACT.Copy).then_inc(pt_out, 1)
                    if n % every == 0:
                        mod.take(ac, n // every)
                ac.wait_ge(o_done, len(units))
                for m, i in enumerate(tiles):
                    if m:
                        ac.wait_ge(sq_done, m)
                    ac.activation(osq[:], O[:, i, :], ACT.Square, scale=float(AT_W) ** -0.5, accum_out=ms[:, i:i + 1]).then_inc(sq_done, 1)
                ac.wait_ge(eps_done, 1)
                ac.activation(ms[:, tiles[0]:tiles[-1] + 1], ms[:, tiles[0]:tiles[-1] + 1], ACT.Sqrt).then_inc(root_done, 1)
                for m, i in enumerate(tiles):
                    ac.wait_ge(ot_in, m + 1)
                    for j in range(4):
                        r = ROWS["at_out_g"] + j
                        a = ac.activation(g.mix[:, 4 + j, i * P:(i + 1) * P], tps[:, m % 2, j * P:(j + 1) * P], ACT.Copy, scale=g.par[:, l, r:r + 1])
                    a.then_inc(ot_out, 1)

            @block.vector
            def _(ve):
                step = chained(ve, v_done)
                ve.wait_ge(rot_in, 1)
                qk = g.S[:, Q0:Q0 + 5, lat]
                step(ve.tensor_tensor(rot[:], sps[:].rearrange("p a b (c t) -> p (a b c) t", c=2)[:, 0:5, :], g.rope[:, 1, :].unsqueeze(1).to_broadcast([P, 5, SEQ]), ALU.mult))
                step(ve.tensor_tensor(qk, qk, g.rope[:, 0, :].unsqueeze(1).to_broadcast([P, 5, SEQ]), ALU.mult))
                ve.tensor_tensor(qk, qk, rot[:], ALU.add).then_inc(rope_done, 1)

                def softmax_head(n):
                    i, j = units[n]
                    b, w = n % 2, keys(i)
                    ve.wait_ge(s_in, n + 1)
                    if n >= 2:
                        ve.wait_ge(pt_in, 2 * n - 2)
                    if i >= 2:
                        ve.tensor_tensor(E[:, b, :, 0:w], sps[:, b, :, 0:w], g.band[:, i - 2, :].unsqueeze(1).to_broadcast([P, 2, TOK]), ALU.add).then_inc(s_out, 1)
                    else:
                        ve.tensor_copy(E[:, b, :, 0:w], sps[:, b, :, 0:w]).then_inc(s_out, 1)
                    ve.wait_ge(s_out, n + 1)
                    sink = g.sink[:, l, 2 * j:2 * j + 2]
                    step(ve.tensor_reduce(mx[:, b, :], E[:, b, :, 0:w], AX.X, ALU.max))
                    step(ve.tensor_tensor(mx[:, b, :], mx[:, b, :], g.sink8[:, l, 2 * j:2 * j + 2], ALU.max))
                    step(ve.tensor_scalar(nm[:, b, :], mx[:, b, :], -SCALE, None, ALU.mult))
                    ve.tensor_tensor(es[:, b, :], sink, nm[:, b, :], ALU.add).then_inc(max_done, 1)

                def weigh(n):
                    i, j = units[n]
                    b = n % 2
                    ve.wait_ge(pv_in, n + 1)
                    ve.tensor_tensor(O[:, i, j * P:(j + 1) * P].rearrange("p (h c) -> p h c", h=2), out_ps[:, 0:P].rearrange("p (h c) -> p h c", h=2),
                                     rden[:, b, :].unsqueeze(2).to_broadcast([P, 2, 64]), ALU.mult).then_inc(o_done, 1)

                softmax_head(0)
                for n, (i, j) in enumerate(units):
                    b = n % 2
                    if n + 1 < len(units):
                        softmax_head(n + 1)
                    ve.wait_ge(exp_done, n + 1)
                    if n >= 2:
                        ve.wait_ge(o_done, n - 1)
                    step(ve.tensor_tensor(rden[:, b, :], total[:, b, :], es[:, b, :], ALU.add))
                    step(ve.reciprocal(rden[:, b, :], rden[:, b, :]))
                    ve.wait_ge(pt_in, 2 * n + 2)
                    if n >= 2:
                        ve.wait_ge(pv_in, n - 1)
                    ve.tensor_copy(PT[:, b, 1, 0:keys(i)], tps[:, 1, 0:keys(i)]).then_inc(pt_out, 1)
                    if n:
                        weigh(n - 1)
                weigh(len(units) - 1)
                mod.finish(ve)
                ve.wait_ge(sq_done, len(tiles))
                part = ms[:, tiles[0]:tiles[-1] + 1]
                ve.tensor_scalar(part, part, 1e-6, None, ALU.add).then_inc(eps_done, 1)
                ve.wait_ge(root_done, 1)
                step(ve.reciprocal(part, part))
                for i in tiles:
                    ve.tensor_scalar(O[:, i, :], O[:, i, :], ms[:, i:i + 1], None, ALU.mult).then_inc(on_done, 1)


KK, RR, KC, VC = 0, 6, 8, 10
B_AT, KD_AT, Y_AT = (2, 4), (15, 17), (12, 19)


def stage_rwkv_operands(nc, g, l):
    with ExitStack() as st:
        sem = g.sems.begin(st)
        sb = lambda name, shape: st.enter_context(nc.sbuf_tensor(g.name(name), shape, F32))
        wup, aup = sb("w_up", [P, RW_W]), sb("a_up", [P, RW_W])
        sq, lw, keep = sb("kk_sq", [P, 2, TOK]), sb("log_decay", [P, 2, 2, TOK]), sb("chunk_keep", [P, TOK])
        ps = st.enter_context(nc.psum_tensor(g.name("rwkv_ps"), [P, 8, BANK], F32))
        w_in, keep_set, sq_done, kk_in, eps_done, root_done, kk_done, lora_in, sig_done, v_done, log_done, exp_done = (
            sem(n) for n in ("w_in", "keep_set", "sq_done", "kk_in", "eps_done", "root_done", "kk_done", "lora_in", "sig_done", "v_done", "log_done", "exp_done"))
        par = lambda name, k: g.par[:, l, ROWS[name] + k:ROWS[name] + k + 1]
        kk = g.S[:, KK:KK + 2, :]
        bank = lambda d, q, p: (2 + 4 * d + 2 * q + p) % 8

        with nc.Block() as block:
            @block.sync
            def _(sp):
                sp.dma_start(wup[:], g.dram["rw_w_up"][l].rearrange("d r n -> (d r) n")).then_inc(w_in, 16)
                sp.dma_start(aup[:], g.dram["rw_a_up"][l].rearrange("d r n -> (d r) n")).then_inc(w_in, 16)

            @block.gpsimd
            def _(po):
                po.sem_clear(g.sems.other)
                po.memset(keep[:], 1.0).then_inc(keep_set, 1)
                po.wait_ge(keep_set, 1)
                po.memset(keep[:].rearrange("p (c t) -> p c t", t=CHUNK)[:, :, 0:1], 0.0).then_inc(keep_set, 1)

            @block.tensor
            def _(pe):
                pe.wait_ge(w_in, 32)
                for d in range(2):
                    if d:
                        pe.wait_ge(sq_done, 1)
                        for p in range(2):
                            mm = pe.matmul(ps[:, p, :], g.pair[:], sq[:, p, :], start=True, stop=True)
                        mm.then_inc(kk_in, 1)
                        pe.wait_ge(eps_done, 1)
                    for q, (up, src) in enumerate(((wup, LORA0), (aup, LORA0 + 1))):
                        for p in range(2):
                            mm = pe.matmul(ps[:, bank(d, q, p), :], up[64 * d:64 * d + 64, p * P:(p + 1) * P], g.S[64 * d:64 * d + 64, src, :], start=True, stop=True)
                    mm.then_inc(lora_in, 1)

            @block.scalar
            def _(ac):
                for d in range(2):
                    ac.wait_ge(lora_in, d + 1)
                    for p in range(2):
                        ac.activation(lw[:, d, p, :], ps[:, bank(d, 0, p), :], ACT.Sigmoid, bias=par("rw_w0", 2 * d + p))
                        a = ac.activation(g.S[:, B_AT[d] + p, :], ps[:, bank(d, 1, p), :], ACT.Sigmoid, bias=par("rw_a0", 2 * d + p))
                    a.then_inc(sig_done, 1)
                ac.wait_ge(eps_done, 1)
                ac.activation(sq[:], sq[:], ACT.Sqrt).then_inc(root_done, 1)
                for d in range(2):
                    ac.wait_ge(log_done, d + 1)
                    ac.activation(g.eL[:, d, :, :], g.eN[:, d, :, :], ACT.Exp).then_inc(exp_done, 1)
                    ac.wait_ge(exp_done, 3 * d + 1)
                    ac.activation(g.eN[:, d, :, :], g.eN[:, d, :, :], ACT.Exp, scale=-1.0).then_inc(exp_done, 1)
                    ac.activation(g.eP[:, d, :, :], g.eP[:, d, :, :], ACT.Exp).then_inc(exp_done, 1)

            @block.vector
            def _(ve):
                step = chained(ve, v_done)
                for p in range(2):
                    step(ve.tensor_scalar(kk[:, p, :], g.S[:, KC + p, :], par("rw_k_k", p), None, ALU.mult))
                ve.tensor_tensor(sq[:], kk, kk, ALU.mult).then_inc(sq_done, 1)
                ve.wait_ge(kk_in, 1)
                ve.tensor_scalar(sq[:], ps[:, 0:2, :], 1e-12, None, ALU.add).then_inc(eps_done, 1)
                ve.wait_ge(keep_set, 2)
                for d in range(2):
                    ve.wait_ge(sig_done, d + 1)
                    step(ve.tensor_scalar(lw[:, d, :, :], lw[:, d, :, :], -DECAY, None, ALU.mult))
                    for p in range(2):
                        src, dst = lw[:, d, p, :], g.eN[:, d, p, :]
                        if d:
                            src, dst = lw[:, d, p, ::-1], g.eN[:, d, p, ::-1]
                        step(ve.tensor_tensor_scan(dst, keep[:], src, 0.0, ALU.mult, ALU.add))
                    ve.tensor_tensor(g.eP[:, d, :, :], g.eN[:, d, :, :], lw[:, d, :, :], ALU.subtract).then_inc(log_done, 1)
                ve.wait_ge(root_done, 1)
                step(ve.reciprocal(sq[:], sq[:]))
                step(ve.tensor_tensor(kk, kk, sq[:], ALU.mult))
                for d in range(2):
                    a, k = g.S[:, B_AT[d]:B_AT[d] + 2, :], g.S[:, KD_AT[d]:KD_AT[d] + 2, :]
                    for p in range(2):
                        step(ve.tensor_scalar(k[:, p, :], a[:, p, :], par("rw_k_a", p), g.omka[:, l, p:p + 1], ALU.mult, ALU.add))
                    step(ve.tensor_tensor(k, k, g.S[:, KC:KC + 2, :], ALU.mult))
                    step(ve.tensor_tensor(a, a, kk, ALU.mult))


def stage_rwkv_chunks(nc, g, l):
    STEPS = 16
    order = [(n, t, d) for n in range(TILES) for t in range(1, STEPS + 1) for d in range(2)]
    outputs = lambda i: i // 2 in needed_streams(l)
    H4 = 4
    with ExitStack() as st:
        sem = g.sems.begin(st)
        ps = [st.enter_context(nc.psum_tensor(g.name(f"chunk_ps{d}"), [P, 4, BANK], F32)) for d in range(2)]

        class Stream:
            pass
        streams = []
        for d in range(2):
            s = Stream()
            sb = lambda name, shape: st.enter_context(nc.sbuf_tensor(g.name(f"{name}{d}"), shape, F32))
            s.AR = sb("a_r", [P, 2, 2, P])
            s.bt, s.kt, s.bh, s.kh, s.v = (sb(n, [P, 2, P]) for n in ("b_in", "k_in", "b_end", "k_end", "v_col"))
            s.rows1, s.rows2 = sb("rows_a_b", [P, 4, P]), sb("rows_k_v", [P, 4, P])
            s.A, s.AT, s.A32T, s.A64T = (sb(n, [P, H4, P]) for n in ("A16_", "A16T_", "A32T_", "A64T_"))
            s.MakT, s.MrbT, s.MrkT = (sb(n, [P, H4, P]) for n in ("MakT_", "MrbT_", "MrkT_"))
            s.A2, s.A2T, s.A4, s.A4T = (sb(n, [P, H4, P]) for n in ("A2_", "A2T_", "A4_", "A4T_"))
            s.X, s.XT = (sb(n, [P, H4, P]) for n in ("X_", "XT_"))
            s.A8, s.Q, s.rhs, s.GE, s.Z = s.A, s.A2, s.AT, s.A4, s.X
            s.QT, s.S = sb("QT_", [P, 2, P]), sb("state_", [P, 2, P])
            s.Phi, s.Psi = s.A4T, s.A2T
            s.pe, s.ve, s.ac = sem(f"products{d}"), sem(f"vector_out{d}"), sem(f"scalar_out{d}")
            streams.append(s)
        ready = [sem(f"operands_ready{d}") for d in range(2)]
        v_done, state_zero = sem("v_done"), sem("state_zero")
        flat = lambda t: t.rearrange("p a b -> p (a b)")
        heads = lambda t: t.rearrange("p (h s) -> p h s", h=H4)
        mask = lambda d, m: g.masks[:, (m if d == 0 else m + 5), :].unsqueeze(1).to_broadcast([P, H4, P])
        maskT = lambda d, m: g.masks[:, (m + 5 if d == 0 else m), :].unsqueeze(1).to_broadcast([P, H4, P])
        M16, M32, M64, STRICT, INCL = range(5)
        tile_of = lambda d, n: n if d == 0 else (n ^ 1)

        with nc.Block() as block:
            @block.gpsimd
            def _(po):
                po.sem_clear(g.sems.other)
                for s in streams:
                    po.memset(s.S[:], 0.0).then_inc(state_zero, 1)

            @block.tensor
            def _(pe):
                for n, t, d in order:
                    s, b = streams[d], ps[d]
                    used = outputs(tile_of(d, n))
                    N = 2 * P if used else P
                    if t == 1:
                        if n == 0:
                            pe.wait_ge(state_zero, 2)
                        pe.wait_ge(ready[d], 2 * n + 2)
                    if n or t > 1:
                        pe.wait_ge(s.ve, n * STEPS + t - 1)
                        pe.wait_ge(s.ac, n * STEPS + t - 1)
                    hp = lambda h: slice(64 * (h // 2), 64 * (h // 2) + 64)
                    if t == 1:
                        for p in range(2):
                            pe.transpose(b[:, 0, p * P:(p + 1) * P], s.AR[:, p, 0, :], g.ident[:])
                            pe.transpose(b[:, 0, (2 + p) * P:(3 + p) * P], s.bh[:, p, :], g.ident[:])
                            pe.transpose(b[:, 1, p * P:(p + 1) * P], s.kh[:, p, :], g.ident[:])
                            pe.transpose(b[:, 1, (2 + p) * P:(3 + p) * P], s.v[:, p, :], g.ident[:])
                        for h in range(H4):
                            mm = pe.matmul(b[:, 2 + h // 2, (h % 2) * 256:(h % 2) * 256 + N], s.bt[hp(h), h % 2, :], flat(s.AR[hp(h), h % 2, :, :])[:, 0:N], start=True, stop=True)
                    elif t == 2:
                        for h in range(H4):
                            pe.matmul(b[:, h // 2, (h % 2) * 256:(h % 2) * 256 + N], s.kt[hp(h), h % 2, :], flat(s.AR[hp(h), h % 2, :, :])[:, 0:N], start=True, stop=True)
                        for h in range(H4):
                            mm = pe.matmul(b[:, 2 + h // 2, (h % 2) * P:(h % 2 + 1) * P], s.AR[hp(h), h % 2, 0, :], s.bt[hp(h), h % 2, :], start=True, stop=True)
                    elif t in (3, 4, 5, 6, 8, 9, 10, 11, 12):
                        todo = {3: ((0, s.AT, s.A), (1, s.A, s.AT)),
                                4: ((0, s.A2T, s.A2), (1, s.A2, s.A2T), (3, s.A2, s.XT)),
                                5: ((0, s.A4T, s.A4), (3, s.A4, s.XT)),
                                6: ((3, s.A8, s.XT),),
                                8: ((0, s.A32T, s.X),),
                                9: ((3, s.Q, s.XT),),
                                10: ((0, s.XT, s.rhs),),
                                11: ((0, s.A64T, s.Z),),
                                12: ((0, s.XT, s.Q),)}[t]
                        for q, lhsT, rhs in todo:
                            for h in range(H4):
                                mm = pe.matmul(b[:, q, h * P:(h + 1) * P], lhsT[:, h, :], rhs[:, h, :], start=True, stop=True)
                        if t == 3:
                            for h in range(H4):
                                mm = pe.matmul(b[:, 2, h * 64:(h + 1) * 64], s.MakT[:, h, :], s.rows2[:, 2 + h % 2, hp(h)], start=True, stop=True)
                    elif t == 7:
                        for h in range(H4):
                            mm = pe.transpose(b[:, 0, h * P:(h + 1) * P], s.XT[:, h, :], g.ident[:])
                    elif t in (13, 14):
                        G, E = s.GE[:, 0:2, :], s.GE[:, 2:4, :]
                        bh, kh, v = s.rows1[:, 2:4, :], s.rows2[:, 0:2, :], s.rows2[:, 2:4, :]
                        if t == 13:
                            for c in range(2):
                                r = slice(64 * c, 64 * c + 64)
                                for p in range(2):
                                    o, o2 = slice(p * P, (p + 1) * P), slice((2 + p) * P, (3 + p) * P)
                                    pe.matmul(b[:, 2 + c, o], G[r, p, :], bh[r, p, :], start=True, stop=True)
                                    pe.matmul(b[:, 2 + c, o2], bh[r, p, :], E[r, p, :], start=True, stop=False)
                                    mm = pe.matmul(b[:, 2 + c, o2], kh[r, p, :], v[r, p, :], start=False, stop=True)
                        elif used:
                            for h in range(H4):
                                p, c = h % 2, slice((h % 2) * P, (h % 2 + 1) * P)
                                pe.matmul(b[hp(h), 0, c], G[:, p, hp(h)], s.MrbT[:, h, :], start=True, stop=True)
                                pe.matmul(b[hp(h), 1, c], E[:, p, hp(h)], s.MrbT[:, h, :], start=True, stop=False)
                                mm = pe.matmul(b[hp(h), 1, c], v[:, p, hp(h)], s.MrkT[:, h, :], start=False, stop=True)
                        else:
                            pe.sem_inc(s.pe, 1)
                            continue
                    else:
                        c = (t - 15) if d == 0 else (16 - t)
                        for p in range(2):
                            if used:
                                pe.matmul(b[:, 0, p * 64:(p + 1) * 64], s.S[:, p, :], s.QT[:, p, 64 * c:64 * c + 64], start=True, stop=True)
                            mm = pe.matmul(b[:, 1, p * P:(p + 1) * P], s.Phi[:, 2 * c + p, :], s.S[:, p, :], start=True, stop=True)
                    mm.then_inc(s.pe, 1)

            @block.scalar
            def _(ac):
                for n, t, d in order:
                    s, b = streams[d], ps[d]
                    ac.wait_ge(s.pe, n * STEPS + t)
                    copies = {1: ((flat(s.rows1[:]), b[:, 0, :]), (flat(s.rows2[:]), b[:, 1, :])),
                              3: ((flat(s.A2[:]), b[:, 0, :]), (flat(s.A2T[:]), b[:, 1, :])),
                              4: ((flat(s.A4[:]), b[:, 0, :]), (flat(s.A4T[:]), b[:, 1, :])),
                              5: ((flat(s.A8[:]), b[:, 0, :]),),
                              7: ((flat(s.X[:]), b[:, 0, :]),),
                              8: ((flat(s.Q[:]), b[:, 0, :]),),
                              10: ((flat(s.Z[:]), b[:, 0, :]),),
                              11: ((flat(s.Q[:]), b[:, 0, :]),)}.get(t, ())
                    if t == 14 and outputs(tile_of(d, n)):
                        tok = slice(tile_of(d, n) * P, tile_of(d, n) * P + P)
                        copies = ((g.S[:, Y_AT[d]:Y_AT[d] + 2, tok], b[:, 1, 0:2 * P].rearrange("p (a c) -> p a c", a=2)),)
                    for dst, src in copies:
                        a = ac.activation(dst, src, ACT.Copy)
                    if copies:
                        a.then_inc(s.ac, 1)
                    else:
                        ac.sem_inc(s.ac, 1)

            @block.vector
            def _(ve):
                step = chained(ve, v_done)

                def operands(n, d):
                    s, i = streams[d], tile_of(d, n)
                    tok = slice(i * P, i * P + P)
                    if n:
                        ve.wait_ge(s.pe, (n - 1) * STEPS + 2)
                    eN, eP = (x[:, d, :, tok] for x in (g.eN, g.eP))
                    b, k = g.S[:, B_AT[d]:B_AT[d] + 2, tok], g.S[:, KD_AT[d]:KD_AT[d] + 2, tok]
                    ve.scalar_tensor_tensor(out=s.AR[:, :, 0, :], in0=g.S[:, KK:KK + 2, tok], scalar=-1.0, in1=eP, op0=ALU.mult, op1=ALU.mult)
                    ve.tensor_copy(s.v[:], g.S[:, VC:VC + 2, tok])
                    step(ve.tensor_tensor(s.bt[:], b, eN, ALU.mult))
                    step(ve.tensor_tensor(s.kt[:], k, eN, ALU.mult))
                    end = CHUNK - 1 if d == 0 else 0
                    for p in range(2):
                        pe_ = g.eL[:, d, p, i * P + end:i * P + end + CHUNK + 1:CHUNK].unsqueeze(2).to_broadcast([P, 2, CHUNK])
                        split = lambda x: x.rearrange("p (c t) -> p c t", c=2)
                        ve.tensor_tensor(split(s.bh[:, p, :]), split(s.bt[:, p, :]), pe_, ALU.mult)
                        o = ve.tensor_tensor(split(s.kh[:, p, :]), split(s.kt[:, p, :]), pe_, ALU.mult)
                    o.then_inc(ready[d], 1)

                def receptance(n, d):
                    s, i = streams[d], tile_of(d, n)
                    tok = slice(i * P, i * P + P)
                    if outputs(i):
                        ve.tensor_tensor(s.AR[:, :, 1, :], g.S[:, RR:RR + 2, tok], g.eL[:, d, :, tok], ALU.mult).then_inc(ready[d], 1)
                    else:
                        ve.sem_inc(ready[d], 1)

                def evacuate(n, t, d):
                    s, b = streams[d], ps[d]
                    used = outputs(tile_of(d, n))
                    ve.wait_ge(s.pe, n * STEPS + t)
                    two = lambda q, x: b[:, q:q + 2, :].rearrange("p a (h x c) -> p (a h) x c", h=2, x=2)[:, :, x, :]
                    idb = g.ident[:].unsqueeze(1).to_broadcast([P, H4, P])
                    if t == 1:
                        step(ve.tensor_tensor(s.AT[:], two(2, 0), maskT(d, M16), ALU.mult))
                        ve.tensor_tensor(s.A32T[:], two(2, 0), maskT(d, M32), ALU.mult)
                        ve.tensor_tensor(s.A64T[:], two(2, 0), maskT(d, M64), ALU.mult)
                        o = ve.tensor_tensor(s.XT[:], s.AT[:], idb, ALU.add)
                        if used:
                            o = ve.tensor_tensor(s.MrbT[:], two(2, 1), maskT(d, INCL), ALU.mult)
                    elif t == 2:
                        ve.tensor_tensor(s.A[:].rearrange("p (a h) c -> p a h c", a=2), b[:, 2:4, 0:2 * P].rearrange("p a (h c) -> p a h c", h=2),
                                         mask(d, M16).rearrange("p (a h) c -> p a h c", a=2), ALU.mult)
                        o = ve.tensor_tensor(s.MakT[:], two(0, 0), maskT(d, STRICT), ALU.mult)
                        if used:
                            o = ve.tensor_tensor(s.MrkT[:], two(0, 1), maskT(d, INCL), ALU.mult)
                    elif t == 3:
                        ve.wait_ge(s.ac, n * STEPS + 1)
                        ve.tensor_copy(s.rhs[:, :, 0:64].rearrange("p (b a) c -> p b a c", b=2), s.rows1[:, 0:2, :].rearrange("p a (b c) -> p b a c", b=2))
                        o = ve.tensor_copy(s.rhs[:, :, 64:P], b[:, 2, 0:256].rearrange("p (h c) -> p h c", h=4))
                    elif t in (4, 5, 6, 9):
                        o = ve.tensor_tensor(s.XT[:], s.XT[:], heads(b[:, 3, :]), ALU.add)
                    elif t == 12:
                        for q in range(2):
                            split = lambda x: x.rearrange("p (b a q c) -> p b a q c", b=2, a=2, q=2)[:, :, :, q, :]
                            o = ve.tensor_tensor(s.GE[:, 2 * q:2 * q + 2, :].rearrange("p a (b c) -> p b a c", b=2), split(b[:, 0, :]), split(flat(s.Z[:])), ALU.add)
                    elif t == 13:
                        i, end = tile_of(d, n), CHUNK - 1 if d == 0 else 0
                        bd = g.pair[:].unsqueeze(1).to_broadcast([P, H4, P])
                        half = lambda x: b[:, 2:4, x * 2 * P:(x + 1) * 2 * P].rearrange("p c (a k) -> p c a k", a=2)
                        cp = lambda x: x.rearrange("p (c a) k -> p c a k", c=2)
                        step(ve.tensor_tensor(cp(s.Phi[:]), half(0), cp(bd), ALU.mult))
                        for c in range(2):
                            for p in range(2):
                                x = i * P + c * CHUNK + end
                                ve.scalar_tensor_tensor(out=s.Phi[:, 2 * c + p, :], in0=g.ident[:], scalar=g.eL[:, d, p, x:x + 1], in1=s.Phi[:, 2 * c + p, :],
                                                        op0=ALU.mult, op1=ALU.add)
                        o = ve.tensor_tensor(cp(s.Psi[:]), half(1), cp(bd), ALU.mult)
                    elif t == 14 and used:
                        o = ve.tensor_tensor(s.QT[:], s.AR[:, :, 1, :], b[:, 0, 0:2 * P].rearrange("p (a c) -> p a c", a=2), ALU.add)
                    elif t >= 15:
                        c = (t - 15) if d == 0 else (16 - t)
                        x = tile_of(d, n) * P + c * CHUNK
                        y = g.S[:, Y_AT[d]:Y_AT[d] + 2, x:x + CHUNK]
                        if t == 15:
                            ve.wait_ge(s.ac, n * STEPS + 14)
                        if used:
                            ve.tensor_tensor(y, y, b[:, 0, 0:P].rearrange("p (a c) -> p a c", a=2), ALU.add)
                        o = ve.tensor_tensor(s.S[:], s.Psi[:, 2 * c:2 * c + 2, :], b[:, 1, 0:2 * P].rearrange("p (a c) -> p a c", a=2), ALU.add)
                    else:
                        ve.sem_inc(s.ve, 1)
                        return
                    o.then_inc(s.ve, 1)

                for d in range(2):
                    operands(0, d)
                    receptance(0, d)
                for n, t, d in order:
                    evacuate(n, t, d)
                    if t == 7 and n + 1 < TILES:
                        operands(n + 1, d)
                    if t == 15 and n + 1 < TILES:
                        ve.wait_ge(streams[d].ve, n * STEPS + 14)
                        receptance(n + 1, d)


def stage_rwkv_output(nc, g, l):
    part = slice(needed_streams(l)[0] * SEQ, TOK)
    with ExitStack() as st:
        sem = g.sems.begin(st)
        sb = lambda name, shape: st.enter_context(nc.sbuf_tensor(g.name(name), shape, F32))
        gup, y, sq, t = sb("g_up", [P, RW_W]), sb("y_sum", [P, 2, TOK]), sb("y_sq", [P, 2, TOK]), sb("rk", [P, 2, TOK])
        ps = st.enter_context(nc.psum_tensor(g.name("gn_ps"), [P, 8, BANK], F32))
        w_in, v_done, y_done, mu_in, t_done, bonus_in, sq_done, var_in, eps_done, root_done, gate_in = (
            sem(n) for n in ("w_in", "v_done", "y_done", "mean_in", "rk_done", "bonus_in", "sq_done", "var_in", "eps_done", "root_done", "gate_in"))
        par = lambda name, k: g.par[:, l, ROWS[name] + k:ROWS[name] + k + 1]
        Y = lambda d: g.S[:, Y_AT[d]:Y_AT[d] + 2, part]
        KDc = lambda d: g.S[:, KD_AT[d]:KD_AT[d] + 2, part]

        with nc.Block() as block:
            @block.sync
            def _(sp):
                sp.dma_start(gup[:], g.dram["rw_g_up"][l]).then_inc(w_in, 16)
                for k in range(0, KD, 2):
                    sp.dma_start(g.w_out[:, k:k + 2, :], g.dram["w_out"][l].rearrange("(k p) n -> p k n", p=P)[:, k:k + 2, :]).then_inc(g.w_out_in[k // 2], 16)

            @block.gpsimd
            def _(po):
                po.sem_clear(g.sems.other)

            @block.tensor
            def _(pe):
                def sums(first, src, done):
                    for p in range(2):
                        mm = pe.matmul(ps[:, first + p, part], g.pair[:], src[:, p, part], start=True, stop=True)
                    mm.then_inc(done, 1)
                pe.wait_ge(y_done, 1)
                sums(0, y, mu_in)
                pe.wait_ge(t_done, 1)
                sums(2, t, bonus_in)
                pe.wait_ge(w_in, 16)
                for p in range(2):
                    mm = pe.matmul(ps[:, 6 + p, part], gup[:, p * P:(p + 1) * P], g.S[:, LORA0 + 2, part], start=True, stop=True)
                mm.then_inc(gate_in, 1)
                pe.wait_ge(sq_done, 1)
                sums(4, sq, var_in)

            @block.scalar
            def _(ac):
                ac.wait_ge(eps_done, 1)
                ac.activation(sq[:, :, part], sq[:, :, part], ACT.Sqrt).then_inc(root_done, 1)

            @block.vector
            def _(ve):
                step = chained(ve, v_done)
                ve.tensor_tensor(y[:, :, part], Y(0), Y(1), ALU.add).then_inc(y_done, 1)
                step(ve.tensor_tensor(t[:, :, part], KDc(0), KDc(1), ALU.add))
                for p in range(2):
                    o = ve.scalar_tensor_tensor(out=t[:, p, part], in0=t[:, p, part], scalar=par("rw_r_k", p), in1=g.S[:, RR + p, part], op0=ALU.mult, op1=ALU.mult)
                o.then_inc(t_done, 1)
                ve.wait_ge(mu_in, 1)
                step(ve.scalar_tensor_tensor(out=y[:, :, part], in0=ps[:, 0:2, part], scalar=-1.0 / RW_HD, in1=y[:, :, part], op0=ALU.mult, op1=ALU.add))
                ve.tensor_tensor(sq[:, :, part], y[:, :, part], y[:, :, part], ALU.mult).then_inc(sq_done, 1)
                ve.wait_ge(bonus_in, 1)
                step(ve.tensor_tensor(t[:, :, part], ps[:, 2:4, part], g.S[:, VC:VC + 2, part], ALU.mult))
                ve.wait_ge(var_in, 1)
                ve.tensor_scalar(sq[:, :, part], ps[:, 4:6, part], 1.0 / RW_HD, RW_HD * 1e-5, ALU.mult, ALU.add).then_inc(eps_done, 1)
                ve.wait_ge(root_done, 1)
                step(ve.reciprocal(sq[:, :, part], sq[:, :, part]))
                step(ve.tensor_tensor(y[:, :, part], y[:, :, part], sq[:, :, part], ALU.mult))
                for p in range(2):
                    step(ve.tensor_scalar(y[:, p, part], y[:, p, part], par("rw_ln_w", p), par("rw_ln_b", p), ALU.mult, ALU.add))
                step(ve.tensor_tensor(y[:, :, part], y[:, :, part], t[:, :, part], ALU.add))
                ve.wait_ge(gate_in, 1)
                step(ve.tensor_tensor(g.mix[:, 2:4, part], y[:, :, part], ps[:, 6:8, part], ALU.mult))


def stream_of(i):
    return 0 if i >= 2 else 1


def stage_output_projection(nc, g, l, tiles):
    with ExitStack() as st:
        sem = g.sems.begin(st)
        gate = st.enter_context(nc.sbuf_tensor(g.name("gate1"), [P, 2, D], F32))
        t = st.enter_context(nc.sbuf_tensor(g.name("gated"), [P, D], F32))
        gps = st.enter_context(nc.psum_tensor(g.name("gate_ps"), [P, 2, BANK], F32))
        ps = st.enter_context(nc.psum_tensor(g.name("mixed_ps"), [P, 2, 2, BANK], F32))
        w = g.w_out
        gate_in, gate_out, mm_done, used, v_done = (sem(n) for n in ("gate_in", "gate_out", "mm_done", "used", "v_done"))

        with nc.Block() as block:
            @block.gpsimd
            def _(po):
                po.sem_clear(g.sems.other)

            @block.tensor
            def _(pe):
                for w_ in range(2):
                    if w_:
                        pe.wait_ge(gate_out, 1)
                    broadcast_row(pe, g, l, gps, 2, w_).then_inc(gate_in, 1)
                for n, i in enumerate(tiles):
                    if n >= 2:
                        pe.wait_ge(used, n - 1)
                    for k in range(KD):
                        if n == 0:
                            pe.wait_ge(g.w_out_in[k // 2], 16 * (l + 1))
                        for j in range(2):
                            mm = pe.matmul(ps[:, n % 2, j, :], g.mix[:, k, i * P:(i + 1) * P], w[:, k, j * BANK:(j + 1) * BANK], start=k == 0, stop=k == KD - 1)
                    mm.then_inc(mm_done, 1)

            @block.scalar
            def _(ac):
                for w_ in range(2):
                    ac.wait_ge(gate_in, w_ + 1)
                    ac.activation(gate[:, w_, :], gps[:].rearrange("p a b -> p (a b)"), ACT.Copy).then_inc(gate_out, 1)

            @block.vector
            def _(ve):
                step = chained(ve, v_done)
                ve.wait_ge(gate_out, 2)
                for n, i in enumerate(tiles):
                    ve.wait_ge(mm_done, n + 1)
                    o = ve.tensor_tensor(t[:], ps[:, n % 2, :, :].rearrange("p a b -> p (a b)"), gate[:, stream_of(i), :], ALU.mult)
                    o.then_inc(used, 1)
                    ve.wait_ge(used, n + 1)
                    step(ve.tensor_tensor(g.X[:, i, :], g.X[:, i, :], t[:], ALU.add))


def stage_peer(nc, g, l, tiles, H, HT):
    HH = 2 * HEADS
    N = len(tiles)
    CW, WB, T0 = 2, 4, tiles[0] * P
    with ExitStack() as st:
        sem = g.sems.begin(st)
        sb = lambda name, shape, dt=F32: st.enter_context(nc.sbuf_tensor(g.name(name), shape, dt))
        QT, KT = sb("QT", [P, HH, TOK]), sb("KT", [P, HH, P])
        sc = sb("scores", [P, HH, P])
        val, idx_u, idx = sb("half_vals", [P, HH, 16]), sb("half_idx_u", [P, HH, 16], U32), sb("half_idx", [P, HH, 16])
        cand = sb("cand", [P, HEADS, 256])
        top, pos, part_u, part = sb("top_vals", [P, HEADS, 16]), sb("top_pos", [P, SLOTS], U32), sb("pos_part_u", [P, 2, SLOTS], U32), sb("pos_part", [P, 2, SLOTS])
        found, total = sb("found", [P, 2, SLOTS]), sb("gate_sum", [P, HEADS])
        gates, experts = sb("gates", [P, 2, SLOTS]), sb("experts", [P, 2, SLOTS], U32)
        ring, rows = sb("expert_rows", [P, RING, D]), sb("row_numbers", [P, 2, RING], U32)
        dots8, dots, weight, diag = sb("dots8", [P, RING]), sb("dots", [P, SLOTS]), sb("weight", [P, SLOTS]), sb("diag", [P, BY_PE, P])
        gate, side_sum = sb("gate2", [P, 2, D]), sb("side_sum", [P, D])
        hot = cand[:].rearrange("p h (k j) -> p (h k) j", j=16)
        gated = cand[:, 0:4, :].rearrange("p a b -> p (a b)")
        sps = st.enter_context(nc.psum_tensor(g.name("score_ps"), [P, 4, BANK], F32))
        acc = st.enter_context(nc.psum_tensor(g.name("expert_sum"), [P, 2, BANK], F32))
        gps = st.enter_context(nc.psum_tensor(g.name("gate2_ps"), [P, 2, BANK], F32))
        wq = ring[:].rearrange("p (b a) (k c) -> p b (a k) c", b=WB, k=KD // 2)
        key_rows = cand[:].rearrange("p (s h) (x d) -> p s (h x) d", s=2, d=P)
        q_bank = lambda j: (acc, gps)[j // 2 % 2][:, j % 2, :]
        wq_landed = [sem(f"wq_landed{b}") for b in range(WB)]
        keys_in, key_tp, key_out, q_done, q_out = (sem(n) for n in ("keys_in", "keys_transposed", "keys_out", "queries_done", "queries_out"))
        ahead = Modulation(nc, g, st, sem, l + 1, 0, gps[0:2, 0, :], HT[:].unsqueeze(1)) if l + 1 < DEPTH else None
        landed, before = g.rows_landed, g.rows_used
        g.rows_used += 2 * N * GROUPS
        free = [sem(f"free{b}") for b in range(RING)]
        s_in, s_out, shifted, exped, selected = (sem(n) for n in ("scores_in", "scores_out", "shifted", "exped", "selected"))
        rows_copied, issued, v_go = sem("rows_copied"), sem("issued"), sem("v_go")
        dots_kept, gelu_done, weight_done, diag_done, acc_read = (sem(n) for n in ("dots_kept", "gelu_done", "weight_done", "diag_done", "acc_read"))
        gate_in, gate_out, v_done = sem("gate_in"), sem("gate_out"), sem("v_done")
        table = {0: g.dram["peer_u"].rearrange("l n d -> (l n) d"), 1: g.dram["peer_v"].rearrange("l n d -> (l n) d")}
        flat = lambda t: t.rearrange("p a b -> p (a b)")

        with nc.Block() as block:
            @block.sync
            def _(sp):
                for s, name in enumerate(("peer_k1", "peer_k2")):
                    sp.dma_start(key_rows[:, s, :, :], g.dram[name][l].rearrange("h n d -> n h d")).then_inc(keys_in, 16)
                wv = g.dram["peer_wq"][l].rearrange("(k p) n -> p k n", p=P)
                for n in range(HH // CW):
                    if n >= WB:
                        sp.wait_ge(q_done, (n - WB + 1) * CW)
                    sp.dma_start(wq[:, n % WB, :, :], wv[:, :, n * CW * P:(n + 1) * CW * P]).then_inc(wq_landed[n % WB], 16)
                if ahead:
                    sp.wait_ge(q_done, HH)
                    ahead.traffic(sp)

            @block.gpsimd
            def _(po):
                po.sem_clear(g.sems.other)
                if ahead:
                    ahead.gain_ones(po)
                for b in range(RING):
                    po.sem_inc(free[b], 2)
                for n in range(N):
                    po.wait_ge(selected, n + 1)
                    for half in range(2):
                        with po.Fori(0, GROUPS // 2) as pair:
                            for side in range(2):
                                k = pair * 2 + side
                                use = k + (n * 2 + half) * GROUPS
                                for b in range(RING):
                                    po.wait_ge(free[b], use + 1)
                                    po.sem_inc(issued, 1)
                                po.tensor_copy(rows[:, side, :], experts[:, n % 2, bass.ds(k * RING, RING)]).then_inc(rows_copied, 1)
                                po.wait_ge(rows_copied, use + 1)
                                po.sem_inc(issued, 1)
                                for b in range(RING):
                                    po.wait_ge(free[b], use + 2)
                                    po.sem_inc(issued, 1)
                                    po.indirect_dma_start(out=ring[:, b, :], out_offset=None, in_=table[half],
                                                          in_offset=bass.IndirectOffsetOnAxis(ap=rows[:, side, b:b + 1], axis=0)).then_inc(landed[b], 16)

            @block.vector
            def _(ve):
                step = chained(ve, v_done)

                def top16(pair):
                    for first in (True, False):
                        k = slice(0, 8) if first else slice(8, 16)
                        for src, vals, where in pair:
                            step(ve.max(vals[:, k], src), lag=1)
                        for src, vals, where in pair:
                            step(ve.max_index(where[:, k], vals[:, k], src), lag=1)
                        for src, vals, where in pair if first else ():
                            step(ve.match_replace(src, vals[:, k], src, -3.0e38), lag=1)
                    step.settle()

                def select_halves(c):
                    top16([(sc[:, x, :], val[:, x, :], idx_u[:, x, :]) for x in (c, c + 1)])

                def select_heads(h):
                    c = slice(2 * h, 2 * h + 4)
                    step(ve.tensor_copy(idx[:, c, :], idx_u[:, c, :]), lag=1)
                    halves = val[:, c, :].rearrange("p (h s) k -> p h s k", s=2)
                    step(ve.tensor_tensor(cand[:, h:h + 2, :].rearrange("p h (a b) -> p h a b", a=16), halves[:, :, 0, :].unsqueeze(3).to_broadcast([P, 2, 16, 16]),
                                          halves[:, :, 1, :].unsqueeze(2).to_broadcast([P, 2, 16, 16]), ALU.add))
                    top16([(cand[:, x, :], top[:, x, :], pos[:, x * 16:x * 16 + 16]) for x in (h, h + 1)])

                pieces = [piece for q in range(4) for piece in ((select_halves, 4 * q), (select_halves, 4 * q + 2), (select_heads, 2 * q))]

                def select_rows(n):
                    gt = gates[:, n % 2, :].rearrange("p (h k) -> p h k", h=HEADS)
                    ve.tensor_tensor(gt, top[:], top[:, :, 0:1].to_broadcast([P, HEADS, 16]), ALU.subtract).then_inc(shifted, 1)
                    step(ve.tensor_scalar(part_u[:, 0, :], pos[:], 4, None, ALU.logical_shift_right))
                    step(ve.tensor_scalar(part_u[:, 1, :], pos[:], 15, None, ALU.bitwise_and))
                    step(ve.tensor_copy(part[:], part_u[:]))
                    lists = idx[:].rearrange("p (h s) k -> p h s k", s=2)
                    for s in range(2):
                        step(ve.tensor_tensor(hot, g.iota[:].unsqueeze(1).to_broadcast([P, SLOTS, 16]), part[:, s, :].unsqueeze(2).to_broadcast([P, SLOTS, 16]), ALU.is_equal))
                        h4 = hot.rearrange("p (h k) j -> p h k j", h=HEADS)
                        step(ve.tensor_tensor(h4, h4, lists[:, :, s, :].unsqueeze(2).to_broadcast([P, HEADS, 16, 16]), ALU.mult))
                        step(ve.tensor_reduce(found[:, s, :], hot, AX.X, ALU.add))
                    step(ve.tensor_scalar(found[:, 0, :], found[:, 0, :], float(NKEYS), float(l * NEXP), ALU.mult, ALU.add))
                    if n >= 2:
                        ve.wait_ge(rows_copied, (n - 1) * 2 * GROUPS)
                    ve.tensor_tensor(experts[:, n % 2, :], found[:, 0, :], found[:, 1, :], ALU.add).then_inc(selected, 1)

                def select_pieces(n, first, last):
                    for m in range(first, min(last, len(pieces))):
                        if m % 3 == 0:
                            ve.wait_ge(s_out, 4 * n + m // 3 + 1)
                        pieces[m][0](pieces[m][1])
                    if first < len(pieces) <= last:
                        select_rows(n)

                def softmax(n):
                    gt = gates[:, n % 2, :].rearrange("p (h k) -> p h k", h=HEADS)
                    ve.wait_ge(exped, n + 1)
                    step(ve.tensor_reduce(total[:], gt, AX.X, ALU.add))
                    step(ve.reciprocal(total[:], total[:]))
                    step(ve.tensor_tensor(gt, gt, total[:].unsqueeze(2).to_broadcast([P, HEADS, 16]), ALU.mult))

                for c in range(4):
                    ve.wait_ge(key_tp, c + 1)
                    ve.tensor_copy(KT[:, 4 * c:4 * c + 4, :], sps[:, c, :].rearrange("p (a b) -> p a b", a=4)).then_inc(key_out, 1)
                select_pieces(0, 0, len(pieces))
                softmax(0)
                ve.wait_ge(gate_out, 2)
                for n, i in enumerate(tiles):
                    with ve.Fori(0, GROUPS) as k:
                        use = k + n * 2 * GROUPS
                        for b in range(RING):
                            ve.wait_ge(landed[b], 16 * (use + before + 1))
                            ve.tensor_tensor_reduce(ring[:, b, :], ring[:, b, :], H[:, i, :], 1.0, 0.0, ALU.mult, ALU.add, dots8[:, b:b + 1]).then_inc(free[b], 1)
                        ve.wait_ge(free[RING - 1], use + 3)
                        ve.sem_inc(v_go, 1)
                        ve.tensor_copy(dots[:, bass.ds(k * RING, RING)], dots8[:]).then_inc(dots_kept, 1)
                        ve.wait_ge(dots_kept, k + n * GROUPS + 1)
                        ve.sem_inc(v_go, 1)
                    ve.wait_ge(gelu_done, n + 1)
                    ve.tensor_tensor(weight[:], dots[:], gates[:, n % 2, :], ALU.mult).then_inc(weight_done, 1)
                    ve.wait_ge(weight_done, n + 1)
                    for k in range(GROUPS):
                        if n + 1 < N:
                            select_pieces(n + 1, k, k + 1)
                        use = k + (2 * n + 1) * GROUPS
                        for b in range(BY_PE, RING):
                            ve.wait_ge(landed[b], 16 * (use + before + 1))
                            w = weight[:, k * RING + b:k * RING + b + 1]
                            if k == 0 and b == BY_PE:
                                o = ve.tensor_scalar(side_sum[:], ring[:, b, :], w, None, ALU.mult)
                            else:
                                o = ve.scalar_tensor_tensor(out=side_sum[:], in0=ring[:, b, :], scalar=w, in1=side_sum[:], op0=ALU.mult, op1=ALU.add)
                            o.then_inc(free[b], 1)
                            ve.wait_ge(free[b], use + 3)
                    if ahead and n == 0:
                        ahead.finish(ve)
                    ve.wait_ge(free[BY_PE - 1], (2 * n + 2) * GROUPS + 2)
                    ve.tensor_tensor(gated, flat(acc[:]), side_sum[:], ALU.add).then_inc(acc_read, 1)
                    ve.wait_ge(acc_read, n + 1)
                    step(ve.tensor_tensor(gated, gated, gate[:, stream_of(i), :], ALU.mult))
                    step(ve.tensor_tensor(g.X[:, i, :], g.X[:, i, :], gated, ALU.add))
                    if n + 1 < N:
                        softmax(n + 1)

            @block.scalar
            def _(ac):
                def scores_out(n, q):
                    ac.wait_ge(s_in, 4 * n + q + 1)
                    if n and q == 0:
                        ac.wait_ge(selected, n)
                    ac.activation(sc[:, 4 * q:4 * q + 4, :], sps[:, q, :].rearrange("p (a b) -> p a b", a=4), ACT.Copy).then_inc(s_out, 1)

                def exps(n):
                    ac.wait_ge(shifted, n + 1)
                    ac.activation(gates[:, n % 2, :], gates[:, n % 2, :], ACT.Exp).then_inc(exped, 1)

                for j in range(HH):
                    ac.wait_ge(q_done, j + 1)
                    ac.activation(QT[:, j, T0:TOK], q_bank(j)[:, 0:TOK - T0], ACT.Copy).then_inc(q_out, 1)
                    if j and j % 4 == 0:
                        scores_out(0, j // 4 - 1)
                scores_out(0, 3)
                exps(0)
                for w in range(2):
                    ac.wait_ge(gate_in, w + 1)
                    ac.activation(gate[:, w, :], flat(gps[:]), ACT.Copy).then_inc(gate_out, 1)
                for n in range(N):
                    for q in range(4) if n + 1 < N else ():
                        scores_out(n + 1, q)
                    if ahead and n == 0:
                        for m in range(ahead.count):
                            ahead.take(ac, m)
                    ac.wait_ge(dots_kept, (n + 1) * GROUPS)
                    ac.activation(dots[:], dots[:], ACT.Gelu).then_inc(gelu_done, 1)
                    ac.wait_ge(weight_done, n + 1)
                    with ac.Fori(0, GROUPS) as k:
                        for b in range(BY_PE):
                            ac.wait_ge(free[b], k + (2 * n + 1) * GROUPS + 2)
                            ac.activation(diag[:, b, :], g.ident[:], ACT.Copy, scale=weight[:, bass.ds(k * RING + b, 1)]).then_inc(diag_done, 1)
                    if n + 1 < N:
                        exps(n + 1)

            @block.tensor
            def _(pe):
                def scores(n, q):
                    if n:
                        pe.wait_ge(s_out, 4 * (n - 1) + q + 1)
                    for c in range(4 * q, 4 * q + 4):
                        mm = pe.matmul(sps[:, q, (c % 4) * P:(c % 4 + 1) * P], QT[:, c, tiles[n] * P:(tiles[n] + 1) * P], KT[:, c, :], start=True, stop=True)
                    mm.then_inc(s_in, 1)

                def group(n, k, first, last):
                    use = k + (n * 2 + 1) * GROUPS
                    for b in range(BY_PE):
                        pe.wait_ge(landed[b], 16 * (use + before + 1))
                        pe.wait_ge(diag_done, (k + n * GROUPS) * BY_PE + b + 1)
                        for j in range(2):
                            mm = pe.matmul(acc[:, j, :], diag[:, b, :], ring[:, b, j * BANK:(j + 1) * BANK], start=first and b == 0, stop=last and b == BY_PE - 1)
                        mm.then_inc(free[b], 1)

                pe.wait_ge(keys_in, 32)
                for c in range(HH):
                    mm = pe.transpose(sps[:, c // 4, (c % 4) * P:(c % 4 + 1) * P], key_rows[:, c % 2, c // 2, :], g.ident[:])
                    if c % 4 == 3:
                        mm.then_inc(key_tp, 1)
                for j in range(HH):
                    pe.wait_ge(wq_landed[j // CW % WB], 16 * (j // CW // WB + 1))
                    if j >= 4:
                        pe.wait_ge(q_out, j - 3)
                    for k in range(KD):
                        mm = pe.matmul(q_bank(j)[:, 0:TOK - T0], wq[:, j // CW % WB, k, (j % CW) * P:(j % CW + 1) * P], HT[:, k, T0:TOK], start=k == 0, stop=k == KD - 1)
                    mm.then_inc(q_done, 1)
                    if j and j % 4 == 0:
                        if j == 4:
                            pe.wait_ge(key_out, 4)
                        pe.wait_ge(q_out, j)
                        scores(0, j // 4 - 1)
                pe.wait_ge(q_out, HH)
                scores(0, 3)
                for w in range(2):
                    if w:
                        pe.wait_ge(gate_out, 1)
                    broadcast_row(pe, g, l, gps, 5, w).then_inc(gate_in, 1)
                for n in range(N):
                    for q in range(4) if n + 1 < N else ():
                        scores(n + 1, q)
                    if ahead and n == 0:
                        pe.wait_ge(gate_out, 2)
                        for m in range(ahead.count):
                            ahead.product(pe, m)
                    if n:
                        pe.wait_ge(acc_read, n)
                    group(n, 0, True, False)
                    with pe.Fori(1, GROUPS - 1) as k:
                        group(n, k, False, False)
                    group(n, GROUPS - 1, False, True)


def stage_final_norm(nc, g, out):
    with ExitStack() as st:
        sem = g.sems.begin(st)
        sb = lambda name, shape: st.enter_context(nc.sbuf_tensor(g.name(name), shape, F32))
        gain, sq, ms, y = sb("final_gain", [P, D]), sb("squares", [P, 2, D]), sb("mean_square", [P, 2]), sb("y", [P, 2, D])
        gain_in, ms_done, eps_done, root_done, v_done, y_done = (sem(n) for n in ("gain_in", "ms_done", "eps_done", "root_done", "v_done", "y_done"))
        rows = out[0].rearrange("(i p) d -> i p d", p=P)

        with nc.Block() as block:
            @block.sync
            def _(sp):
                sp.dma_start(gain[:], g.dram["final_g"].rearrange("(a n) -> a n", a=1).to_broadcast([P, D])).then_inc(gain_in, 16)
                for i in range(2):
                    sp.wait_ge(y_done, i + 1)
                    sp.dma_start(rows[i], y[:, i, :]).then_inc(g.stored, 16)
                sp.wait_ge(g.stored, 32)

            @block.scalar
            def _(ac):
                for i in range(2):
                    ac.activation(sq[:, i, :], g.X[:, 2 + i, :], ACT.Square, scale=float(D) ** -0.5, accum_out=ms[:, i:i + 1]).then_inc(ms_done, 1)
                ac.wait_ge(eps_done, 1)
                ac.activation(ms[:], ms[:], ACT.Sqrt).then_inc(root_done, 1)

            @block.vector
            def _(ve):
                step = chained(ve, v_done)
                ve.wait_ge(ms_done, 2)
                ve.tensor_scalar(ms[:], ms[:], 1e-6, None, ALU.add).then_inc(eps_done, 1)
                ve.wait_ge(root_done, 1)
                step(ve.reciprocal(ms[:], ms[:]))
                ve.wait_ge(gain_in, 16)
                for i in range(2):
                    ve.scalar_tensor_tensor(out=y[:, i, :], in0=g.X[:, 2 + i, :], scalar=ms[:, i:i + 1], in1=gain[:], op0=ALU.mult, op1=ALU.mult).then_inc(y_done, 1)


def program(nc, dram, out):
    with ExitStack() as st:
        g = Shared()
        g.rows_landed, g.rows_used = [st.enter_context(nc.semaphore(f"expert_rows_landed{b}")) for b in range(RING)], 0
        g.w_out_in = [st.enter_context(nc.semaphore(f"w_out_landed{k}")) for k in range(KD // 2)]
        g.dram, g.stored, g.sems = dram, st.enter_context(nc.semaphore("output_stored")), Semaphores(nc)
        sb = lambda name, shape, dt=F32: st.enter_context(nc.sbuf_tensor(g.name(name), shape, dt))
        g.X = sb("X", [P, TILES, D])
        g.mod = [[sb("mod_a", [4, D]), sb("mod_b", [8, D])] for _ in range(DEPTH)]
        g.one = sb("one", [8, 2])
        g.par = sb("par", [P, DEPTH, P])
        g.omka = sb("one_minus_k_a", [P, DEPTH, 2])
        g.cond = sb("cond", [P, KD, 2])
        g.ident, g.pair, g.rot, g.swap = (sb(n, [P, P]) for n in ("ident", "pair", "rot", "swap"))
        g.rope = sb("rope", [P, 2, SEQ])
        g.band = sb("band", [P, 2, 2 * SEQ])
        g.ones = sb("ones", [P, P])
        g.masks = sb("masks", [P, 10, P])
        g.iota = sb("iota", [P, 16])
        g.sink = sb("sink", [P, DEPTH, AT_HQ])
        g.sink8 = sb("sink8", [P, DEPTH, AT_HQ])
        stage_constants(nc, g)
        for l in range(DEPTH):
            done = [2, 3] if l == DEPTH - 1 else [0, 1, 2, 3]
            with ExitStack() as mixer:
                keep = lambda name, shape, dt=F32: mixer.enter_context(nc.sbuf_tensor(g.name(name), shape, dt))
                g.S = keep("S", [P, IN_TILES, TOK])
                with ExitStack() as front:
                    HT = front.enter_context(nc.sbuf_tensor(g.name("HT"), [P, KD, TOK], F32))
                    stage_norm(nc, g, l, [0, 1, 2, 3], 0, None, HT)
                    stage_input_projection(nc, g, l, HT)
                g.mix = keep("mix", [P, KD, TOK])
                stage_hyena(nc, g, l)
                stage_attention(nc, g, l, done)
                with ExitStack() as rwkv:
                    g.eL, g.eN, g.eP = (rwkv.enter_context(nc.sbuf_tensor(g.name(n), [P, 2, 2, TOK], F32)) for n in ("decay_in", "decay_out", "decay_before"))
                    stage_rwkv_operands(nc, g, l)
                    stage_rwkv_chunks(nc, g, l)
                g.w_out = keep("w_out", [P, KD, D])
                stage_rwkv_output(nc, g, l)
                stage_output_projection(nc, g, l, done)
            with ExitStack() as peer:
                keep = lambda name, shape: peer.enter_context(nc.sbuf_tensor(g.name(name), shape, F32))
                H, HT = keep("H", [P, TILES, D]), keep("HT2", [P, KD, TOK])
                stage_norm(nc, g, l, done, 3, H, HT)
                stage_peer(nc, g, l, done, H, HT)
        stage_final_norm(nc, g, out)


_INS = ['x', 'c', 'ctx', 'c_ctx', 'mod_w', 'mod_b', 'norm1_g', 'norm2_g', 'w_in', 'conv_w', 'conv_b', 'hy_w1', 'hy_b1',
        'hy_w2', 'hy_b2', 'hy_w3', 'hy_b3', 'hy_freq', 'hy_bias', 'rw_w0', 'rw_w_up', 'rw_a0', 'rw_a_up', 'rw_g_up',
        'rw_k_k', 'rw_k_a', 'rw_r_k', 'rw_ln_w', 'rw_ln_b', 'attn_sink', 'hy_out_g', 'at_out_g', 'w_out', 'peer_wq',
        'peer_k1', 'peer_k2', 'peer_u', 'peer_v', 'final_g']
_OUT = (1, SEQ, D)


def kernel(**inputs):
    import numpy as _np
    import concourse.bacc as _bacc
    from concourse import mybir as _mybir
    from concourse.bass_utils import run_bass_kernel_spmd as _run

    nc = _bacc.Bacc("TRN2", target_bir_lowering=False, num_devices=1)
    arrays, dram = {}, {}
    for name in _INS:
        arrays[f"in_{name}"] = _np.ascontiguousarray(inputs[name])
    for name, a in host_constants().items():
        arrays[f"in_{name}"] = a
    for name, a in arrays.items():
        dram[name[3:]] = nc.dram_tensor(name, a.shape, _mybir.dt.from_np(a.dtype), kind="ExternalInput").ap()
    out = nc.dram_tensor("out_0", _OUT, _mybir.dt.float32, kind="ExternalOutput").ap()
    program(nc, dram, out)
    r = _run(nc, [arrays], core_ids=[0])
    return r.results[0]["out_0"]
```
